# Optimizing a Trainium2 kernel written in Bass

```python
import math
import jax, jax.numpy as jnp
from jax import lax
import numpy as np

D_MODEL = 1024
BATCH = 1
SEQ = 1024
DEPTH = 1

CHUNK = 64
ATTN_HEAD_DIM = 64
ATTN_HEADS = (D_MODEL // 2) // ATTN_HEAD_DIM
ATTN_WIDTH = ATTN_HEADS * ATTN_HEAD_DIM
LEFT_CHUNKS = 8
BAND_CHUNKS = LEFT_CHUNKS + 1
REL_CLIP = 128
DN_HEAD_DIM = 128
DN_HEADS = (D_MODEL - ATTN_WIDTH) // DN_HEAD_DIM
DN_WIDTH = DN_HEADS * DN_HEAD_DIM
CONV_K = 4
FFN_HIDDEN = -(-8 * D_MODEL // (3 * 256)) * 256
IN_COLS = 3 * ATTN_WIDTH + 4 * DN_WIDTH + 2 * DN_HEADS
EPS = 1e-6

kernel_name = 'hymba_chunked_attn_gated_deltanet_block'

def rms_norm(x, g):
    xf = x.astype(jnp.float32)
    y = xf * lax.rsqrt(jnp.mean(xf * xf, axis=-1, keepdims=True) + EPS)
    return (y * g.astype(jnp.float32)).astype(x.dtype)

def l2norm(t):
    return t * lax.rsqrt(jnp.sum(t * t, axis=-1, keepdims=True) + EPS)

def chunked_band_attention(q, k, v, q_g, k_g, rel_bias):
    B, T, H, Dh = q.shape
    nc = T // CHUNK
    f32 = jnp.float32
    q = rms_norm(q, q_g).astype(f32)
    k = rms_norm(k, k_g).astype(f32)
    v = v.astype(f32)
    qc = q.reshape(B, nc, CHUNK, H, Dh)

    def band(t):
        tc = t.reshape(B, nc, CHUNK, H, Dh)
        tp = jnp.pad(tc, ((0, 0), (LEFT_CHUNKS, 0), (0, 0), (0, 0), (0, 0)))
        return jnp.concatenate([tp[:, i:i + nc] for i in range(BAND_CHUNKS)], axis=2)

    kb, vb = band(k), band(v)
    scores = jnp.einsum('bcqhd,bckhd->bchqk', qc, kb) * (Dh ** -0.5)
    q_off = jnp.arange(CHUNK)
    k_off = jnp.arange(BAND_CHUNKS * CHUNK) - LEFT_CHUNKS * CHUNK
    rel = q_off[:, None] - k_off[None, :]
    idx = jnp.clip(rel, -REL_CLIP, REL_CLIP) + REL_CLIP
    bias = jnp.transpose(rel_bias.astype(f32)[idx], (2, 0, 1))
    key_chunk = jnp.arange(nc)[:, None] - LEFT_CHUNKS + jnp.arange(BAND_CHUNKS)[None, :]
    valid = jnp.repeat(key_chunk >= 0, CHUNK, axis=1)
    scores = jnp.where(valid[None, :, None, None, :], scores + bias[None, None], -1e30)
    p = jax.nn.softmax(scores, axis=-1)
    out = jnp.einsum('bchqk,bckhd->bcqhd', p, vb)
    return out.reshape(B, T, H * Dh)

def causal_depthwise_conv(x, w):
    C = x.shape[-1]
    return lax.conv_general_dilated(
        x.astype(jnp.float32), w.astype(jnp.float32)[:, None, :],
        window_strides=(1,), padding=[(CONV_K - 1, 0)],
        dimension_numbers=('NWC', 'WIO', 'NWC'), feature_group_count=C)

def gated_delta_rule(q, k, v, beta_logit, alpha_logit, a_log, dt_bias):
    B, T, H, Dk = q.shape
    Dv = v.shape[-1]
    nc = T // CHUNK
    f32 = jnp.float32
    q = l2norm(q.astype(f32)) * (Dk ** -0.5)
    k = l2norm(k.astype(f32))
    v = v.astype(f32)
    beta = jax.nn.sigmoid(beta_logit.astype(f32))
    g = -jnp.exp(a_log.astype(f32)) * jax.nn.softplus(alpha_logit.astype(f32) + dt_bias.astype(f32))

    def to_chunks(t):
        return t.reshape(B, nc, CHUNK, H, -1).transpose(0, 3, 1, 2, 4)

    qc, kc, vc = to_chunks(q), to_chunks(k), to_chunks(v)
    bc = beta.reshape(B, nc, CHUNK, H).transpose(0, 3, 1, 2)
    gc = jnp.cumsum(g.reshape(B, nc, CHUNK, H).transpose(0, 3, 1, 2), axis=-1)
    tri_incl = jnp.tril(jnp.ones((CHUNK, CHUNK), bool))
    tri_strict = jnp.tril(jnp.ones((CHUNK, CHUNK), bool), -1)
    gdiff = gc[..., :, None] - gc[..., None, :]
    decay = jnp.where(tri_incl, jnp.exp(jnp.where(tri_incl, gdiff, 0.0)), 0.0)
    kb = kc * bc[..., None]
    vb = vc * bc[..., None]
    L = jnp.where(tri_strict, jnp.einsum('bhnid,bhnjd->bhnij', kb, kc) * decay, 0.0)
    eye = jnp.eye(CHUNK, dtype=f32)
    rhs = jnp.concatenate([vb, kb * jnp.exp(gc)[..., None]], axis=-1)
    sol = lax.linalg.triangular_solve(eye + L, rhs, left_side=True, lower=True, unit_diagonal=True)
    u, w = sol[..., :Dv], sol[..., Dv:]
    intra = jnp.einsum('bhnid,bhnjd->bhnij', qc, kc) * decay
    q_dec = qc * jnp.exp(gc)[..., None]
    g_last = gc[..., -1]
    k_dec = kc * jnp.exp(g_last[..., None] - gc)[..., None]

    def step(S, inp):
        u_n, w_n, intra_n, qd_n, kd_n, gl_n = inp
        v_new = u_n - jnp.einsum('bhcd,bhde->bhce', w_n, S)
        o = jnp.einsum('bhcd,bhde->bhce', qd_n, S) + jnp.einsum('bhij,bhje->bhie', intra_n, v_new)
        S = S * jnp.exp(gl_n)[..., None, None] + jnp.einsum('bhcd,bhce->bhde', kd_n, v_new)
        return S, o

    xs = (jnp.moveaxis(u, 2, 0), jnp.moveaxis(w, 2, 0), jnp.moveaxis(intra, 2, 0),
          jnp.moveaxis(q_dec, 2, 0), jnp.moveaxis(k_dec, 2, 0), jnp.moveaxis(g_last, 2, 0))
    S0 = jnp.zeros((B, H, Dk, Dv), f32)
    _, o = lax.scan(step, S0, xs)
    return jnp.transpose(o, (1, 0, 3, 2, 4)).reshape(B, T, H, Dv)

def setup_inputs(seed: int = 0) -> dict:
    key = jax.random.key(seed)
    ks = jax.random.split(key, 17)
    f32 = jnp.float32

    def nrm(k, shape, scale):
        return jax.random.normal(k, shape, f32) * scale

    def gain(k, n):
        return 1.0 + 0.01 * jax.random.normal(k, (DEPTH, n), f32)

    x = jax.random.normal(ks[0], (BATCH, SEQ, D_MODEL), f32)
    dt = jnp.exp(jax.random.uniform(ks[9], (DEPTH, DN_HEADS), f32, math.log(1e-3), math.log(1e-1)))
    return {
        'x': x,
        'norm_mix_g': gain(ks[1], D_MODEL),
        'w_in': nrm(ks[2], (DEPTH, D_MODEL, IN_COLS), D_MODEL ** -0.5),
        'attn_q_norm_g': gain(ks[3], ATTN_HEAD_DIM),
        'attn_k_norm_g': gain(ks[4], ATTN_HEAD_DIM),
        'rel_bias': nrm(ks[5], (DEPTH, 2 * REL_CLIP + 1, ATTN_HEADS), 0.1),
        'attn_out_norm_g': gain(ks[6], ATTN_WIDTH),
        'conv_w': nrm(ks[7], (DEPTH, CONV_K, 3 * DN_WIDTH), CONV_K ** -0.5),
        'a_log': jnp.log(jax.random.uniform(ks[8], (DEPTH, DN_HEADS), f32, 1.0, 16.0)),
        'dt_bias': dt + jnp.log(-jnp.expm1(-dt)),
        'dn_out_norm_g': gain(ks[10], DN_HEAD_DIM),
        'w_out': nrm(ks[11], (DEPTH, D_MODEL, D_MODEL), D_MODEL ** -0.5),
        'norm_ffn_g': gain(ks[12], D_MODEL),
        'w_gate': nrm(ks[13], (DEPTH, D_MODEL, FFN_HIDDEN), D_MODEL ** -0.5),
        'w_up': nrm(ks[14], (DEPTH, D_MODEL, FFN_HIDDEN), D_MODEL ** -0.5),
        'w_down': nrm(ks[15], (DEPTH, FFN_HIDDEN, D_MODEL), FFN_HIDDEN ** -0.5),
    }

def reference(x, norm_mix_g, w_in, attn_q_norm_g, attn_k_norm_g, rel_bias, attn_out_norm_g,
              conv_w, a_log, dt_bias, dn_out_norm_g, w_out, norm_ffn_g, w_gate, w_up, w_down):
    B, T, _ = x.shape
    splits = [ATTN_WIDTH, 2 * ATTN_WIDTH, 3 * ATTN_WIDTH,
              3 * ATTN_WIDTH + 3 * DN_WIDTH, 3 * ATTN_WIDTH + 4 * DN_WIDTH,
              3 * ATTN_WIDTH + 4 * DN_WIDTH + DN_HEADS]
    for l in range(DEPTH):
        h = rms_norm(x, norm_mix_g[l])
        proj = jnp.einsum('bsd,de->bse', h, w_in[l])
        a_q, a_k, a_v, d_qkv, d_z, d_beta, d_alpha = jnp.split(proj, splits, axis=-1)
        a_out = chunked_band_attention(
            a_q.reshape(B, T, ATTN_HEADS, ATTN_HEAD_DIM),
            a_k.reshape(B, T, ATTN_HEADS, ATTN_HEAD_DIM),
            a_v.reshape(B, T, ATTN_HEADS, ATTN_HEAD_DIM),
            attn_q_norm_g[l], attn_k_norm_g[l], rel_bias[l])
        a_out = rms_norm(a_out, attn_out_norm_g[l]).astype(x.dtype)
        d_qkv = jax.nn.silu(causal_depthwise_conv(d_qkv, conv_w[l]))
        d_q, d_k, d_v = jnp.split(d_qkv, 3, axis=-1)
        o = gated_delta_rule(
            d_q.reshape(B, T, DN_HEADS, DN_HEAD_DIM),
            d_k.reshape(B, T, DN_HEADS, DN_HEAD_DIM),
            d_v.reshape(B, T, DN_HEADS, DN_HEAD_DIM),
            d_beta, d_alpha, a_log[l], dt_bias[l])
        z = d_z.reshape(B, T, DN_HEADS, DN_HEAD_DIM).astype(jnp.float32)
        o = rms_norm(o, dn_out_norm_g[l]) * jax.nn.silu(z)
        d_out = o.reshape(B, T, DN_WIDTH).astype(x.dtype)
        mix = jnp.concatenate([a_out, d_out], axis=-1)
        x = x + jnp.einsum('bse,ed->bsd', mix, w_out[l])
        h = rms_norm(x, norm_ffn_g[l])
        gate = jnp.einsum('bsd,df->bsf', h, w_gate[l])
        up = jnp.einsum('bsd,df->bsf', h, w_up[l])
        x = x + jnp.einsum('bsf,fd->bsd', jax.nn.silu(gate) * up, w_down[l])
    return x


_drawn_inputs = setup_inputs


def setup_inputs(seed=0):
    import zlib

    import numpy as np

    out = dict(_drawn_inputs(seed))
    spreads = {}
    factors = {'norm_mix_g': 4.31,
     'attn_q_norm_g': 7.999,
     'attn_k_norm_g': 8.0,
     'attn_out_norm_g': 64.0,
     'dn_out_norm_g': 31.357,
     'norm_ffn_g': 34.616,
     'rel_bias': 8.0}
    for name, (base, spread) in spreads.items():
        noise = np.random.default_rng([zlib.crc32(name.encode()), seed]).standard_normal(out[name].shape)
        drawn = base * np.exp(spread * noise) if base else spread * noise
        out[name] = __import__('jax').numpy.asarray(drawn.astype(out[name].dtype))
    for name, factor in factors.items():
        out[name] = (out[name] * factor).astype(out[name].dtype)
    return out
```

```python
from contextlib import ExitStack

import numpy as np
import concourse.bass as bass
from concourse import mybir

F32 = mybir.dt.float32
F32R = mybir.dt.float32r
ACT = mybir.ActivationFunctionType
ALU = mybir.AluOpType
ds = bass.ds

P = 128
T = 1024
D = 1024
NT = T // P
KT = D // P
HALF = 512
CHUNK = 64
DHA = 64
NHA = 8
NPAIR = NHA // 2
BAND = 5
KEYS = BAND * P
CLIP = 128
NHD = 4
CONV = 4
FFN = 2816
NF = FFN // P
EPS = 1e-6
NEG = -1e30
LEVELS = 7

Q0, K0, V0, DQ0, Z0, NPROJ = 0, 4, 8, 12, 24, 28
U_GATES = NPROJ
U_OUT = U_GATES + 1
U_FFN = U_OUT + KT
N_UNITS = U_FFN + 3 * NF
BANKS0 = 2
ADDED0 = 4
AO0 = 2
MIXED0 = 1


def down_unit(f):
    return U_FFN + 3 * f + 4 if not isinstance(f, int) or f < NF - 1 else N_UNITS - 1


def gate_unit(f):
    return U_FFN + 3 * f - 1 if not isinstance(f, int) or f > 0 else U_FFN


def up_unit(f):
    return U_FFN + 3 * f if not isinstance(f, int) or f > 0 else U_FFN + 1


def ge(eng, sem, value):
    if isinstance(value, int) and value <= 0:
        return
    eng.wait_ge(sem, value)


def wait_apart(eng, sem, value, passed):
    eng.wait_ge(sem, value)
    eng.sem_inc(passed, 1)


def hymba_block(nc, x, units, gain_mix, gain_q, gain_k, bias_rev, gain_att, conv_w, a_log, dt_bias,
                gain_dn, gain_ffn, bias_ext, bias_rows, out):
    with ExitStack() as ctx:
        def sb(name, shape, dt=F32, stack=ctx):
            return stack.enter_context(nc.sbuf_tensor(name, shape, dt))

        def sem(name):
            return ctx.enter_context(nc.semaphore(name))

        ident = sb("ident", [P, P])
        ones = sb("ones", [P, P])
        ones_pair = sb("ones_pair", [P, P])
        tri = sb("tri", [P, P])
        causal = sb("causal", [P, P])
        level_mask = sb("level_mask", [P, LEVELS, P])
        eps_col = sb("eps_col", [P, 1])
        ssq = sb("ssq", [P, NT])
        rstd = sb("rstd", [P, NT])
        gq_col = sb("gq_col", [P, 1])
        gk_col = sb("gk_col", [P, 1])
        gdn_col = sb("gdn_col", [P, 1])
        taps = sb("taps", [P, 12, CONV])
        alog_row = sb("alog_row", [P, NHD])
        dtb_row = sb("dtb_row", [P, NHD])
        neg_max = sb("neg_max", [P, 2])
        row_sum = sb("row_sum", [P, 4])
        row_inv = sb("row_inv", [P, 2])
        gates = sb("gates", [P, NT, 8])
        beta = sb("beta", [P, NT, NHD])
        gstep = sb("gstep", [P, NT, NHD])
        gcum = sb("gcum", [P, NT, NHD])
        nbeg = sb("nbeg", [P, NT, NHD])
        gtmp = sb("gtmp", [P, NT, NHD])
        KDS = sb("KDS", [P, 2, NHD])
        RAW = sb("RAW", [P, 2, D])
        SPLIT = sb("SPLIT", [P, 2, 2, D], F32R)

        def overlapped(*layouts):
            got = []
            for layout in layouts:
                with ExitStack() as stack:
                    got.append([sb(n, s, d, stack) for n, s, d in layout])
            return got

        att_layout = [("QB", [P, T], F32), ("KB", [P, T], F32), ("SQ", [P, 2, HALF], F32),
                      ("RS", [P, 2, HALF], F32), ("BIAS", [P, 2, KEYS], F32), ("SX", [P, 2, KEYS], F32),
                      ("PT", [P, 2, KEYS], F32), ("AO", [P, NT, HALF], F32), ("GT", [P, T], F32),
                      ("gain_att_bc", [P, HALF], F32), ("AON", [P, 2, HALF], F32)]
        a_bufs = ["dSQ", "dKQ"]
        b_bufs = ["dVS", "dGD", "dBD", "dD", "dEX", "dNL", "dKB", "dIN", "dVB", "dWT", "dQD", "dKD", "dU"]
        dn1 = []
        for p in range(2):
            dn1 += [(f"{n}{p}", [P, 8, P], F32) for n in a_bufs]
            dn1 += [(f"{n}{p}", [P, NHD, P], F32) for n in b_bufs[:-2 if p else None]]
        with ExitStack() as stack:
            HT = sb("HT", [P, 2, KT, T], F32R, stack)
        (att, dna, mixs) = overlapped(
            att_layout, dn1,
            [("MS", [P, 2, 2, T], F32R)])
        ctx.enter_context(nc.sbuf_tensor("region1", [P, 2 * KT * T], F32))
        QB, KB, SQ, RS, BIAS, SX, PT, AO, GT, gain_att_bc, AON = att
        MS = mixs[0]
        (proj_l, dn2, ffn_l, mix_l) = overlapped(
            [("PROJ", [P, NPROJ, T], F32)],
            [("pad_mix", [P, 8, T], F32), ("dKD1", [P, NHD, P], F32), ("dU1", [P, NHD, P], F32),
             ("STATE", [P, NHD, P], F32), ("VNEW", [P, NHD, P], F32), ("OSQ", [P, NHD, P], F32),
             ("ORS", [P, NHD, P], F32)],
            [("HS", [P, 2, 2, T], F32R), ("GG", [P, 2, T], F32), ("FXN", [P, 2, T], F32),
             ("gain_ffn_bc", [P, T], F32), ("FJUNK", [P, T], F32),
             ("pad_f", [P, 10, T], F32), ("X2", [P, NT, T], F32)],
            [("MIX", [P, KT, T], F32)])
        PROJ = proj_l[0]
        _, dKD1, dU1, STATE, VNEW, OSQ, ORS = dn2
        HS, GG, FXN, gain_ffn_bc, FJUNK, _, X2 = ffn_l
        MIX = mix_l[0]
        ctx.enter_context(nc.sbuf_tensor("region2", [P, NPROJ * T], F32))
        byname = {n: t for (n, _, _), t in zip(dn1, dna)}
        byname["dKD1"], byname["dU1"] = dKD1, dU1
        DN = [{n: byname[f"{n}{p}"] for n in a_bufs + b_bufs} for p in range(2)]

        XIN = PROJ[:, 20:28, :]
        gain_mix_bc = PROJ[:, 19, :]
        XN = PROJ[:, 17:19, :]
        JUNK = PROJ[:, 16, :]
        EXT = PROJ[:, 15, :]

        ps = ctx.enter_context(nc.psum_tensor("ps", [P, 8, HALF], F32))

        small_in = sem("small_in")
        x_in = [sem(f"x_in{m}") for m in range(NT)]
        x_again = sem("x_again")
        ext_in, ext_filled, ext_out = sem("ext_in"), sem("ext_filled"), sem("ext_out")
        gain_ffn_in, gain_att_in = sem("gain_ffn_in"), sem("gain_att_in")
        bias_in = sem("bias_in")
        out_stored = sem("out_stored")
        passed_pool, passed_act, passed_dve = sem("passed_pool"), sem("passed_act"), sem("passed_dve")
        consts, const_step = sem("consts"), sem("const_step")
        raw_in = [sem("raw_in0"), sem("raw_in1")]
        hi_done, split_done, unit_used = sem("hi_done"), sem("split_done"), sem("unit_used")
        nrm = {w: {n: sem(f"norm_{w}_{n}") for n in
                   ("ssq", "ln", "rstd", "xn", "turned", "hi", "lo")} for w in ("inp", "ffn")}
        conv_first, conv_tap = sem("conv_first"), sem("conv_tap")
        banks_free = sem("banks_free")
        proj_final = sem("proj_final")
        rows_done, rows_added = sem("rows_done"), sem("rows_added")

        def bank_pair(slot, base=0):
            b = base + 2 * slot
            return ps[:, b:b + 2, :]

        def unit_dma(sp, j, slot):
            sp.dma_start(RAW[:, slot, :], units[j, :, :] if isinstance(j, int)
                         else units[ds(j, 1), :, :].rearrange("u p n -> (u p) n")).then_inc(raw_in[slot], 16)

        def unit_split(pool, slot, turn, used, j):
            pool.wait_ge(raw_in[slot], 16 * turn)
            if isinstance(used, int):
                ge(pool, unit_used, used)
            else:
                wait_apart(pool, unit_used, used, passed_pool)
            pool.tensor_copy(SPLIT[:, slot, 0, :], RAW[:, slot, :]).then_inc(hi_done, 1)
            pool.wait_ge(hi_done, j)
            pool.tensor_tensor(SPLIT[:, slot, 1, :], RAW[:, slot, :],
                               SPLIT[:, slot, 0, :].bitcast(F32), ALU.subtract).then_inc(split_done, 1)

        def norm_act_stats(act, w, src, junk, m, n):
            act.activation(junk, src, ACT.Square, accum_out=ssq[:, ds(m, 1)]).then_inc(nrm[w]["ssq"], 1)
            act.wait_ge(nrm[w]["ssq"], n)
            act.activation(rstd[:, ds(m, 1)], ssq[:, ds(m, 1)], ACT.Ln, bias=eps_col[:, :],
                           scale=1.0 / D).then_inc(nrm[w]["ln"], 1)
            act.wait_ge(nrm[w]["ln"], n)
            act.activation(rstd[:, ds(m, 1)], rstd[:, ds(m, 1)], ACT.Exp, scale=-0.5).then_inc(nrm[w]["rstd"], 1)

        def norm_act(act, w, src_of, junk, ready):
            for m in range(NT):
                ready(act, m)
                norm_act_stats(act, w, src_of(m), junk, m, m + 1)
                if m:
                    norm_act_hi(act, w, m - 1)
            norm_act_hi(act, w, NT - 1)

        def norm_act_hi(act, w, m):
            act.wait_ge(nrm[w]["turned"], m + 1)
            act.activation(HT[:, 0, :, m * P:(m + 1) * P],
                           bank_pair(m % 2).rearrange("p b (k c) -> p (b k) c", c=P),
                           ACT.Copy).then_inc(nrm[w]["hi"], 1)

        def norm_dve(dve, w, src_of, gain_bc, xn):
            for m in range(NT + 1):
                if m < NT:
                    dve.wait_ge(nrm[w]["rstd"], m + 1)
                    ge(dve, nrm[w]["turned"], m - 1)
                    dve.scalar_tensor_tensor(out=xn[:, m % 2, :], in0=src_of(m), scalar=rstd[:, m:m + 1],
                                             in1=gain_bc, op0=ALU.mult, op1=ALU.mult).then_inc(nrm[w]["xn"], 1)
                if m:
                    dve.wait_ge(nrm[w]["hi"], m)
                    dve.tensor_tensor(HT[:, 1, :, (m - 1) * P:m * P],
                                      bank_pair((m - 1) % 2).rearrange("p b (k c) -> p (b k) c", c=P),
                                      HT[:, 0, :, (m - 1) * P:m * P].bitcast(F32),
                                      ALU.subtract).then_inc(nrm[w]["lo"], 1)

        def norm_pe(pe, w, xn):
            for m in range(NT):
                pe.wait_ge(nrm[w]["xn"], m + 1)
                ge(pe, nrm[w]["lo"], m - 1)
                for k in range(KT):
                    mm = pe.transpose(ps[:, 2 * (m % 2) + k // 4, (k % 4) * P:(k % 4 + 1) * P],
                                      xn[:, m % 2, k * P:(k + 1) * P], ident[:, :])
                mm.then_inc(nrm[w]["turned"], 1)

        def columns_unit(pe, slot, bank):
            for k in range(KT):
                for part in range(2):
                    w = SPLIT[:, slot, part, k * P:(k + 1) * P]
                    for th in range(2):
                        for other in range(2 - part):
                            mm = pe.matmul(ps[:, bank + th, :], w, HT[:, other, k, th * HALF:(th + 1) * HALF],
                                           start=(k == 0 and part == 0 and other == 0),
                                           stop=(k == KT - 1 and part == 1))
            return mm

        def rows_unit(pe, slot, left, row0, pairs, base):
            for t in range(NT):
                b = base + 2 * (t % pairs)
                pe.wait_ge(rows_added, row0 + (ADDED0 + t + 1 - pairs))
                for part in range(2):
                    w = left(part, t)
                    for dh in range(2):
                        for other in range(2 - part):
                            mm = pe.matmul(ps[:, b + dh, :], w,
                                           SPLIT[:, slot, other, dh * HALF:(dh + 1) * HALF],
                                           start=(part == 0 and other == 0), stop=(part == 1))
                mm.then_inc(rows_done if t < NT - 1 else unit_used, 1)

        def add_rows(dve, unit, done0, t, pairs, base):
            if t < NT - 1:
                dve.wait_ge(rows_done, done0 + (t + 1))
            else:
                dve.wait_ge(unit_used, unit + 1)
            b = base + 2 * (t % pairs)
            row = X2[:, t, :].rearrange("p (b c) -> p b c", c=HALF)
            dve.tensor_tensor(row, ps[:, b:b + 2, :], row, ALU.add).then_inc(rows_added, 1)

        A = {n: sem("att_" + n) for n in
             ("gt", "gt_turned", "v_turned", "v_back", "sq", "sums", "ln", "rs", "qk", "masked", "scores", "biased",
              "prob", "turned", "pt", "pv", "inv", "ao", "ssq", "ln2", "rstd2", "aon", "turned2", "mix")}
        G = {n: sem("gate_" + n) for n in ("in", "act", "dve", "cum")}
        DS = [{n: sem(f"dn{p}_{n}") for n in
               ("diag", "rows", "sq", "sums", "vs", "ex", "sub", "pre", "dec", "ln", "rs", "kq", "gram", "kds",
                "intra", "db", "nl", "turned", "scaled", "p_mm", "p", "du_mm", "tu", "wt_mm", "wt",
                "new_mm", "new", "out_mm", "kv_mm", "st", "osq", "osum", "oln", "ors", "of", "mixed")}
              for p in range(2)]
        state_zero = sem("state_zero")
        mix_hi, mix_lo = sem("mix_hi"), sem("mix_lo")
        F = {n: sem("ffn_" + n) for n in ("silu", "h", "hi", "lo")}

        NU = 2 * NT

        def unit_of(u):
            qb, s = u // 2, u % 2
            nt = min(qb + 1, BAND)
            return qb, s, nt, qb + 1 - nt

        def heads(bank):
            return ps[:, bank, :].rearrange("p (h c) -> p h c", c=P)

        def over_heads(tile):
            return tile.unsqueeze(1).to_broadcast([P, NHD, P])

        def over_cols(col):
            return col.unsqueeze(2).to_broadcast([P, NHD, P])

        def tile_cols(t, m):
            return t[:, ds(m, 1), :].rearrange("p a h -> p (a h)")

        def proj_tile(j):
            return PROJ[:, ds(j, 1), :].rearrange("p a c -> p (a c)")

        def proj_banks(j):
            return PROJ[:, ds(j, 1), :].rearrange("p a (b c) -> p (a b) c", c=HALF)

        with nc.Block() as block:

            @block.sync
            def _(sp):
                for m in range(NT):
                    sp.dma_start(XIN[:, m, :], x[m * P:(m + 1) * P, :]).then_inc(x_in[m], 16)
                unit_dma(sp, 0, 0)
                unit_dma(sp, 1, 1)
                with sp.Fori(1, N_UNITS // 2) as i:
                    for slot in range(2):
                        sp.wait_ge(split_done, i * 2 + (slot - 1))
                        unit_dma(sp, i * 2 + slot, slot)
                sp.wait_ge(split_done, N_UNITS - 2)
                unit_dma(sp, N_UNITS - 1, 0)
                for t in range(NT):
                    sp.wait_ge(rows_added, ADDED0 + NT * (KT + NF - 1) + t + 1)
                    sp.dma_start(out[t * P:(t + 1) * P, :], X2[:, t, :]).then_inc(out_stored, 16)
                sp.wait_ge(out_stored, 16 * NT)

            @block.gpsimd
            def _(pool):
                pool.memset(ident[:, :], 0.0).then_inc(const_step, 1)
                pool.memset(ones[:, :], 1.0).then_inc(const_step, 1)
                pool.memset(ones_pair[:, :], 1.0).then_inc(const_step, 1)
                pool.memset(tri[:, :], 1.0).then_inc(const_step, 1)
                pool.memset(causal[:, :], 0.0).then_inc(const_step, 1)
                pool.memset(level_mask[:, :, :], 1.0).then_inc(const_step, 1)
                pool.memset(eps_col[:, :], EPS).then_inc(const_step, 1)
                pool.wait_ge(const_step, 7)
                pool.affine_select(out=ident[:, :], in_=ident[:, :], compare_op=ALU.not_equal, fill=1.0, base=0,
                                   pattern=[[-1, P]], channel_multiplier=1).then_inc(consts, 1)
                pair = ones_pair[:, :].rearrange("p (b c) -> p b c", c=DHA)
                pool.affine_select(out=pair, in_=pair, compare_op=ALU.is_ge, fill=0.0, base=0,
                                   pattern=[[-DHA, 2], [0, DHA]], channel_multiplier=1).then_inc(const_step, 1)
                pool.wait_ge(const_step, 8)
                pool.affine_select(out=pair, in_=pair, compare_op=ALU.is_ge, fill=0.0, base=DHA - 1,
                                   pattern=[[DHA, 2], [0, DHA]], channel_multiplier=-1).then_inc(const_step, 1)
                pool.affine_select(out=tri[:, :], in_=tri[:, :], compare_op=ALU.is_ge, fill=0.0, base=0,
                                   pattern=[[1, P]], channel_multiplier=-1).then_inc(const_step, 1)
                pool.affine_select(out=causal[:, :], in_=causal[:, :], compare_op=ALU.is_ge, fill=NEG, base=0,
                                   pattern=[[1, P]], channel_multiplier=-1).then_inc(const_step, 1)
                unit_split(pool, 0, 1, 0, 1)
                unit_split(pool, 1, 1, 0, 2)
                n = 11
                for lv in range(LEVELS):
                    s = 1 << lv
                    blocks = level_mask[:, lv, :].rearrange("p (b h r) -> p b h r", h=2, r=s)
                    pool.wait_ge(const_step, n)
                    pool.affine_select(out=blocks, in_=blocks, compare_op=ALU.is_ge, fill=0.0, base=-s,
                                       pattern=[[-2 * s, P // (2 * s)], [0, 2], [0, s]],
                                       channel_multiplier=1).then_inc(const_step, 1)
                    pool.wait_ge(const_step, n + 1)
                    pool.affine_select(out=blocks, in_=blocks, compare_op=ALU.is_ge, fill=0.0, base=2 * s - 1,
                                       pattern=[[2 * s, P // (2 * s)], [0, 2], [0, s]],
                                       channel_multiplier=-1).then_inc(const_step, 1)
                    pool.wait_ge(const_step, n + 2)
                    pool.memset(blocks[:, :, 1, :], 0.0).then_inc(const_step if lv < LEVELS - 1 else consts, 1)
                    n += 3
                with pool.Fori(1, N_UNITS // 2) as i:
                    for slot in range(2):
                        unit_split(pool, slot, i + 1, i * 2 + (slot - 1), i * 2 + (slot + 1))
                unit_split(pool, 0, N_UNITS // 2 + 1, N_UNITS - 2, N_UNITS)

            def att_rs(act, i, n):
                half = n % 2
                act.wait_ge(A["sums"], i * 4 + (n + 1))
                if n >= 2:
                    act.wait_ge(A["qk"], i * 4 + (n - 1))
                act.activation(RS[:, half, :], ps[:, 6 + half, :], ACT.Ln, bias=eps_col[:, :],
                               scale=1.0 / DHA).then_inc(A["ln"], 1)
                act.wait_ge(A["ln"], i * 4 + (n + 1))
                act.activation(RS[:, half, :], RS[:, half, :], ACT.Exp, scale=-0.5).then_inc(A["rs"], 1)

            def att_pt(eng, i, u):
                nt = unit_of(u)[2]
                eng.wait_ge(A["turned"], i * NU + (u + 1))
                if u >= 2:
                    eng.wait_ge(A["pv"], i * NU + (u - 1))
                if u >= 1:
                    eng.wait_ge(A["pt"], i * NU + u)
                src = ps[:, 4:6, :].rearrange("p b c -> p (b c)")[:, 0:nt * P]
                if u % 2 == 0:
                    eng.activation(PT[:, u % 2, 0:nt * P], src, ACT.Copy).then_inc(A["pt"], 1)
                else:
                    eng.tensor_copy(PT[:, u % 2, 0:nt * P], src).then_inc(A["pt"], 1)

            def dn_act_1(act, i, p):
                S, B = DS[p], DN[p]
                tok = ds(i * (2 * P) + p * P, P)
                wait_apart(act, S["mixed"], i + MIXED0, passed_act)
                act.activation(B["dSQ"][:, :, :], PROJ[:, DQ0:DQ0 + 8, tok], ACT.Square).then_inc(S["sq"], 1)
                act.activation(B["dVS"][:, :, :], PROJ[:, DQ0 + 8:DQ0 + 12, tok], ACT.Copy).then_inc(S["vs"], 1)
                act.wait_ge(S["rows"], i + 1)
                act.activation(B["dEX"][:, :, :], heads(4 * p + 2), ACT.Exp).then_inc(S["ex"], 1)

            def dn_act_2(act, i, p):
                S, B = DS[p], DN[p]
                act.wait_ge(S["sums"], i + 1)
                act.activation(B["dSQ"][:, :, :], ps[:, 4 * p:4 * p + 2, :].rearrange("p b (h c) -> p (b h) c", c=P),
                               ACT.Ln, bias=eps_col[:, :]).then_inc(S["ln"], 1)
                act.wait_ge(S["ln"], i + 1)
                act.activation(B["dSQ"][:, :, :], B["dSQ"][:, :, :], ACT.Exp, scale=-0.5).then_inc(S["rs"], 1)
                act.wait_ge(S["pre"], i + 1)
                act.activation(B["dD"][:, :, :], B["dD"][:, :, :], ACT.Exp).then_inc(S["dec"], 1)

            def dn_act_b(act, i, p):
                S, B = DS[p], DN[p]
                act.wait_ge(S["new_mm"], i + 1)
                act.activation(VNEW[:, :, :], heads(4 * p), ACT.Copy).then_inc(S["new"], 1)
                act.wait_ge(S["out_mm"], i + 1)
                act.activation(OSQ[:, :, :], heads(4 * p + 1), ACT.Square).then_inc(S["osq"], 1)
                act.wait_ge(S["osum"], i + 1)
                if p:
                    act.wait_ge(DS[0]["mixed"], i + 1 + MIXED0)
                act.activation(ORS[:, :, :], heads(4 * p + 3), ACT.Ln, bias=eps_col[:, :],
                               scale=1.0 / P).then_inc(S["oln"], 1)
                act.wait_ge(S["oln"], i + 1)
                act.activation(ORS[:, :, :], ORS[:, :, :], ACT.Exp, scale=-0.5).then_inc(S["ors"], 1)

            def ffn_act(act, f, par):
                act.wait_ge(unit_used, gate_unit(f) + 1)
                act.activation(GG[:, par, :].rearrange("p (b c) -> p b c", c=HALF), bank_pair(0),
                               ACT.Silu).then_inc(F["silu"], 1)
                act.wait_ge(F["h"], f + 1)
                if not isinstance(f, int) or f >= 2:
                    act.wait_ge(unit_used, down_unit(f - 2) + 1)
                act.activation(HS[:, par, 0, :], GG[:, par, :], ACT.Copy).then_inc(F["hi"], 1)

            @block.scalar
            def _(act):
                act.dma_start(gain_mix_bc, gain_mix.partition_broadcast(P)).then_inc(small_in, 16)
                act.dma_start(EXT[0:NHA, 4 * P - 1:4 * P + 2 * CLIP], bias_rev).then_inc(ext_in, 16)
                for half in range(2):
                    act.dma_start(gq_col[half * 64:(half + 1) * 64, :], gain_q).then_inc(small_in, 16)
                    act.dma_start(gk_col[half * 64:(half + 1) * 64, :], gain_k).then_inc(small_in, 16)
                act.dma_start(gdn_col[:, :], gain_dn).then_inc(small_in, 16)
                act.dma_start(taps[:, :, :], conv_w).then_inc(small_in, 16)
                act.dma_start(alog_row[:, :], a_log.partition_broadcast(P)).then_inc(small_in, 16)
                act.dma_start(dtb_row[:, :], dt_bias.partition_broadcast(P)).then_inc(small_in, 16)
                act.wait_ge(consts, 1)
                norm_act(act, "inp", lambda m: XIN[:, m, :], JUNK, lambda a, m: a.wait_ge(x_in[m], 16))
                act.wait_ge(ext_filled, 1)
                act.dma_start(bias_ext, EXT[0:NHA, 0:6 * P]).then_inc(ext_out, 16)
                act.wait_ge(ext_out, 16)
                act.dma_start(bias_rows.rearrange("a s p c -> (a s) p c"),
                              bass.AP(bias_ext.tensor, P - 1, [[6 * P, NHA], [-1, P], [1, KEYS]])).then_inc(ext_out, 16)
                act.wait_ge(small_in, 9 * 16)
                with act.Fori(0, V0 // 2 + 2) as i:
                    for slot in range(2):
                        wait_apart(act, unit_used, i * 2 + (slot + 1), passed_act)
                        act.activation(proj_banks(i * 2 + slot), bank_pair(slot, 4), ACT.Copy).then_inc(banks_free, 1)
                with act.Fori(0, 6) as i:
                    for slot in range(2):
                        wait_apart(act, unit_used, i * 2 + (DQ0 + slot + 1), passed_act)
                        act.activation(proj_banks(i * 2 + (DQ0 + slot)), bank_pair(slot, 4), ACT.Copy,
                                       scale=taps[:, ds(i * 2 + slot, 1), CONV - 1]).then_inc(conv_first, 1)
                        wait_apart(act, banks_free, i * 2 + (DQ0 + slot + 1 + BANKS0), passed_act)
                        act.activation(proj_tile(i * 2 + (DQ0 + slot)), proj_tile(i * 2 + (DQ0 + slot)),
                                       ACT.Silu).then_inc(proj_final, 1)
                with act.Fori(0, 2) as i:
                    for slot in range(2):
                        wait_apart(act, unit_used, i * 2 + (Z0 + slot + 1), passed_act)
                        act.activation(proj_banks(i * 2 + (Z0 + slot)), bank_pair(slot, 4),
                                       ACT.Silu).then_inc(banks_free, 1)
                act.wait_ge(unit_used, U_GATES + 1)
                act.activation(GT[0:8, :].rearrange("p (b c) -> p b c", c=HALF), bank_pair(0, 4)[0:8],
                               ACT.Copy).then_inc(A["gt"], 1)
                act.dma_start(gain_att_bc[:, :], gain_att.partition_broadcast(P)).then_inc(gain_att_in, 16)
                act.wait_ge(G["dve"], 1)
                act.activation(gtmp[:, :, :], gstep[:, :, :], ACT.Abs).then_inc(G["act"], 1)
                act.activation(beta[:, :, :], gates[:, :, 0:NHD], ACT.Exp, scale=-1.0).then_inc(G["act"], 1)
                act.activation(alog_row[:, :], alog_row[:, :], ACT.Exp).then_inc(G["act"], 1)
                act.wait_ge(G["act"], 3)
                act.activation(gtmp[:, :, :], gtmp[:, :, :], ACT.Exp, scale=-1.0).then_inc(G["act"], 1)
                act.wait_ge(G["act"], 4)
                act.activation(gtmp[:, :, :], gtmp[:, :, :], ACT.Ln, bias=1.0).then_inc(G["act"], 1)
                act.wait_ge(G["dve"], 6)
                act.activation(nbeg[:, :, :], gcum[:, :, :], ACT.Exp).then_inc(G["act"], 1)

                act.wait_ge(ext_out, 32)
                with act.Fori(0, NPAIR) as i:
                    act.dma_start(BIAS[:, :, :], bias_rows[ds(i, 1), :, :, :].rearrange("a s p c -> p (a s) c")
                                  ).then_inc(bias_in, 16)
                    for n in range(4):
                        act.activation(SQ[:, n % 2, :],
                                       PROJ[:, ds(i + 4 * (n // 2), 1), (n % 2) * HALF:(n % 2 + 1) * HALF]
                                       .rearrange("p a c -> p (a c)"), ACT.Square).then_inc(A["sq"], 1)
                        if n >= 1:
                            att_rs(act, i, n - 1)
                    att_rs(act, i, 3)
                    for u in range(NU):
                        nt = unit_of(u)[2]
                        act.wait_ge(A["biased"], i * NU + (u + 1))
                        act.activation(SX[:, u % 2, 0:nt * P], SX[:, u % 2, 0:nt * P], ACT.Exp, scale=-1.0,
                                       bias=neg_max[:, u % 2:u % 2 + 1],
                                       accum_out=row_sum[:, u % 4:u % 4 + 1]).then_inc(A["prob"], 1)
                        if u % 2 == 1:
                            att_pt(act, i, u - 1)
                act.wait_ge(A["ao"], NPAIR * NU + AO0)
                for m in range(NT):
                    ge(act, A["ssq"], m - 1)
                    act.activation(SX[:, m % 2, 0:HALF], AO[:, m, :], ACT.Square,
                                   accum_out=ssq[:, m:m + 1]).then_inc(A["ssq"], 1)
                act.wait_ge(A["ssq"], NT)
                act.activation(rstd[:, :], ssq[:, :], ACT.Ln, bias=eps_col[:, :],
                               scale=1.0 / HALF).then_inc(A["ln2"], 1)
                act.wait_ge(A["ln2"], 1)
                act.activation(rstd[:, :], rstd[:, :], ACT.Exp, scale=-0.5).then_inc(A["rstd2"], 1)
                for m in range(NT):
                    act.wait_ge(A["turned2"], m + 1)
                    act.activation(MIX[:, 0:4, m * P:(m + 1) * P], heads(m % 2), ACT.Copy).then_inc(A["mix"], 1)

                act.wait_ge(proj_final, 12)
                act.wait_ge(A["mix"], NT)
                with act.Fori(0, NT // 2) as i:
                    for p in range(2):
                        dn_act_1(act, i, p)
                    for p in range(2):
                        dn_act_2(act, i, p)
                    for p in range(2):
                        act.wait_ge(DS[p]["wt_mm"], i + 1)
                        act.activation(DN[p]["dWT"][:, :, :], heads(4 * p + 3), ACT.Copy).then_inc(DS[p]["wt"], 1)
                    for p in range(2):
                        dn_act_b(act, i, p)

                for p in range(2):
                    act.wait_ge(DS[p]["mixed"], NT // 2 + MIXED0)
                for m in range(NT):
                    act.dma_start(X2[:, m, :], x[m * P:(m + 1) * P, :]).then_inc(x_in[m], 16)
                act.dma_start(gain_ffn_bc[:, :], gain_ffn.partition_broadcast(P)).then_inc(gain_ffn_in, 16)
                with act.Fori(0, KT // 2) as i:
                    for slot in range(2):
                        wait_apart(act, unit_used, i * 2 + (U_OUT + slot - 1), passed_act)
                        act.activation(MS[:, slot, 0, :], MIX[:, ds(i * 2 + slot, 1), :].rearrange("p a c -> p (a c)"),
                                       ACT.Copy).then_inc(mix_hi, 1)
                act.wait_ge(unit_used, U_FFN)
                norm_act(act, "ffn", lambda m: X2[:, m, :], FJUNK[:, :],
                         lambda a, m: a.wait_ge(rows_added, ADDED0 + NT * (KT - 1) + m + 1))
                ffn_act(act, 0, 0)
                with act.Fori(0, (NF - 2) // 2) as i:
                    ffn_act(act, i * 2 + 1, 1)
                    ffn_act(act, i * 2 + 2, 0)
                ffn_act(act, NF - 1, 1)

            def dn_dve_diag(dve, i, p):
                S, B, m = DS[p], DN[p], i * 2 + p
                dve.tensor_tensor(B["dGD"][:, :, :], over_heads(ident[:, :]), over_cols(tile_cols(gcum, m)),
                                  ALU.mult).then_inc(S["diag"], 1)
                dve.tensor_tensor(B["dBD"][:, :, :], over_heads(ident[:, :]), over_cols(tile_cols(beta, m)),
                                  ALU.mult).then_inc(S["diag"], 1)

            def dn_dve_decay(dve, i, p):
                S, B, m = DS[p], DN[p], i * 2 + p
                dve.wait_ge(S["ex"], i + 1)
                dve.tensor_tensor(B["dD"][:, :, :], heads(4 * p + 2), over_cols(tile_cols(gcum, m)),
                                  ALU.subtract).then_inc(S["sub"], 1)
                dve.wait_ge(S["sub"], i + 1)
                dve.tensor_tensor(B["dD"][:, :, :], B["dD"][:, :, :], over_heads(causal[:, :]),
                                  ALU.add).then_inc(S["pre"], 1)

            def dn_dve_kq(dve, i, p):
                S, B = DS[p], DN[p]
                tok = ds(i * (2 * P) + p * P, P)
                kq = B["dKQ"][:, :, :].rearrange("p (h w) c -> p h w c", w=2)
                dve.wait_ge(S["rs"], i + 1)
                dve.tensor_tensor(kq[:, :, 0, :], PROJ[:, DQ0 + 4:DQ0 + 8, tok], B["dSQ"][:, 4:8, :],
                                  ALU.mult).then_inc(S["kq"], 1)
                dve.scalar_tensor_tensor(out=kq[:, :, 1, :], in0=PROJ[:, DQ0:DQ0 + 4, tok], scalar=float(P) ** -0.5,
                                         in1=B["dSQ"][:, 0:4, :], op0=ALU.mult, op1=ALU.mult).then_inc(S["kq"], 1)

            def dn_dve_local(dve, i, p):
                S, B = DS[p], DN[p]
                kq = B["dKQ"][:, :, :].rearrange("p (h w) c -> p h w c", w=2)
                gram = ps[:, 4 * p:4 * p + 2, :].rearrange("p b (h w c) -> p (b h) w c", w=2, c=P)
                dve.wait_ge(S["dec"], i + 1)
                dve.tensor_copy(KDS[:, p, :], B["dD"][:, :, P - 1:P].rearrange("p h a -> p (h a)")).then_inc(S["kds"], 1)
                dve.wait_ge(S["kq"], 2 * i + 2)
                dve.tensor_tensor(B["dQD"][:, :, :], kq[:, :, 1, :], B["dEX"][:, :, :], ALU.mult).then_inc(S["kds"], 1)
                dve.wait_ge(S["gram"], i + 1)
                dve.tensor_tensor(B["dIN"][:, :, :], gram[:, :, 1, :], B["dD"][:, :, :], ALU.mult).then_inc(S["intra"], 1)
                dve.wait_ge(S["kds"], 2 * i + 2)
                dve.wait_ge(S["intra"], i + 1)
                dve.tensor_tensor(B["dD"][:, :, :], heads(4 * p + 3), B["dD"][:, :, :], ALU.mult).then_inc(S["db"], 1)
                dve.wait_ge(S["db"], i + 1)
                dve.scalar_tensor_tensor(out=B["dNL"][:, :, :], in0=gram[:, :, 0, :], scalar=-1.0,
                                         in1=B["dD"][:, :, :], op0=ALU.mult, op1=ALU.mult).then_inc(S["nl"], 1)

            def dn_dve_scaled(dve, i, p):
                S, B, m = DS[p], DN[p], i * 2 + p
                dve.wait_ge(S["turned"], i + 1)
                dve.tensor_tensor(B["dKB"][:, :, :], heads(4 * p + 2), over_cols(tile_cols(nbeg, m)),
                                  ALU.mult).then_inc(S["scaled"], 1)
                dve.tensor_tensor(B["dKD"][:, :, :], heads(4 * p + 2), over_cols(KDS[:, p, :]),
                                  ALU.mult).then_inc(S["scaled"], 1)
                dve.tensor_tensor(B["dVB"][:, :, :], heads(4 * p + 3), over_cols(tile_cols(beta, m)),
                                  ALU.mult).then_inc(S["scaled"], 1)

            def dn_dve_p(dve, i, p, lv):
                S, B = DS[p], DN[p]
                dve.wait_ge(S["p_mm"], i * LEVELS + (lv + 1))
                dve.tensor_tensor(B["dGD"][:, :, :], heads(4 * p), over_heads(level_mask[:, lv, :]),
                                  ALU.mult).then_inc(S["p"], 1)

            def dn_dve_tu(dve, i, p, lv):
                S, B = DS[p], DN[p]
                dve.wait_ge(S["du_mm"], i * LEVELS + (lv + 1))
                dve.wait_ge(S["p"], i * LEVELS + (lv + 1))
                if lv == 0:
                    dve.tensor_tensor(B["dBD"][:, :, :], B["dGD"][:, :, :], over_heads(ident[:, :]),
                                      ALU.add).then_inc(S["tu"], 1)
                elif lv < LEVELS - 1:
                    dve.wait_ge(S["tu"], i * (2 * LEVELS - 1) + 2 * lv)
                    dve.tensor_tensor(B["dBD"][:, :, :], heads(4 * p + 1), B["dBD"][:, :, :],
                                      ALU.add).then_inc(S["tu"], 1)
                before = over_heads(ident[:, :]) if lv == 0 else B["dU"][:, :, :]
                dve.tensor_tensor(B["dU"][:, :, :], heads(4 * p + 2), before, ALU.add).then_inc(S["tu"], 1)

            def dn_dve_b(dve, i, p):
                S, B = DS[p], DN[p]
                dve.wait_ge(S["kv_mm"], i + 1)
                for h in range(NHD):
                    dve.scalar_tensor_tensor(out=STATE[:, h, :], in0=STATE[:, h, :],
                                             scalar=B["dEX"][:, h, P - 1:P], in1=ps[:, 4 * p + 2, h * P:(h + 1) * P],
                                             op0=ALU.mult, op1=ALU.add).then_inc(S["st"], 1)
                dve.wait_ge(S["ors"], i + 1)
                dve.scalar_tensor_tensor(out=ORS[:, :, :], in0=heads(4 * p + 1), scalar=gdn_col[:, 0:1],
                                         in1=ORS[:, :, :], op0=ALU.mult, op1=ALU.mult).then_inc(S["of"], 1)
                dve.wait_ge(S["of"], i + 1)
                tok = ds(i * (2 * P) + p * P, P)
                dve.tensor_tensor(MIX[:, 4:8, tok], ORS[:, :, :], PROJ[:, Z0:Z0 + 4, tok],
                                  ALU.mult).then_inc(S["mixed"], 1)

            def ffn_dve(dve, f, par, adds):
                dve.wait_ge(F["silu"], f + 1)
                dve.wait_ge(unit_used, up_unit(f) + 1)
                half = GG[:, par, :].rearrange("p (b c) -> p b c", c=HALF)
                dve.tensor_tensor(half, bank_pair(1), half, ALU.mult).then_inc(F["h"], 1)
                if adds:
                    for t in range(2):
                        ffn_add(dve, f - 1, t)
                dve.wait_ge(F["hi"], f + 1)
                if not isinstance(f, int) or f >= 2:
                    dve.wait_ge(unit_used, down_unit(f - 2) + 1)
                dve.tensor_tensor(HS[:, par, 1, :], GG[:, par, :], HS[:, par, 0, :].bitcast(F32),
                                  ALU.subtract).then_inc(F["lo"], 1)
                if adds:
                    for t in range(2, NT):
                        ffn_add(dve, f - 1, t)

            def ffn_add(dve, f, t):
                add_rows(dve, down_unit(f), (NT - 1) * KT + f * (NT - 1), t, 2, 4)

            @block.vector
            def _(dve):
                dve.sem_inc(banks_free, BANKS0)
                dve.sem_inc(rows_added, ADDED0)
                dve.sem_inc(A["ao"], AO0)
                for p in range(2):
                    dve.sem_inc(DS[p]["mixed"], MIXED0)
                dve.wait_ge(ext_in, 16)
                dve.tensor_copy(EXT[0:NHA, 0:4 * P - 1],
                                EXT[0:NHA, 4 * P - 1:4 * P].to_broadcast([NHA, 4 * P - 1])).then_inc(ext_filled, 1)
                dve.wait_ge(small_in, 9 * 16)
                norm_dve(dve, "inp", lambda m: XIN[:, m, :], gain_mix_bc, XN)
                with dve.Fori(0, 6) as i:
                    for slot in range(2):
                        dve.wait_ge(conv_first, i * 2 + (slot + 1))
                        for d in range(1, CONV):
                            y = PROJ[:, ds(i * 2 + (DQ0 + slot), 1), d:T].rearrange("p a c -> p (a c)")
                            if d > 1:
                                dve.wait_ge(conv_tap, i * 4 + (2 * slot + d - 1))
                            dve.scalar_tensor_tensor(
                                out=y, in0=bank_pair(slot, 4).rearrange("p b c -> p (b c)")[:, 0:T - d],
                                scalar=taps[:, ds(i * 2 + slot, 1), CONV - 1 - d], in1=y,
                                op0=ALU.mult, op1=ALU.add).then_inc(conv_tap if d < CONV - 1 else banks_free, 1)
                dve.wait_ge(A["gt_turned"], 1)
                dve.tensor_copy(gates[:, :, :], ps[:, 0, 0:NT * 8].rearrange("p (m c) -> p m c", c=8)).then_inc(G["in"], 1)
                dve.wait_ge(G["in"], 1)
                dve.tensor_tensor(gstep[:, :, :], gates[:, :, NHD:2 * NHD],
                                  dtb_row[:, :].unsqueeze(1).to_broadcast([P, NT, NHD]), ALU.add).then_inc(G["dve"], 1)
                dve.wait_ge(G["act"], 3)
                dve.tensor_scalar(beta[:, :, :], beta[:, :, :], 1.0, None, ALU.add).then_inc(G["dve"], 1)
                dve.wait_ge(G["dve"], 2)
                dve.reciprocal(beta[:, :, :], beta[:, :, :]).then_inc(G["dve"], 1)
                dve.wait_ge(G["act"], 5)
                dve.scalar_tensor_tensor(out=gstep[:, :, :], in0=gstep[:, :, :], scalar=0.0, in1=gtmp[:, :, :],
                                         op0=ALU.max, op1=ALU.add).then_inc(G["dve"], 1)
                dve.wait_ge(G["dve"], 4)
                dve.scalar_tensor_tensor(out=gstep[:, :, :], in0=gstep[:, :, :], scalar=-1.0,
                                         in1=alog_row[:, :].unsqueeze(1).to_broadcast([P, NT, NHD]),
                                         op0=ALU.mult, op1=ALU.mult).then_inc(G["dve"], 1)
                for m in range(NT):
                    dve.wait_ge(A["v_turned"], m + 1)
                    dve.tensor_copy(PROJ[:, V0:V0 + 4, m * P:(m + 1) * P], heads(1 + m % 2)).then_inc(A["v_back"], 1)
                dve.wait_ge(G["cum"], 1)
                dve.tensor_copy(gcum[:, :, :], ps[:, 0, 0:NT * NHD].rearrange("p (m c) -> p m c", c=NHD)
                                ).then_inc(G["dve"], 1)
                dve.wait_ge(G["act"], 6)
                dve.scalar_tensor_tensor(out=nbeg[:, :, :], in0=nbeg[:, :, :], scalar=-1.0, in1=beta[:, :, :],
                                         op0=ALU.mult, op1=ALU.mult).then_inc(G["dve"], 1)
                dve.tensor_scalar(gq_col[:, :], gq_col[:, :], float(DHA) ** -0.5, None, ALU.mult).then_inc(G["dve"], 1)
                dve.wait_ge(G["dve"], 8)
                with dve.Fori(0, NPAIR) as i:
                    for n in range(4):
                        dst, gain = (QB, gq_col) if n < 2 else (KB, gk_col)
                        half = n % 2
                        dve.wait_ge(A["rs"], i * 4 + (n + 1))
                        dve.scalar_tensor_tensor(
                            out=dst[:, half * HALF:(half + 1) * HALF],
                            in0=PROJ[:, ds(i + 4 * (n // 2), 1), half * HALF:(half + 1) * HALF].rearrange("p a c -> p (a c)"),
                            scalar=gain[:, 0:1], in1=RS[:, half, :], op0=ALU.mult, op1=ALU.mult).then_inc(A["qk"], 1)
                    dve.wait_ge(bias_in, i * 16 + 16)
                    dve.memset(BIAS[CHUNK:P, :, 0:CHUNK], NEG).then_inc(A["masked"], 1)
                    dve.memset(BIAS[0:CHUNK, :, KEYS - CHUNK:KEYS], NEG).then_inc(A["masked"], 1)
                    dve.wait_ge(A["masked"], i * 2 + 2)
                    for u in range(NU + 2):
                        if u < NU:
                            qb, s, nt, kb0 = unit_of(u)
                            wait_apart(dve, A["scores"], i * NU + (u + 1), passed_dve)
                            if u >= 2:
                                wait_apart(dve, A["turned"], i * NU + (u - 1), passed_dve)
                            dve.tensor_tensor_reduce(
                                SX[:, u % 2, 0:nt * P],
                                ps[:, 2 * (u % 2):2 * (u % 2) + 2, :].rearrange("p b c -> p (b c)")[:, 0:nt * P],
                                BIAS[:, s, (BAND - nt) * P:KEYS], -1.0, 3.0e38, ALU.add, ALU.min,
                                neg_max[:, u % 2:u % 2 + 1]).then_inc(A["biased"], 1)
                        if u >= 2 and (u - 1) % 2 == 1 and u - 1 < NU:
                            att_pt(dve, i, u - 1)
                        if u >= 2:
                            w = u - 2
                            qb, s, _, _ = unit_of(w)
                            dve.wait_ge(A["prob"], i * NU + (w + 1))
                            dve.reciprocal(row_inv[:, w % 2:w % 2 + 1], row_sum[:, w % 4:w % 4 + 1]).then_inc(A["inv"], 1)
                            dve.wait_ge(A["pv"], i * NU + (w + 1))
                            dve.wait_ge(A["inv"], i * NU + (w + 1))
                            dve.tensor_scalar(AO[:, qb, ds(i * P + s * DHA, DHA)], ps[:, 6 + w % 2, 0:DHA],
                                              row_inv[:, w % 2:w % 2 + 1], None, ALU.mult).then_inc(A["ao"], 1)
                dve.wait_ge(A["rstd2"], 1)
                dve.wait_ge(gain_att_in, 16)
                for m in range(NT):
                    ge(dve, A["turned2"], m - 1)
                    dve.scalar_tensor_tensor(out=AON[:, m % 2, :], in0=AO[:, m, :], scalar=rstd[:, m:m + 1],
                                             in1=gain_att_bc[:, :], op0=ALU.mult, op1=ALU.mult).then_inc(A["aon"], 1)
                dve.wait_ge(A["turned2"], NT)
                dve.memset(STATE[:, :, :], 0.0).then_inc(state_zero, 1)
                with dve.Fori(0, NT // 2) as i:
                    for p in range(2):
                        dn_dve_diag(dve, i, p)
                    for p in range(2):
                        dn_dve_decay(dve, i, p)
                    for p in range(2):
                        dn_dve_kq(dve, i, p)
                    for p in range(2):
                        dn_dve_local(dve, i, p)
                    for p in range(2):
                        dn_dve_scaled(dve, i, p)
                    for lv in range(LEVELS):
                        for p in range(2):
                            dn_dve_p(dve, i, p, lv)
                        for p in range(2):
                            dn_dve_tu(dve, i, p, lv)
                    for p in range(2):
                        dn_dve_b(dve, i, p)
                with dve.Fori(0, KT // 2) as i:
                    for slot in range(2):
                        dve.wait_ge(mix_hi, i * 2 + (slot + 1))
                        dve.tensor_tensor(MS[:, slot, 1, :], MIX[:, ds(i * 2 + slot, 1), :].rearrange("p a c -> p (a c)"),
                                          MS[:, slot, 0, :].bitcast(F32), ALU.subtract).then_inc(mix_lo, 1)
                        for t in range(NT):
                            if slot == 0:
                                dve.wait_ge(x_in[t], 32)
                            add_rows(dve, i * 2 + (U_OUT + slot), i * (2 * (NT - 1)) + slot * (NT - 1), t, 4, 0)
                dve.wait_ge(gain_ffn_in, 16)
                norm_dve(dve, "ffn", lambda m: X2[:, m, :], gain_ffn_bc[:, :], FXN)
                ffn_dve(dve, 0, 0, False)
                with dve.Fori(0, (NF - 2) // 2) as i:
                    ffn_dve(dve, i * 2 + 1, 1, True)
                    ffn_dve(dve, i * 2 + 2, 0, True)
                ffn_dve(dve, NF - 1, 1, True)
                for t in range(NT):
                    ffn_add(dve, NF - 1, t)

            def att_scores(pe, i, u):
                qb, s, nt, kb0 = unit_of(u)
                if u >= 2:
                    pe.wait_ge(A["biased"], i * NU + (u - 1))
                q = QB[s * DHA:(s + 1) * DHA, qb * P:(qb + 1) * P]
                for j0 in range(0, nt, 4):
                    j1 = min(nt, j0 + 4)
                    mm = pe.matmul(ps[:, 2 * (u % 2) + j0 // 4, 0:(j1 - j0) * P], q,
                                   KB[s * DHA:(s + 1) * DHA, (kb0 + j0) * P:(kb0 + j1) * P], start=True, stop=True)
                mm.then_inc(A["scores"], 1)

            def att_turn(pe, i, u):
                nt = unit_of(u)[2]
                pe.wait_ge(A["prob"], i * NU + (u + 1))
                if u >= 1:
                    pe.wait_ge(A["pt"], i * NU + u)
                for j in range(nt):
                    mm = pe.transpose(ps[:, 4 + j // 4, (j % 4) * P:(j % 4 + 1) * P], SX[:, u % 2, j * P:(j + 1) * P],
                                      ident[:, :])
                mm.then_inc(A["turned"], 1)

            def att_pv(pe, i, u):
                qb, s, nt, kb0 = unit_of(u)
                pe.wait_ge(A["pt"], i * NU + (u + 1))
                pe.wait_ge(A["ao"], i * NU + (u + 1))
                for j in range(nt):
                    v = PROJ[:, ds(i + V0, 1), (kb0 + j) * P + s * DHA:(kb0 + j) * P + (s + 1) * DHA]
                    mm = pe.matmul(ps[:, 6 + u % 2, 0:DHA], PT[:, u % 2, j * P:(j + 1) * P],
                                   v.rearrange("p a c -> p (a c)"), start=(j == 0), stop=(j == nt - 1))
                mm.then_inc(A["pv"], 1)

            def per_head(pe, bank, left, right, start=True, stop=True):
                for h in range(NHD):
                    mm = pe.matmul(ps[:, bank, h * P:(h + 1) * P], left(h), right(h), start=start, stop=stop)
                return mm

            def dn_pe_1(pe, i, p):
                S, B = DS[p], DN[p]
                b = 4 * p
                pe.wait_ge(S["mixed"], i + MIXED0)
                pe.wait_ge(S["diag"], 2 * i + 2)
                pe.matmul(ps[:, b + 3, :], ones[:, :], B["dBD"][:, :, :].rearrange("p h c -> p (h c)"),
                          start=True, stop=True)
                pe.matmul(ps[:, b + 2, :], ones[:, :], B["dGD"][:, :, :].rearrange("p h c -> p (h c)"),
                          start=True, stop=True).then_inc(S["rows"], 1)
                pe.wait_ge(S["sq"], i + 1)
                for w in range(2):
                    mm = pe.matmul(ps[:, b + w, :], ones[:, :], B["dSQ"][:, 4 * w:4 * w + 4, :].rearrange("p h c -> p (h c)"),
                                   start=True, stop=True)
                mm.then_inc(S["sums"], 1)

            def dn_pe_2(pe, i, p):
                S, B = DS[p], DN[p]
                b = 4 * p
                pe.wait_ge(S["kq"], 2 * i + 2)
                for h in range(NHD):
                    mm = pe.matmul(ps[:, b + h // 2, (h % 2) * 2 * P:(h % 2 + 1) * 2 * P], B["dKQ"][:, 2 * h, :],
                                   B["dKQ"][:, 2 * h:2 * h + 2, :].rearrange("p w c -> p (w c)"), start=True, stop=True)
                mm.then_inc(S["gram"], 1)

            def dn_pe_3(pe, i, p):
                S, B = DS[p], DN[p]
                b = 4 * p
                pe.wait_ge(S["nl"], i + 1)
                pe.wait_ge(S["vs"], i + 1)
                for h in range(NHD):
                    pe.transpose(ps[:, b + 2, h * P:(h + 1) * P], B["dKQ"][:, 2 * h, :], ident[:, :])
                for h in range(NHD):
                    mm = pe.transpose(ps[:, b + 3, h * P:(h + 1) * P], B["dVS"][:, h, :], ident[:, :])
                mm.then_inc(S["turned"], 1)

            def dn_pe_p(pe, i, p, lv):
                S, B = DS[p], DN[p]
                if lv:
                    pe.wait_ge(S["tu"], i * (2 * LEVELS - 1) + 2 * lv)
                per_head(pe, 4 * p, lambda h: B["dNL"][:, h, :],
                         lambda h: ident[:, :] if lv == 0 else B["dBD"][:, h, :]).then_inc(S["p_mm"], 1)

            def dn_pe_du(pe, i, p, lv):
                S, B = DS[p], DN[p]
                if lv == 0:
                    pe.wait_ge(S["scaled"], 3 * i + 3)
                pe.wait_ge(S["p"], i * LEVELS + (lv + 1))
                if 0 < lv < LEVELS - 1:
                    per_head(pe, 4 * p + 1, lambda h: B["dU"][:, h, :], lambda h: B["dGD"][:, h, :])
                per_head(pe, 4 * p + 2, lambda h: B["dGD"][:, h, :],
                         lambda h: ident[:, :] if lv == 0 else B["dU"][:, h, :]).then_inc(S["du_mm"], 1)

            def dn_pe_wt(pe, i, p):
                S, B = DS[p], DN[p]
                pe.wait_ge(S["tu"], (i + 1) * (2 * LEVELS - 1))
                per_head(pe, 4 * p + 3, lambda h: B["dKB"][:, h, :], lambda h: B["dU"][:, h, :]).then_inc(S["wt_mm"], 1)

            def dn_pe_b(pe, i, p):
                S, B = DS[p], DN[p]
                b = 4 * p
                pe.wait_ge(S["wt"], i + 1)
                if p == 0:
                    pe.wait_ge(state_zero, 1)
                else:
                    pe.wait_ge(DS[0]["st"], 4 * i + 4)
                for h in range(NHD):
                    o = ps[:, b, h * P:(h + 1) * P]
                    pe.matmul(o, B["dU"][:, h, :], B["dVB"][:, h, :], start=True, stop=False)
                    mm = pe.matmul(o, B["dWT"][:, h, :], STATE[:, h, :], start=False, stop=True)
                mm.then_inc(S["new_mm"], 1)
                pe.wait_ge(S["new"], i + 1)
                for h in range(NHD):
                    o = ps[:, b + 1, h * P:(h + 1) * P]
                    pe.matmul(o, STATE[:, h, :], B["dQD"][:, h, :], start=True, stop=False)
                    mm = pe.matmul(o, VNEW[:, h, :], B["dIN"][:, h, :], start=False, stop=True)
                mm.then_inc(S["out_mm"], 1)
                per_head(pe, b + 2, lambda h: B["dKD"][:, h, :], lambda h: VNEW[:, h, :]).then_inc(S["kv_mm"], 1)
                pe.wait_ge(S["osq"], i + 1)
                pe.matmul(ps[:, b + 3, :], ones[:, :], OSQ[:, :, :].rearrange("p h c -> p (h c)"),
                          start=True, stop=True).then_inc(S["osum"], 1)

            def ffn_pe(pe, f, par, slot):
                first = isinstance(f, int) and f == 0
                if not first:
                    pe.wait_ge(F["silu"], f)
                pe.wait_ge(split_done, gate_unit(f) + 1)
                columns_unit(pe, slot, 0).then_inc(unit_used, 1)
                if not first:
                    pe.wait_ge(F["h"], f)
                pe.wait_ge(split_done, up_unit(f) + 1)
                columns_unit(pe, 1 - slot, 2).then_inc(unit_used, 1)
                if not first:
                    down_pe(pe, f - 1, 1 - par, slot)

            def down_pe(pe, f, par, slot):
                pe.wait_ge(F["hi"], f + 1)
                pe.wait_ge(F["lo"], f + 1)
                pe.wait_ge(split_done, down_unit(f) + 1)
                rows_unit(pe, slot, lambda part, t: HS[:, par, part, t * P:(t + 1) * P], f * NT + KT * NT, 2, 4)

            @block.tensor
            def _(pe):
                pe.wait_ge(consts, 1)
                norm_pe(pe, "inp", XN)
                pe.wait_ge(nrm["inp"]["lo"], NT)
                with pe.Fori(0, NPROJ // 2) as i:
                    for slot in range(2):
                        pe.wait_ge(split_done, i * 2 + (slot + 1))
                        pe.wait_ge(banks_free, i * 2 + (slot + 1))
                        columns_unit(pe, slot, 4 + 2 * slot).then_inc(unit_used, 1)
                pe.wait_ge(split_done, U_GATES + 1)
                pe.wait_ge(banks_free, U_GATES + 1)
                columns_unit(pe, 0, 4).then_inc(unit_used, 1)
                pe.wait_ge(A["gt"], 1)
                for m in range(NT):
                    mm = pe.transpose(ps[:, 0, m * 8:(m + 1) * 8], GT[0:8, m * P:(m + 1) * P], ident[0:8, 0:8])
                mm.then_inc(A["gt_turned"], 1)
                for m in range(NT):
                    ge(pe, A["v_back"], m - 1)
                    for t in range(4):
                        mm = pe.transpose(ps[:, 1 + m % 2, t * P:(t + 1) * P], PROJ[:, V0 + t, m * P:(m + 1) * P],
                                          ident[:, :])
                    mm.then_inc(A["v_turned"], 1)
                pe.wait_ge(consts, 2)
                pe.wait_ge(G["dve"], 5)
                pe.matmul(ps[:, 0, 0:NT * NHD], tri[:, :], gstep[:, :, :].rearrange("p m h -> p (m h)"),
                          start=True, stop=True).then_inc(G["cum"], 1)
                pe.wait_ge(A["v_back"], NT)
                pe.wait_ge(banks_free, U_GATES + BANKS0)
                with pe.Fori(0, NPAIR) as i:
                    for n in range(4):
                        pe.wait_ge(A["sq"], i * 4 + (n + 1))
                        if n >= 2:
                            pe.wait_ge(A["ln"], i * 4 + (n - 1))
                        else:
                            pe.wait_ge(A["ao"], i * NU + AO0)
                        pe.matmul(ps[:, 6 + n % 2, :], ones_pair[:, :], SQ[:, n % 2, :], start=True,
                                  stop=True).then_inc(A["sums"], 1)
                    pe.wait_ge(A["qk"], i * 4 + 4)
                    att_scores(pe, i, 0)
                    for u in range(NU):
                        if u + 1 < NU:
                            att_scores(pe, i, u + 1)
                        att_turn(pe, i, u)
                        if u >= 1:
                            att_pv(pe, i, u - 1)
                    att_pv(pe, i, NU - 1)
                for m in range(NT):
                    pe.wait_ge(A["aon"], m + 1)
                    ge(pe, A["mix"], m - 1)
                    for t in range(4):
                        mm = pe.transpose(ps[:, m % 2, t * P:(t + 1) * P], AON[:, m % 2, t * P:(t + 1) * P], ident[:, :])
                    mm.then_inc(A["turned2"], 1)
                pe.wait_ge(A["mix"], NT)
                with pe.Fori(0, NT // 2) as i:
                    for p in range(2):
                        dn_pe_1(pe, i, p)
                    for p in range(2):
                        dn_pe_2(pe, i, p)
                    for p in range(2):
                        dn_pe_3(pe, i, p)
                    for lv in range(LEVELS):
                        for p in range(2):
                            dn_pe_p(pe, i, p, lv)
                        for p in range(2):
                            dn_pe_du(pe, i, p, lv)
                    for p in range(2):
                        dn_pe_wt(pe, i, p)
                    for p in range(2):
                        dn_pe_b(pe, i, p)
                for p in range(2):
                    pe.wait_ge(DS[p]["mixed"], NT // 2 + MIXED0)
                with pe.Fori(0, KT // 2) as i:
                    for slot in range(2):
                        pe.wait_ge(mix_hi, i * 2 + (slot + 1))
                        pe.wait_ge(mix_lo, i * 2 + (slot + 1))
                        pe.wait_ge(split_done, i * 2 + (U_OUT + slot + 1))
                        rows_unit(pe, (U_OUT + slot) % 2, lambda part, t, slot=slot: MS[:, slot, part, t * P:(t + 1) * P],
                                  i * (2 * NT) + slot * NT, 4, 0)
                norm_pe(pe, "ffn", FXN)
                pe.wait_ge(nrm["ffn"]["lo"], NT)
                ffn_pe(pe, 0, 0, U_FFN % 2)
                with pe.Fori(0, (NF - 2) // 2) as i:
                    ffn_pe(pe, i * 2 + 1, 1, 1)
                    ffn_pe(pe, i * 2 + 2, 0, 0)
                ffn_pe(pe, NF - 1, 1, 1)
                down_pe(pe, NF - 1, 1, 0)


def _units(w_in, w_out, w_gate, w_up, w_down):
    def columns(w, j):
        c = w[:, j * P:(j + 1) * P]
        if c.shape[1] < P:
            c = np.concatenate([c, np.zeros((D, P - c.shape[1]), w.dtype)], axis=1)
        return c.reshape(KT, P, P).transpose(1, 0, 2).reshape(P, D)

    def rows(w, j):
        return w[j * P:(j + 1) * P, :]

    order = [columns(w_in, j) for j in range(NPROJ + 1)] + [rows(w_out, j) for j in range(KT)]
    for f in range(NF):
        order += [columns(w_gate, f), columns(w_up, f)]
        if f:
            order.append(rows(w_down, f - 1))
    order.append(rows(w_down, NF - 1))
    return np.ascontiguousarray(np.stack(order))


def kernel(x, norm_mix_g, w_in, attn_q_norm_g, attn_k_norm_g, rel_bias, attn_out_norm_g, conv_w, a_log, dt_bias,
           dn_out_norm_g, w_out, norm_ffn_g, w_gate, w_up, w_down):
    import concourse.bacc as bacc
    from concourse.bass_utils import run_bass_kernel_spmd

    arrays = {
        "x": np.ascontiguousarray(x[0]),
        "units": _units(np.asarray(w_in[0]), np.asarray(w_out[0]), np.asarray(w_gate[0]), np.asarray(w_up[0]),
                        np.asarray(w_down[0])),
        "gain_mix": np.ascontiguousarray(norm_mix_g[0]),
        "gain_q": np.ascontiguousarray(attn_q_norm_g[0].reshape(DHA, 1)),
        "gain_k": np.ascontiguousarray(attn_k_norm_g[0].reshape(DHA, 1)),
        "bias_rev": np.ascontiguousarray(rel_bias[0][::-1].T),
        "gain_att": np.ascontiguousarray(attn_out_norm_g[0]),
        "conv_w": np.ascontiguousarray(np.asarray(conv_w[0]).reshape(CONV, 12, P).transpose(2, 1, 0)),
        "a_log": np.ascontiguousarray(a_log[0]),
        "dt_bias": np.ascontiguousarray(dt_bias[0]),
        "gain_dn": np.ascontiguousarray(dn_out_norm_g[0].reshape(P, 1)),
        "gain_ffn": np.ascontiguousarray(norm_ffn_g[0]),
    }
    nc = bacc.Bacc("TRN2", target_bir_lowering=False, num_devices=1)
    args = {n: nc.dram_tensor(n, a.shape, F32, kind="ExternalInput").ap() for n, a in arrays.items()}
    bias_ext = nc.dram_tensor("bias_ext", (NHA, 6 * P), F32, kind="Internal").ap()
    bias_rows = nc.dram_tensor("bias_rows", (NPAIR, 2, P, KEYS), F32, kind="Internal").ap()
    out = nc.dram_tensor("out", (T, D), F32, kind="ExternalOutput").ap()
    hymba_block(nc, bias_ext=bias_ext, bias_rows=bias_rows, out=out, **args)
    r = run_bass_kernel_spmd(nc, [arrays], core_ids=[0])
    return r.results[0]["out"].reshape(1, T, D)
```

```python
from contextlib import ExitStack

import numpy as np
import concourse.bass as bass
from concourse import mybir

F32 = mybir.dt.float32
F32R = mybir.dt.float32r
ACT = mybir.ActivationFunctionType
ALU = mybir.AluOpType
ds = bass.ds

P = 128
T = 1024
D = 1024
NT = T // P
KT = D // P
HALF = 512
CHUNK = 64
DHA = 64
NHA = 8
NPAIR = NHA // 2
BAND = 5
KEYS = BAND * P
CLIP = 128
NHD = 4
CONV = 4
FFN = 2816
NF = FFN // P
EPS = 1e-6
NEG = -1e30
LEVELS = 7
DOUBLINGS = LEVELS - 1

Q0, K0, V0, DQ0, DK0, DV0, Z0, NPROJ = 0, 4, 8, 12, 16, 20, 24, 28
U_GATES, U_TILE = 0, 1
U_OUT = U_TILE + NPROJ
U_FFN = U_OUT + KT
N_UNITS = U_FFN + 3 * NF
BANKS0 = 2
ADDED0 = 4
AO0 = 2
FREE0 = 1
USED0 = 2


def down_unit(f):
    return U_FFN + 3 * f + 4 if not isinstance(f, int) or f < NF - 1 else N_UNITS - 1


def gate_unit(f):
    return U_FFN + 3 * f - 1 if not isinstance(f, int) or f > 0 else U_FFN


def up_unit(f):
    return U_FFN + 3 * f if not isinstance(f, int) or f > 0 else U_FFN + 1


def ge(eng, sem, value):
    if isinstance(value, int) and value <= 0:
        return
    eng.wait_ge(sem, value)


def at(t, per=1, plus=0):
    i, off = t
    return off * per + plus if i is None else i * (2 * per) + (off * per + plus)


def wait_apart(eng, sem, value, passed):
    if isinstance(value, int):
        ge(eng, sem, value)
    else:
        eng.wait_ge(sem, value)
        eng.sem_inc(passed, 1)


def hymba_block(nc, x, units, gain_mix, gain_q, gain_k, bias_rev, gain_att, conv_w, a_log, dt_bias,
                gain_dn, gain_ffn, bias_ext, bias_rows, out):
    with ExitStack() as ctx:
        def sb(name, shape, dt=F32, stack=ctx):
            return stack.enter_context(nc.sbuf_tensor(name, shape, dt))

        def sem(name):
            return ctx.enter_context(nc.semaphore(name))

        ident = sb("ident", [P, P])
        ones = sb("ones", [P, P])
        ones_pair = sb("ones_pair", [P, P])
        tri = sb("tri", [P, P])
        causal = sb("causal", [P, P])
        level_mask = sb("level_mask", [P, LEVELS, P])
        eps_col = sb("eps_col", [P, 1])
        ssq = sb("ssq", [P, NT])
        rstd = sb("rstd", [P, NT])
        gq_col = sb("gq_col", [P, 1])
        gk_col = sb("gk_col", [P, 1])
        gdn_col = sb("gdn_col", [P, 1])
        taps = sb("taps", [P, 12, CONV])
        alog_row = sb("alog_row", [P, NHD])
        dtb_row = sb("dtb_row", [P, NHD])
        neg_max = sb("neg_max", [P, 2])
        gain_att_col = sb("gain_att_col", [P, 4])
        gates = sb("gates", [P, NT, 8])
        beta = sb("beta", [P, NT, NHD])
        gstep = sb("gstep", [P, NT, NHD])
        gcum = sb("gcum", [P, NT, NHD])
        nbeg = sb("nbeg", [P, NT, NHD])
        gtmp = sb("gtmp", [P, NT, NHD])
        EXL = sb("EXL", [P, 2, NHD])
        RAW = sb("RAW", [P, 2, D])
        SPLIT = sb("SPLIT", [P, 2, 2, D], F32R)

        def overlapped(*layouts):
            got = []
            for layout in layouts:
                with ExitStack() as stack:
                    got.append([sb(n, s, d, stack) for n, s, d in layout])
            return got

        att_layout = [("QB", [P, 2, T], F32), ("KA", [P, 2, T], F32), ("VB", [P, 2, NT, 2, P], F32),
                      ("BIAS", [P, 4, KEYS], F32),
                      ("SX", [P, 2, KEYS], F32), ("PT", [P, 2, KEYS], F32), ("RI", [P, 2, P], F32)]
        dn_two = ["NL", "KB", "VBD", "IN", "QD", "KD", "UT", "TT"]
        dn_one = ["PP", "DG", "DB", "KS", "EX", "DD", "BR", "WT", "VNEW", "OSQ", "ORS", "STATE"]
        dn_layout = [(n, [P, 2, NHD, P], F32) for n in dn_two] + [(n, [P, NHD, P], F32) for n in dn_one]
        with ExitStack() as stack:
            HT = sb("HT", [P, 2, KT, T], F32R, stack)
        (att, dna, mixs) = overlapped(
            att_layout, dn_layout,
            [("MS", [P, 2, 2, T], F32R)])
        ctx.enter_context(nc.sbuf_tensor("region1", [P, 2 * KT * T], F32))
        QB, KA, VB, BIAS, SX, PT, RI = att
        NL, KB, VBD, IN, QD, KD, UT, TT, PP, DG, DB, KS, EX, DD, BR, WT, VNEW, OSQ, ORS, STATE = dna
        MS = mixs[0]
        (proj_l, ffn_l, mix_l) = overlapped(
            [("PROJ", [P, NPROJ, T], F32)],
            [("pad_f", [P, V0, T], F32), ("X2", [P, NT, T], F32), ("gain_ffn_bc", [P, T], F32),
             ("FXN", [P, 2, T], F32), ("FJUNK", [P, T], F32), ("HS", [P, 2, 2, T], F32R), ("GG", [P, 2, T], F32)],
            [("MIX", [P, KT, T], F32)])
        PROJ = proj_l[0]
        _, X2, gain_ffn_bc, FXN, FJUNK, HS, GG = ffn_l
        MIX = mix_l[0]
        ctx.enter_context(nc.sbuf_tensor("region2", [P, NPROJ * T], F32))

        XIN = PROJ[:, 20:28, :]
        gain_mix_bc = PROJ[:, 19, :]
        XN = PROJ[:, 17:19, :]
        JUNK = PROJ[:, 16, :]
        EXT = PROJ[:, 15, :]
        SQ, RS, GT, VT = (PROJ[:, j, :] for j in (26, 27, 24, 25))
        ASQ, ARS = PROJ[:, V0:V0 + 2, :], PROJ[:, V0 + 2, :]

        ps = ctx.enter_context(nc.psum_tensor("ps", [P, 8, HALF], F32))

        small_in = sem("small_in")
        x_in = [sem(f"x_in{m}") for m in range(NT)]
        x_again = sem("x_again")
        ext_in, ext_filled, ext_out = sem("ext_in"), sem("ext_filled"), sem("ext_out")
        gain_ffn_in = sem("gain_ffn_in")
        bias_in = [sem("bias_in0"), sem("bias_in1")]
        out_stored = sem("out_stored")
        passed_pool, passed_act, passed_dve = sem("passed_pool"), sem("passed_act"), sem("passed_dve")
        consts, const_step = sem("consts"), sem("const_step")
        raw_in = [sem("raw_in0"), sem("raw_in1")]
        hi_done, split_done, unit_used = sem("hi_done"), sem("split_done"), sem("unit_used")
        nrm = {w: {n: sem(f"norm_{w}_{n}") for n in
                   ("ssq", "ln", "rstd", "xn", "turned", "hi", "lo")} for w in ("inp", "ffn")}
        conv_first, conv_tap = sem("conv_first"), sem("conv_tap")
        banks_free = sem("banks_free")
        proj_final = sem("proj_final")
        rows_done, rows_added = sem("rows_done"), sem("rows_added")

        def bank_pair(slot, base=0):
            b = base + 2 * slot
            return ps[:, b:b + 2, :]

        def unit_dma(sp, j, slot):
            sp.dma_start(RAW[:, slot, :], units[j, :, :] if isinstance(j, int)
                         else units[ds(j, 1), :, :].rearrange("u p n -> (u p) n")).then_inc(raw_in[slot], 16)

        def unit_split(pool, slot, turn, used, j):
            pool.wait_ge(raw_in[slot], 16 * turn)
            if isinstance(used, int):
                ge(pool, unit_used, used)
            else:
                wait_apart(pool, unit_used, used, passed_pool)
            pool.tensor_copy(SPLIT[:, slot, 0, :], RAW[:, slot, :]).then_inc(hi_done, 1)
            pool.wait_ge(hi_done, j)
            pool.tensor_tensor(SPLIT[:, slot, 1, :], RAW[:, slot, :],
                               SPLIT[:, slot, 0, :].bitcast(F32), ALU.subtract).then_inc(split_done, 1)

        def norm_act_stats(act, w, src, junk, m, n):
            act.activation(junk, src, ACT.Square, accum_out=ssq[:, ds(m, 1)]).then_inc(nrm[w]["ssq"], 1)
            act.wait_ge(nrm[w]["ssq"], n)
            act.activation(rstd[:, ds(m, 1)], ssq[:, ds(m, 1)], ACT.Ln, bias=eps_col[:, :],
                           scale=1.0 / D).then_inc(nrm[w]["ln"], 1)
            act.wait_ge(nrm[w]["ln"], n)
            act.activation(rstd[:, ds(m, 1)], rstd[:, ds(m, 1)], ACT.Exp, scale=-0.5).then_inc(nrm[w]["rstd"], 1)

        def norm_act(act, w, src_of, junk, ready):
            for m in range(NT):
                ready(act, m)
                norm_act_stats(act, w, src_of(m), junk, m, m + 1)
                if m:
                    norm_act_hi(act, w, m - 1)
            norm_act_hi(act, w, NT - 1)

        def norm_act_hi(act, w, m):
            act.wait_ge(nrm[w]["turned"], m + 1)
            act.activation(HT[:, 0, :, m * P:(m + 1) * P],
                           bank_pair(m % 2).rearrange("p b (k c) -> p (b k) c", c=P),
                           ACT.Copy).then_inc(nrm[w]["hi"], 1)

        def norm_dve(dve, w, src_of, gain_bc, xn):
            for m in range(NT + 1):
                if m < NT:
                    dve.wait_ge(nrm[w]["rstd"], m + 1)
                    ge(dve, nrm[w]["turned"], m - 1)
                    dve.scalar_tensor_tensor(out=xn[:, m % 2, :], in0=src_of(m), scalar=rstd[:, m:m + 1],
                                             in1=gain_bc, op0=ALU.mult, op1=ALU.mult).then_inc(nrm[w]["xn"], 1)
                if m:
                    dve.wait_ge(nrm[w]["hi"], m)
                    dve.tensor_tensor(HT[:, 1, :, (m - 1) * P:m * P],
                                      bank_pair((m - 1) % 2).rearrange("p b (k c) -> p (b k) c", c=P),
                                      HT[:, 0, :, (m - 1) * P:m * P].bitcast(F32),
                                      ALU.subtract).then_inc(nrm[w]["lo"], 1)

        def norm_pe(pe, w, xn):
            for m in range(NT):
                pe.wait_ge(nrm[w]["xn"], m + 1)
                ge(pe, nrm[w]["lo"], m - 1)
                for k in range(KT):
                    mm = pe.transpose(ps[:, 2 * (m % 2) + k // 4, (k % 4) * P:(k % 4 + 1) * P],
                                      xn[:, m % 2, k * P:(k + 1) * P], ident[:, :])
                mm.then_inc(nrm[w]["turned"], 1)

        def columns_unit(pe, slot, bank):
            for k in range(KT):
                for part in range(2):
                    w = SPLIT[:, slot, part, k * P:(k + 1) * P]
                    for th in range(2):
                        for other in range(2 - part):
                            mm = pe.matmul(ps[:, bank + th, :], w, HT[:, other, k, th * HALF:(th + 1) * HALF],
                                           start=(k == 0 and part == 0 and other == 0),
                                           stop=(k == KT - 1 and part == 1))
            return mm

        def rows_unit(pe, slot, left, row0, pairs, base):
            for t in range(NT):
                b = base + 2 * (t % pairs)
                pe.wait_ge(rows_added, row0 + (ADDED0 + t + 1 - pairs))
                for part in range(2):
                    w = left(part, t)
                    for dh in range(2):
                        for other in range(2 - part):
                            mm = pe.matmul(ps[:, b + dh, :], w,
                                           SPLIT[:, slot, other, dh * HALF:(dh + 1) * HALF],
                                           start=(part == 0 and other == 0), stop=(part == 1))
                mm.then_inc(rows_done if t < NT - 1 else unit_used, 1)

        def add_rows(dve, unit, done0, t, pairs, base):
            if t < NT - 1:
                dve.wait_ge(rows_done, done0 + (t + 1))
            else:
                dve.wait_ge(unit_used, unit + 1)
            b = base + 2 * (t % pairs)
            row = X2[:, t, :].rearrange("p (b c) -> p b c", c=HALF)
            dve.tensor_tensor(row, ps[:, b:b + 2, :], row, ALU.add).then_inc(rows_added, 1)

        J = {n: sem("side_" + n) for n in ("sq", "mm", "free", "rs", "normed", "q", "v", "q_gain")}
        A = {n: sem("att_" + n) for n in
             ("gt", "gt_turned", "masked", "scores", "biased", "prob", "turned", "pt", "pv", "inv", "ao",
              "sq", "sums", "ln", "rs", "mix")}
        G = {n: sem("gate_" + n) for n in ("in", "act", "dve", "cum")}
        S = {n: sem("dn_" + n) for n in
             ("diag", "ks", "rows", "ex", "br", "exl", "sub", "pre", "dec", "qd", "gram", "in", "db", "nl", "turned",
              "kb", "kd", "vb", "u_masked", "u_first", "u_turned", "t_first", "wt_mm", "wt",
              "new_mm", "new", "out_mm", "kv_mm", "st", "osq", "osum", "oln", "ors", "of", "mixed")}
        C = [{n: sem(f"dn_half{c}_{n}") for n in ("p_mm", "p", "t_mm", "t", "u_mm", "u")} for c in range(2)]
        mix_hi, mix_lo = sem("mix_hi"), sem("mix_lo")
        F = {n: sem("ffn_" + n) for n in ("silu", "h", "hi", "lo")}

        NU = 2 * NT

        def unit_of(w):
            qb, s = w // 2, w % 2
            nt = min(qb + 1, BAND)
            return qb, s, nt, qb + 1 - nt

        def heads(bank):
            return ps[:, bank, :].rearrange("p (h c) -> p h c", c=P)

        def half_heads(bank):
            return ps[:, bank, 0:2 * P].rearrange("p (h c) -> p h c", c=P)

        def over_heads(tile, n=NHD):
            return tile.unsqueeze(1).to_broadcast([P, n, P])

        def over_cols(col):
            return col.unsqueeze(2).to_broadcast([P, NHD, P])

        def tile_cols(t, m):
            return t[:, ds(m, 1), :].rearrange("p a h -> p (a h)")

        def flat(t):
            return t.rearrange("p h c -> p (h c)")

        def proj_tile(j):
            return PROJ[:, ds(j, 1), :].rearrange("p a c -> p (a c)")

        def proj_banks(j):
            return PROJ[:, ds(j, 1), :].rearrange("p a (b c) -> p (a b) c", c=HALF)

        def slot_of(t):
            return (t[1] + U_TILE) % 2

        def tokens(t):
            return ds(at(t) * P, P)

        with nc.Block() as block:

            @block.sync
            def _(sp):
                for m in range(NT):
                    sp.dma_start(XIN[:, m, :], x[m * P:(m + 1) * P, :]).then_inc(x_in[m], 16)
                unit_dma(sp, 0, 0)
                unit_dma(sp, 1, 1)
                with sp.Fori(1, N_UNITS // 2) as i:
                    for slot in range(2):
                        sp.wait_ge(split_done, i * 2 + (slot - 1))
                        unit_dma(sp, i * 2 + slot, slot)
                sp.wait_ge(split_done, N_UNITS - 2)
                unit_dma(sp, N_UNITS - 1, 0)
                for t in range(NT):
                    sp.wait_ge(rows_added, ADDED0 + NT * (KT + NF - 1) + t + 1)
                    sp.dma_start(out[t * P:(t + 1) * P, :], X2[:, t, :]).then_inc(out_stored, 16)
                sp.wait_ge(out_stored, 16 * NT)

            def dn_pool(pool, t):
                p, m = t[1] % 2, at(t)
                ge(pool, S["rows"], m + FREE0)
                pool.tensor_tensor(DG[:, :, :], over_heads(ident[:, :]), over_cols(tile_cols(gcum, m)),
                                   ALU.mult).then_inc(S["diag"], 1)
                pool.tensor_tensor(DB[:, :, :], over_heads(ident[:, :]), over_cols(tile_cols(beta, m)),
                                   ALU.mult).then_inc(S["diag"], 1)
                wait_apart(pool, S["turned"], m + FREE0, passed_pool)
                pool.tensor_copy(KS[:, :, :], PROJ[:, DK0:DK0 + NHD, tokens(t)]).then_inc(S["ks"], 1)
                wait_apart(pool, S["new_mm"], at(t, 1, 1), passed_pool)
                pool.tensor_tensor(VBD[:, p, :, :], PROJ[:, DV0:DV0 + NHD, tokens(t)],
                                   over_cols(tile_cols(beta, m)), ALU.mult).then_inc(S["vb"], 1)
                pool.wait_ge(S["sub"], at(t, 1, 1))
                pool.tensor_tensor(DD[:, :, :], DD[:, :, :], over_heads(causal[:, :]), ALU.add).then_inc(S["pre"], 1)
                wait_apart(pool, S["out_mm"], at(t, 1, 1), passed_pool)
                wait_apart(pool, S["ex"], at(t, 1, 1), passed_pool)
                pool.tensor_tensor(QD[:, p, :, :], PROJ[:, DQ0:DQ0 + NHD, tokens(t)], EX[:, :, :],
                                   ALU.mult).then_inc(S["qd"], 1)
                pool.wait_ge(S["br"], at(t, 1, 1))
                pool.wait_ge(S["dec"], at(t, 1, 1))
                pool.tensor_tensor(BR[:, :, :], DD[:, :, :], BR[:, :, :], ALU.mult).then_inc(S["db"], 1)
                pool.wait_ge(S["nl"], at(t, 1, 1))
                pool.tensor_tensor(UT[:, p, :, :], NL[:, p, :, :], over_heads(level_mask[:, 0, :]),
                                   ALU.mult).then_inc(S["u_masked"], 1)
                pool.wait_ge(S["u_masked"], at(t, 1, 1))
                pool.tensor_tensor(UT[:, p, :, :], UT[:, p, :, :], over_heads(ident[:, :]),
                                   ALU.add).then_inc(S["u_first"], 1)

            @block.gpsimd
            def _(pool):
                pool.memset(ident[:, :], 0.0).then_inc(const_step, 1)
                pool.memset(ones[:, :], 1.0).then_inc(const_step, 1)
                pool.memset(ones_pair[:, :], 1.0).then_inc(const_step, 1)
                pool.memset(tri[:, :], 1.0).then_inc(const_step, 1)
                pool.memset(causal[:, :], 0.0).then_inc(const_step, 1)
                pool.memset(level_mask[:, :, :], 1.0).then_inc(const_step, 1)
                pool.memset(eps_col[:, :], EPS).then_inc(const_step, 1)
                pool.wait_ge(const_step, 7)
                pool.affine_select(out=ident[:, :], in_=ident[:, :], compare_op=ALU.not_equal, fill=1.0, base=0,
                                   pattern=[[-1, P]], channel_multiplier=1).then_inc(consts, 1)
                pair = ones_pair[:, :].rearrange("p (b c) -> p b c", c=DHA)
                pool.affine_select(out=pair, in_=pair, compare_op=ALU.is_ge, fill=0.0, base=0,
                                   pattern=[[-DHA, 2], [0, DHA]], channel_multiplier=1).then_inc(const_step, 1)
                pool.wait_ge(const_step, 8)
                pool.affine_select(out=pair, in_=pair, compare_op=ALU.is_ge, fill=0.0, base=DHA - 1,
                                   pattern=[[DHA, 2], [0, DHA]], channel_multiplier=-1).then_inc(const_step, 1)
                pool.affine_select(out=tri[:, :], in_=tri[:, :], compare_op=ALU.is_ge, fill=0.0, base=0,
                                   pattern=[[1, P]], channel_multiplier=-1).then_inc(const_step, 1)
                pool.affine_select(out=causal[:, :], in_=causal[:, :], compare_op=ALU.is_ge, fill=NEG, base=0,
                                   pattern=[[1, P]], channel_multiplier=-1).then_inc(const_step, 1)
                unit_split(pool, 0, 1, 0, 1)
                unit_split(pool, 1, 1, 0, 2)
                n = 11
                for lv in range(LEVELS):
                    s = 1 << lv
                    first = 0 if lv == 0 else s
                    blocks = level_mask[:, lv, :].rearrange("p (b h r) -> p b h r", h=2, r=s)
                    pool.wait_ge(const_step, n)
                    pool.affine_select(out=blocks, in_=blocks, compare_op=ALU.is_ge, fill=0.0, base=-first,
                                       pattern=[[-2 * s, P // (2 * s)], [0, 2], [0, s]],
                                       channel_multiplier=1).then_inc(const_step, 1)
                    pool.wait_ge(const_step, n + 1)
                    pool.affine_select(out=blocks, in_=blocks, compare_op=ALU.is_ge, fill=0.0, base=first + s - 1,
                                       pattern=[[2 * s, P // (2 * s)], [0, 2], [0, s]],
                                       channel_multiplier=-1).then_inc(const_step, 1)
                    pool.wait_ge(const_step, n + 2)
                    pool.memset(blocks[:, :, 0 if lv == 0 else 1, :], 0.0).then_inc(const_step if lv < LEVELS - 1 else consts, 1)
                    n += 3
                first_late = U_OUT + 1
                with pool.Fori(1, first_late // 2) as i:
                    for slot in range(2):
                        unit_split(pool, slot, i + 1, i * 2 + (slot - 1), i * 2 + (slot + 1))
                pool.wait_ge(unit_used, U_OUT)
                for slot in range(2):
                    pool.memset(VB[:, slot, :, 0, DHA:P], 1.0).then_inc(J["v"], 1)
                    pool.memset(VB[:, slot, :, 1, 0:DHA], 1.0).then_inc(J["v"], 1)
                pool.wait_ge(J["normed"], 8 + FREE0)
                pool.wait_ge(J["free"], DQ0 + FREE0)
                for pair in range(NPAIR):
                    slot = pair % 2
                    ge(pool, A["pv"], (pair - 1) * NU)
                    pool.tensor_copy(QB[:, slot, :], PROJ[:, Q0 + pair, :]).then_inc(J["q"], 1)
                    pool.tensor_copy(KA[:, slot, :], PROJ[:, K0 + pair, :]).then_inc(J["q"], 1)
                    v = PROJ[:, V0 + pair, :].rearrange("p (t s c) -> p t s c", s=2, c=DHA)
                    pool.tensor_copy(VB[:, slot, :, 0, 0:DHA], v[:, :, 0, :]).then_inc(J["v"], 1)
                    pool.tensor_copy(VB[:, slot, :, 1, DHA:P], v[:, :, 1, :]).then_inc(J["v"], 1)
                pool.wait_ge(J["normed"], 16 + FREE0)
                pool.wait_ge(J["free"], Z0 + FREE0)
                pool.wait_ge(A["ao"], NPAIR * NU + AO0)
                with pool.Fori(0, NT // 2) as i:
                    for off in range(2):
                        dn_pool(pool, (i, off))
                with pool.Fori(first_late // 2, N_UNITS // 2) as i:
                    for slot in range(2):
                        unit_split(pool, slot, i + 1, i * 2 + (slot - 1), i * 2 + (slot + 1))
                unit_split(pool, 0, N_UNITS // 2 + 1, N_UNITS - 2, N_UNITS)

            def side_scale(act, t, n, width):
                act.wait_ge(J["mm"], at(t, 1, 1))
                ge(act, J["normed"], at(n, 1, FREE0))
                act.activation(RS.rearrange("p (b c) -> p b c", c=HALF), bank_pair(0), ACT.Ln,
                               bias=eps_col[:, :], scale=1.0 / width).then_inc(J["free"], 1)
                act.wait_ge(J["free"], at(t, 1, 1 + FREE0))
                act.activation(RS, RS, ACT.Exp, scale=-0.5).then_inc(J["rs"], 1)

            def side_square(act, t, done, count):
                wait_apart(act, done, count, passed_act)
                wait_apart(act, J["mm"], at(t), passed_act)
                act.activation(SQ, proj_tile(at(t)), ACT.Square).then_inc(J["sq"], 1)

            def plain_tile(act, t):
                wait_apart(act, unit_used, at(t, 1, U_TILE + 1), passed_act)
                act.activation(proj_banks(at(t)), bank_pair(slot_of(t), 4), ACT.Copy).then_inc(banks_free, 1)

            def conv_tile(act, t, dst, before=None):
                wait_apart(act, unit_used, at(t, 1, U_TILE + 1), passed_act)
                act.activation(proj_banks(at(t)), bank_pair(slot_of(t), 4), ACT.Copy,
                               scale=taps[:, ds(at(t, 1, -DQ0), 1), CONV - 1]).then_inc(conv_first, 1)
                if before is not None:
                    before()
                wait_apart(act, banks_free, at(t, 1, U_TILE + 1 + BANKS0), passed_act)
                act.activation(dst, proj_tile(at(t)), ACT.Silu).then_inc(proj_final, 1)

            def conv_square(act, t):
                side_square(act, t, proj_final, at(t, 1, 1 - DQ0))

            def back(t, by):
                return (t[0], t[1] - by)

            def att_pt(eng, i, u):
                nt = unit_of(u % NU)[2]
                c = i * (2 * NU)
                eng.wait_ge(A["turned"], c + (u + 1))
                if u >= 2:
                    eng.wait_ge(A["pv"], c + (u - 1))
                if u >= 1:
                    eng.wait_ge(A["pt"], c + u)
                src = ps[:, 4:6, :].rearrange("p b c -> p (b c)")[:, 0:nt * P]
                if u % 2 == 0:
                    eng.activation(PT[:, u % 2, 0:nt * P], src, ACT.Copy).then_inc(A["pt"], 1)
                else:
                    eng.tensor_copy(PT[:, u % 2, 0:nt * P], src).then_inc(A["pt"], 1)

            def dn_act_rows(act, t):
                act.wait_ge(S["rows"], at(t, 1, 1 + FREE0))
                ge(act, S["qd"], at(t))
                ge(act, S["exl"], at(t))
                act.activation(EX[:, :, :], heads(4), ACT.Exp).then_inc(S["ex"], 1)
                ge(act, S["nl"], at(t))
                act.activation(BR[:, :, :], heads(5), ACT.Copy).then_inc(S["br"], 1)
                act.wait_ge(S["pre"], at(t, 1, 1))
                act.activation(DD[:, :, :], DD[:, :, :], ACT.Exp).then_inc(S["dec"], 1)

            def dn_act_kd(act, t):
                act.wait_ge(S["ex"], at(t, 1, 1))
                ge(act, S["st"], at(t, 4))
                act.activation(EXL[:, t[1] % 2, :], EX[:, :, P - 1:P].rearrange("p h a -> p (h a)"),
                               ACT.Copy).then_inc(S["exl"], 1)
                act.wait_ge(S["turned"], at(t, 1, 1 + FREE0))
                ge(act, S["kb"], at(t, 1, 1))
                act.wait_ge(S["kv_mm"], at(t, 1, 1))
                for h in range(NHD):
                    act.activation(KD[:, t[1] % 2, h, :], ps[:, 4, h * P:(h + 1) * P], ACT.Copy,
                                   scale=DD[:, h, P - 1:P]).then_inc(S["kd"], 1)

            def dn_act_t(act, t):
                act.wait_ge(S["u_turned"], at(t, 1, 1))
                act.activation(TT[:, t[1] % 2, :, :], heads(5), ACT.Copy).then_inc(S["t_first"], 1)

            def dn_act_wt(act, t):
                ge(act, S["new_mm"], at(t, 1, USED0))
                for c in range(2):
                    act.wait_ge(S["wt_mm"], at(t, 2, c + 1))
                    act.activation(WT[:, 2 * c:2 * c + 2, :], half_heads(2 * c + 1), ACT.Copy).then_inc(S["wt"], 1)

            def dn_act_new(act, t):
                act.wait_ge(S["new_mm"], at(t, 1, 1 + USED0))
                ge(act, S["kv_mm"], at(t, 1, USED0))
                act.activation(VNEW[:, :, :], heads(6), ACT.Copy).then_inc(S["new"], 1)

            def dn_act_out(act, t):
                act.wait_ge(S["out_mm"], at(t, 1, 1 + USED0))
                ge(act, S["osum"], at(t, 1, FREE0))
                act.activation(OSQ[:, :, :], heads(7), ACT.Square).then_inc(S["osq"], 1)
                act.wait_ge(S["osum"], at(t, 1, 1 + FREE0))
                ge(act, S["mixed"], at(t, 1, FREE0))
                act.activation(ORS[:, :, :], heads(6), ACT.Ln, bias=eps_col[:, :],
                               scale=1.0 / P).then_inc(S["oln"], 1)
                act.wait_ge(S["oln"], at(t, 1, 1 + FREE0))
                act.activation(ORS[:, :, :], ORS[:, :, :], ACT.Exp, scale=-0.5).then_inc(S["ors"], 1)

            def dn_act(act, t, before, after):
                if after:
                    dn_act_rows(act, (t[0], t[1] + 1))
                if before:
                    dn_act_new(act, back(t, 1))
                    dn_act_out(act, back(t, 1))
                if after:
                    dn_act_kd(act, (t[0], t[1] + 1))
                    dn_act_t(act, (t[0], t[1] + 1))
                dn_act_wt(act, t)

            def ffn_act(act, f, par):
                act.wait_ge(unit_used, gate_unit(f) + 1)
                act.activation(GG[:, par, :].rearrange("p (b c) -> p b c", c=HALF), bank_pair(0),
                               ACT.Silu).then_inc(F["silu"], 1)
                act.wait_ge(F["h"], f + 1)
                if not isinstance(f, int) or f >= 2:
                    act.wait_ge(unit_used, down_unit(f - 2) + 1)
                act.activation(HS[:, par, 0, :], GG[:, par, :], ACT.Copy).then_inc(F["hi"], 1)

            @block.scalar
            def _(act):
                act.dma_start(gain_mix_bc, gain_mix.partition_broadcast(P)).then_inc(small_in, 16)
                act.dma_start(EXT[0:NHA, 4 * P - 1:4 * P + 2 * CLIP], bias_rev).then_inc(ext_in, 16)
                for half in range(2):
                    act.dma_start(gq_col[half * 64:(half + 1) * 64, :], gain_q).then_inc(small_in, 16)
                    act.dma_start(gk_col[half * 64:(half + 1) * 64, :], gain_k).then_inc(small_in, 16)
                act.dma_start(gdn_col[:, :], gain_dn).then_inc(small_in, 16)
                act.dma_start(gain_att_col[:, :], gain_att).then_inc(small_in, 16)
                act.dma_start(taps[:, :, :], conv_w).then_inc(small_in, 16)
                act.dma_start(alog_row[:, :], a_log.partition_broadcast(P)).then_inc(small_in, 16)
                act.dma_start(dtb_row[:, :], dt_bias.partition_broadcast(P)).then_inc(small_in, 16)
                act.wait_ge(consts, 1)
                norm_act(act, "inp", lambda m: XIN[:, m, :], JUNK, lambda a, m: a.wait_ge(x_in[m], 16))
                act.wait_ge(ext_filled, 1)
                act.dma_start(bias_ext, EXT[0:NHA, 0:6 * P]).then_inc(ext_out, 16)
                act.wait_ge(ext_out, 16)
                act.dma_start(bias_rows.rearrange("a s p c -> (a s) p c"),
                              bass.AP(bias_ext.tensor, P - 1, [[6 * P, NHA], [-1, P], [1, KEYS]])).then_inc(ext_out, 16)
                act.wait_ge(small_in, 10 * 16)
                act.wait_ge(unit_used, U_GATES + 1)
                act.activation(GT[0:8].rearrange("p (b c) -> p b c", c=HALF), bank_pair(0, 4)[0:8],
                               ACT.Copy).then_inc(banks_free, 1)
                plain_tile(act, (None, 0))
                side_square(act, (None, 0), banks_free, U_TILE + 1 + BANKS0)
                act.wait_ge(G["dve"], 1)
                act.activation(gtmp[:, :, :], gstep[:, :, :], ACT.Abs).then_inc(G["act"], 1)
                act.activation(beta[:, :, :], gates[:, :, 0:NHD], ACT.Exp, scale=-1.0).then_inc(G["act"], 1)
                act.activation(alog_row[:, :], alog_row[:, :], ACT.Exp).then_inc(G["act"], 1)
                act.wait_ge(G["act"], 3)
                act.activation(gtmp[:, :, :], gtmp[:, :, :], ACT.Exp, scale=-1.0).then_inc(G["act"], 1)
                act.wait_ge(G["act"], 4)
                act.activation(gtmp[:, :, :], gtmp[:, :, :], ACT.Ln, bias=1.0).then_inc(G["act"], 1)
                def qk_tile(t):
                    plain_tile(act, t)
                    side_scale(act, back(t, 1), back(t, 1), DHA)
                    side_square(act, t, banks_free, at(t, 1, U_TILE + 1 + BANKS0))
                with act.Fori(0, 3) as i:
                    for off in (1, 2):
                        qk_tile((i, off))
                qk_tile((None, V0 - 1))
                for j in range(V0, V0 + 4):
                    act.wait_ge(unit_used, U_TILE + j + 1)
                    act.wait_ge(J["mm"], j)
                    act.activation(VT.rearrange("p (b c) -> p b c", c=HALF), bank_pair(slot_of((None, j)), 4),
                                   ACT.Copy).then_inc(banks_free, 1)
                    if j == V0:
                        side_scale(act, (None, V0 - 1), (None, V0 - 1), DHA)
                act.wait_ge(G["dve"], 6)
                act.activation(nbeg[:, :, :], gcum[:, :, :], ACT.Exp).then_inc(G["act"], 1)
                def dn_qk_tile(t):
                    conv_tile(act, t, proj_tile(at(t)), lambda: side_scale(act, back(t, 1), back(t, 5), 1))
                    conv_square(act, t)
                conv_tile(act, (None, DQ0), proj_tile(DQ0))
                conv_square(act, (None, DQ0))
                with act.Fori(DQ0 // 2, DQ0 // 2 + 3) as i:
                    for off in (1, 2):
                        dn_qk_tile((i, off))
                dn_qk_tile((None, DV0 - 1))
                for j in range(DV0, DV0 + 4):
                    act.wait_ge(unit_used, U_TILE + j + 1)
                    act.activation(proj_banks(j), bank_pair(slot_of((None, j)), 4), ACT.Copy,
                                   scale=taps[:, j - DQ0, CONV - 1:CONV]).then_inc(conv_first, 1)
                    if j == DV0:
                        side_scale(act, (None, DV0 - 1), (None, DV0 - 5), 1)
                    act.wait_ge(banks_free, U_TILE + j + 1 + BANKS0)
                    act.wait_ge(J["mm"], j)
                    act.activation(VT, PROJ[:, j, :], ACT.Silu).then_inc(proj_final, 1)
                with act.Fori(Z0 // 2, NPROJ // 2) as i:
                    for off in range(2):
                        wait_apart(act, unit_used, at((i, off), 1, U_TILE + 1), passed_act)
                        act.activation(proj_banks(at((i, off))), bank_pair(slot_of((i, off)), 4),
                                       ACT.Silu).then_inc(banks_free, 1)
                act.wait_ge(unit_used, U_OUT)
                act.wait_ge(ext_out, 32)
                with act.Fori(0, NPAIR // 2) as i:
                    for slot in range(2):
                        act.dma_start(BIAS[:, 2 * slot:2 * slot + 2, :], bias_rows[ds(i * 2 + slot, 1), :, :, :]
                                      .rearrange("a s p c -> p (a s) c")).then_inc(bias_in[slot], 16)
                    for u in range(2 * NU):
                        nt = unit_of(u % NU)[2]
                        act.wait_ge(A["biased"], i * (2 * NU) + (u + 1))
                        act.activation(SX[:, u % 2, 0:nt * P], SX[:, u % 2, 0:nt * P], ACT.Exp, scale=-1.0,
                                       bias=neg_max[:, u % 2:u % 2 + 1]).then_inc(A["prob"], 1)
                        if u % 2 == 1:
                            att_pt(act, i, u - 1)
                act.wait_ge(A["ao"], NPAIR * NU + AO0)
                def att_square(j):
                    ge(act, A["sums"], j - 1)
                    act.activation(ASQ[:, j % 2, :], PROJ[:, j, :], ACT.Square).then_inc(A["sq"], 1)
                att_square(0)
                att_square(1)
                dn_act_rows(act, (None, 0))
                att_square(2)
                att_square(3)
                act.wait_ge(A["sums"], 4)
                act.activation(ARS.rearrange("p (b c) -> p b c", c=HALF), bank_pair(0), ACT.Ln, bias=eps_col[:, :],
                               scale=1.0 / HALF).then_inc(A["ln"], 1)
                act.wait_ge(A["ln"], 1)
                act.activation(ARS, ARS, ACT.Exp, scale=-0.5).then_inc(A["rs"], 1)
                dn_act_kd(act, (None, 0))
                dn_act_t(act, (None, 0))
                dn_act(act, (None, 0), False, True)
                with act.Fori(0, NT // 2 - 1) as i:
                    for off in (1, 2):
                        dn_act(act, (i, off), True, True)
                act.wait_ge(A["mix"], 4)
                act.wait_ge(S["qd"], NT)
                act.wait_ge(S["gram"], NT)
                act.wait_ge(S["turned"], NT + FREE0)
                for m in range(NT):
                    act.dma_start(X2[:, m, :], x[m * P:(m + 1) * P, :]).then_inc(x_in[m], 16)
                act.dma_start(gain_ffn_bc[:, :], gain_ffn.partition_broadcast(P)).then_inc(gain_ffn_in, 16)
                dn_act(act, (None, NT - 1), True, False)
                dn_act_new(act, (None, NT - 1))
                dn_act_out(act, (None, NT - 1))
                act.wait_ge(S["mixed"], NT + FREE0)
                with act.Fori(0, KT // 2) as i:
                    for slot in range(2):
                        wait_apart(act, unit_used, i * 2 + (U_OUT + slot - 1), passed_act)
                        act.activation(MS[:, slot, 0, :], MIX[:, ds(i * 2 + slot, 1), :].rearrange("p a c -> p (a c)"),
                                       ACT.Copy).then_inc(mix_hi, 1)
                act.wait_ge(unit_used, U_FFN)
                norm_act(act, "ffn", lambda m: X2[:, m, :], FJUNK[:, :],
                         lambda a, m: a.wait_ge(rows_added, ADDED0 + NT * (KT - 1) + m + 1))
                ffn_act(act, 0, 0)
                with act.Fori(0, (NF - 2) // 2) as i:
                    ffn_act(act, i * 2 + 1, 1)
                    ffn_act(act, i * 2 + 2, 0)
                ffn_act(act, NF - 1, 1)

            def side_norm(dve, t, n, scalar):
                dve.wait_ge(J["rs"], at(n, 1, 1))
                dve.scalar_tensor_tensor(out=proj_tile(at(t)), in0=proj_tile(at(t)), scalar=scalar, in1=RS,
                                         op0=ALU.mult, op1=ALU.mult).then_inc(J["normed"], 1)

            def side_back(dve, j):
                dve.wait_ge(J["mm"], j + 1)
                dve.tensor_copy(PROJ[:, j, :].rearrange("p (b c) -> p b c", c=HALF), bank_pair(0)
                                ).then_inc(J["free"], 1)

            def conv_taps(dve, t):
                dve.wait_ge(conv_first, at(t, 1, 1 - DQ0))
                for d in range(1, CONV):
                    y = PROJ[:, ds(at(t), 1), d:T].rearrange("p a c -> p (a c)")
                    if d > 1:
                        dve.wait_ge(conv_tap, at(t, 2, d - 1 - 2 * DQ0))
                    dve.scalar_tensor_tensor(
                        out=y, in0=bank_pair(slot_of(t), 4).rearrange("p b c -> p (b c)")[:, 0:T - d],
                        scalar=taps[:, ds(at(t, 1, -DQ0), 1), CONV - 1 - d], in1=y,
                        op0=ALU.mult, op1=ALU.add).then_inc(conv_tap if d < CONV - 1 else banks_free, 1)

            def dn_dve_sub(dve, t):
                dve.wait_ge(S["ex"], at(t, 1, 1))
                ge(dve, S["kd"], at(t, 4))
                ge(dve, S["in"], at(t))
                dve.tensor_tensor(DD[:, :, :], heads(4), over_cols(tile_cols(gcum, at(t))),
                                  ALU.subtract).then_inc(S["sub"], 1)

            def dn_dve_gram(dve, t):
                p = t[1] % 2
                dve.wait_ge(S["gram"], at(t, 1, 1))
                dve.wait_ge(S["dec"], at(t, 1, 1))
                dve.wait_ge(S["out_mm"], at(t, 1, 1))
                dve.tensor_tensor(IN[:, p, :, :], heads(5), DD[:, :, :], ALU.mult).then_inc(S["in"], 1)
                dve.wait_ge(S["db"], at(t, 1, 1))
                dve.scalar_tensor_tensor(out=NL[:, p, :, :], in0=heads(4), scalar=-1.0, in1=BR[:, :, :],
                                         op0=ALU.mult, op1=ALU.mult).then_inc(S["nl"], 1)

            def dn_dve_kb(dve, t):
                dve.wait_ge(S["turned"], at(t, 1, 1 + FREE0))
                dve.tensor_tensor(KB[:, t[1] % 2, :, :], heads(4), over_cols(tile_cols(nbeg, at(t))),
                                  ALU.mult).then_inc(S["kb"], 1)

            def dn_dve_st(dve, t):
                dve.wait_ge(S["kv_mm"], at(t, 1, 1 + USED0))
                dve.wait_ge(S["exl"], at(t, 1, 1))
                dve.wait_ge(S["st"], at(t, 4, 4))
                for h in range(NHD):
                    dve.scalar_tensor_tensor(out=STATE[:, h, :], in0=STATE[:, h, :],
                                             scalar=EXL[:, t[1] % 2, h:h + 1], in1=ps[:, 6, h * P:(h + 1) * P],
                                             op0=ALU.mult, op1=ALU.add).then_inc(S["st"], 1)

            def dn_dve_out(dve, t):
                dve.wait_ge(S["ors"], at(t, 1, 1))
                dve.scalar_tensor_tensor(out=ORS[:, :, :], in0=heads(7), scalar=gdn_col[:, 0:1],
                                         in1=ORS[:, :, :], op0=ALU.mult, op1=ALU.mult).then_inc(S["of"], 1)
                dve.wait_ge(S["of"], at(t, 1, 1 + FREE0))
                dve.tensor_tensor(MIX[:, 4:8, tokens(t)], ORS[:, :, :], PROJ[:, Z0:Z0 + 4, tokens(t)],
                                  ALU.mult).then_inc(S["mixed"], 1)

            def dn_dve(dve, t, before, after):
                p = t[1] % 2
                nxt = (t[0], t[1] + 1)
                for lv in range(1, LEVELS):
                    for c in range(2):
                        dve.wait_ge(C[c]["p_mm"], at(t, DOUBLINGS, lv))
                        dve.tensor_tensor(PP[:, 2 * c:2 * c + 2, :], half_heads(2 * c),
                                          over_heads(level_mask[:, lv, :], 2), ALU.mult).then_inc(C[c]["p"], 1)
                    if lv == 1 and after:
                        dn_dve_sub(dve, nxt)
                    if lv == 3 and after:
                        dn_dve_gram(dve, nxt)
                    if lv == 4 and after:
                        dn_dve_kb(dve, nxt)
                    if lv == 5 and before:
                        dn_dve_out(dve, back(t, 1))
                    for c in range(2):
                        if lv < LEVELS - 1:
                            tt = TT[:, p, 2 * c:2 * c + 2, :]
                            dve.wait_ge(C[c]["t_mm"], at(t, DOUBLINGS - 1, lv))
                            if lv > 1:
                                dve.wait_ge(C[c]["t"], at(t, DOUBLINGS - 1, lv - 1))
                            dve.tensor_tensor(tt, half_heads(2 * c + 1), tt, ALU.add).then_inc(C[c]["t"], 1)
                        ut = UT[:, p, 2 * c:2 * c + 2, :]
                        dve.wait_ge(C[c]["u_mm"], at(t, DOUBLINGS, lv))
                        if lv > 1:
                            dve.wait_ge(C[c]["u"], at(t, DOUBLINGS, lv - 1))
                        dve.tensor_tensor(ut, half_heads(2 * c), ut, ALU.add).then_inc(C[c]["u"], 1)
                    if lv == 2 and before:
                        dn_dve_st(dve, back(t, 1))

            def ffn_dve(dve, f, par, adds):
                dve.wait_ge(F["silu"], f + 1)
                dve.wait_ge(unit_used, up_unit(f) + 1)
                half = GG[:, par, :].rearrange("p (b c) -> p b c", c=HALF)
                dve.tensor_tensor(half, bank_pair(1), half, ALU.mult).then_inc(F["h"], 1)
                if adds:
                    for t in range(2):
                        ffn_add(dve, f - 1, t)
                dve.wait_ge(F["hi"], f + 1)
                if not isinstance(f, int) or f >= 2:
                    dve.wait_ge(unit_used, down_unit(f - 2) + 1)
                dve.tensor_tensor(HS[:, par, 1, :], GG[:, par, :], HS[:, par, 0, :].bitcast(F32),
                                  ALU.subtract).then_inc(F["lo"], 1)
                if adds:
                    for t in range(2, NT):
                        ffn_add(dve, f - 1, t)

            def ffn_add(dve, f, t):
                add_rows(dve, down_unit(f), (NT - 1) * KT + f * (NT - 1), t, 2, 4)

            @block.vector
            def _(dve):
                dve.sem_inc(banks_free, BANKS0)
                dve.sem_inc(rows_added, ADDED0)
                dve.sem_inc(A["ao"], AO0)
                for used in ("new_mm", "out_mm", "kv_mm"):
                    dve.sem_inc(S[used], USED0)
                for one in (J["free"], J["normed"], *(S[n] for n in ("rows", "turned", "osum", "oln", "of", "mixed"))):
                    dve.sem_inc(one, FREE0)
                dve.wait_ge(ext_in, 16)
                dve.tensor_copy(EXT[0:NHA, 0:4 * P - 1],
                                EXT[0:NHA, 4 * P - 1:4 * P].to_broadcast([NHA, 4 * P - 1])).then_inc(ext_filled, 1)
                dve.wait_ge(small_in, 10 * 16)
                norm_dve(dve, "inp", lambda m: XIN[:, m, :], gain_mix_bc, XN)
                dve.wait_ge(A["gt_turned"], 1)
                dve.tensor_copy(gates[:, :, :], ps[:, 2, 0:NT * 8].rearrange("p (m c) -> p m c", c=8)).then_inc(G["in"], 1)
                dve.wait_ge(G["in"], 1)
                dve.tensor_tensor(gstep[:, :, :], gates[:, :, NHD:2 * NHD],
                                  dtb_row[:, :].unsqueeze(1).to_broadcast([P, NT, NHD]), ALU.add).then_inc(G["dve"], 1)
                dve.wait_ge(G["act"], 3)
                dve.tensor_scalar(beta[:, :, :], beta[:, :, :], 1.0, None, ALU.add).then_inc(G["dve"], 1)
                dve.wait_ge(G["dve"], 2)
                dve.reciprocal(beta[:, :, :], beta[:, :, :]).then_inc(G["dve"], 1)
                dve.wait_ge(G["act"], 5)
                dve.scalar_tensor_tensor(out=gstep[:, :, :], in0=gstep[:, :, :], scalar=0.0, in1=gtmp[:, :, :],
                                         op0=ALU.max, op1=ALU.add).then_inc(G["dve"], 1)
                dve.wait_ge(G["dve"], 4)
                dve.scalar_tensor_tensor(out=gstep[:, :, :], in0=gstep[:, :, :], scalar=-1.0,
                                         in1=alog_row[:, :].unsqueeze(1).to_broadcast([P, NT, NHD]),
                                         op0=ALU.mult, op1=ALU.mult).then_inc(G["dve"], 1)
                dve.tensor_scalar(gq_col[:, :], gq_col[:, :], float(DHA) ** -0.5, None, ALU.mult).then_inc(J["q_gain"], 1)
                dve.wait_ge(J["q_gain"], 1)
                for first, gain in ((Q0, gq_col), (K0, gk_col)):
                    with dve.Fori(first // 2, first // 2 + 2) as i:
                        for off in range(2):
                            side_norm(dve, (i, off), (i, off), gain[:, 0:1])
                for j in range(V0, V0 + 4):
                    side_back(dve, j)
                    if j == V0:
                        dve.wait_ge(G["cum"], 1)
                        dve.tensor_copy(gcum[:, :, :], ps[:, 3, 0:NT * NHD].rearrange("p (m c) -> p m c", c=NHD)
                                        ).then_inc(G["dve"], 1)
                conv_taps(dve, (None, DQ0))
                dve.wait_ge(G["act"], 6)
                dve.scalar_tensor_tensor(out=nbeg[:, :, :], in0=nbeg[:, :, :], scalar=-1.0, in1=beta[:, :, :],
                                         op0=ALU.mult, op1=ALU.mult).then_inc(G["dve"], 1)
                for first, scale in ((DQ0, float(P) ** -0.5), (DK0, 1.0)):
                    with dve.Fori(first // 2, first // 2 + 2) as i:
                        for off in (1, 2):
                            t = (i, off)
                            conv_taps(dve, t)
                            side_norm(dve, back(t, 1), back(t, 5), scale)
                for j in range(DV0, DV0 + 4):
                    if j > DV0:
                        conv_taps(dve, (None, j))
                        side_back(dve, j - 1)
                side_back(dve, DV0 + 3)
                dve.wait_ge(G["dve"], 7)
                with dve.Fori(0, NPAIR // 2) as i:
                    for u in range(2 * NU + 2):
                        c = i * (2 * NU)
                        if u < 2 * NU:
                            slot = u // NU
                            qb, s, nt, kb0 = unit_of(u % NU)
                            if u % NU == 0:
                                dve.wait_ge(bias_in[slot], i * 16 + 16)
                                two = slice(2 * slot, 2 * slot + 2)
                                dve.memset(BIAS[CHUNK:P, two, 0:CHUNK], NEG).then_inc(A["masked"], 1)
                                dve.memset(BIAS[0:CHUNK, two, KEYS - CHUNK:KEYS], NEG).then_inc(A["masked"], 1)
                                dve.wait_ge(A["masked"], i * 4 + (2 * slot + 2))
                            wait_apart(dve, A["scores"], c + (u + 1), passed_dve)
                            if u >= 2:
                                wait_apart(dve, A["turned"], c + (u - 1), passed_dve)
                            dve.tensor_tensor_reduce(
                                SX[:, u % 2, 0:nt * P],
                                ps[:, 2 * (u % 2):2 * (u % 2) + 2, :].rearrange("p b c -> p (b c)")[:, 0:nt * P],
                                BIAS[:, 2 * slot + s, (BAND - nt) * P:KEYS], -1.0, 3.0e38, ALU.add, ALU.min,
                                neg_max[:, u % 2:u % 2 + 1]).then_inc(A["biased"], 1)
                        if u >= 2 and (u - 1) % 2 == 1 and u - 1 < 2 * NU:
                            att_pt(dve, i, u - 1)
                        if u >= 2:
                            w = u - 2
                            qb, s, _, _ = unit_of(w % NU)
                            val, tot = slice(s * DHA, (s + 1) * DHA), slice((1 - s) * DHA, (2 - s) * DHA)
                            dve.wait_ge(A["pv"], c + (w + 1))
                            dve.reciprocal(RI[val, w % 2, :], ps[tot, 6 + w % 2, 0:P]).then_inc(A["inv"], 1)
                            dve.wait_ge(A["inv"], c + (w + 1))
                            o = PROJ[val, ds(i * 2 + w // NU, 1), qb * P:(qb + 1) * P].rearrange("p a c -> p (a c)")
                            dve.tensor_tensor(o, ps[val, 6 + w % 2, 0:P], RI[val, w % 2, :], ALU.mult).then_inc(A["ao"], 1)
                dve.wait_ge(A["ao"], NPAIR * NU + AO0)
                dve.memset(STATE[:, :, :], 0.0).then_inc(S["st"], 4)
                dn_dve_sub(dve, (None, 0))
                dn_dve_gram(dve, (None, 0))
                dn_dve_kb(dve, (None, 0))
                dve.wait_ge(A["rs"], 1)
                for j in range(4):
                    dve.scalar_tensor_tensor(out=MIX[:, j, :], in0=PROJ[:, j, :], scalar=gain_att_col[:, j:j + 1],
                                             in1=ARS, op0=ALU.mult, op1=ALU.mult).then_inc(A["mix"], 1)
                dve.wait_ge(S["t_first"], 1)
                dn_dve(dve, (None, 0), False, True)
                with dve.Fori(0, NT // 2 - 1) as i:
                    for off in (1, 2):
                        dn_dve(dve, (i, off), True, True)
                dn_dve(dve, (None, NT - 1), True, False)
                dn_dve_st(dve, (None, NT - 1))
                dn_dve_out(dve, (None, NT - 1))
                with dve.Fori(0, KT // 2) as i:
                    for slot in range(2):
                        dve.wait_ge(mix_hi, i * 2 + (slot + 1))
                        dve.tensor_tensor(MS[:, slot, 1, :], MIX[:, ds(i * 2 + slot, 1), :].rearrange("p a c -> p (a c)"),
                                          MS[:, slot, 0, :].bitcast(F32), ALU.subtract).then_inc(mix_lo, 1)
                        for t in range(NT):
                            if slot == 0:
                                dve.wait_ge(x_in[t], 32)
                            add_rows(dve, i * 2 + (U_OUT + slot), i * (2 * (NT - 1)) + slot * (NT - 1), t, 4, 0)
                dve.wait_ge(gain_ffn_in, 16)
                norm_dve(dve, "ffn", lambda m: X2[:, m, :], gain_ffn_bc[:, :], FXN)
                ffn_dve(dve, 0, 0, False)
                with dve.Fori(0, (NF - 2) // 2) as i:
                    ffn_dve(dve, i * 2 + 1, 1, True)
                    ffn_dve(dve, i * 2 + 2, 0, True)
                ffn_dve(dve, NF - 1, 1, True)
                for t in range(NT):
                    ffn_add(dve, NF - 1, t)

            def project(pe, t):
                pe.wait_ge(split_done, at(t, 1, U_TILE + 1))
                pe.wait_ge(banks_free, at(t, 1, U_TILE + 1))
                columns_unit(pe, slot_of(t), 4 + 2 * slot_of(t)).then_inc(unit_used, 1)

            def side_sum(pe, t, n, which):
                pe.wait_ge(J["sq"], at(n, 1, 1))
                ge(pe, J["free"], at(t, 1, FREE0))
                for th in range(2):
                    mm = pe.matmul(ps[:, th, :], which[:, :], SQ[:, th * HALF:(th + 1) * HALF], start=True, stop=True)
                mm.then_inc(J["mm"], 1)

            def side_turn(pe, j, ready, count):
                pe.wait_ge(ready, count)
                pe.wait_ge(J["free"], j + FREE0)
                for m in range(NT):
                    mm = pe.transpose(ps[:, m // 4, (m % 4) * P:(m % 4 + 1) * P], VT[:, m * P:(m + 1) * P], ident[:, :])
                mm.then_inc(J["mm"], 1)

            def att_scores(pe, i, u):
                qb, s, nt, kb0 = unit_of(u % NU)
                if u % NU == 0:
                    pe.wait_ge(J["q"], i * 4 + (2 * (u // NU) + 2))
                if u >= 2:
                    pe.wait_ge(A["biased"], i * (2 * NU) + (u - 1))
                q = QB[s * DHA:(s + 1) * DHA, u // NU, qb * P:(qb + 1) * P]
                for j0 in range(0, nt, 4):
                    j1 = min(nt, j0 + 4)
                    mm = pe.matmul(ps[:, 2 * (u % 2) + j0 // 4, 0:(j1 - j0) * P], q,
                                   KA[s * DHA:(s + 1) * DHA, u // NU, (kb0 + j0) * P:(kb0 + j1) * P],
                                   start=True, stop=True)
                mm.then_inc(A["scores"], 1)

            def att_turn(pe, i, u):
                nt = unit_of(u % NU)[2]
                pe.wait_ge(A["prob"], i * (2 * NU) + (u + 1))
                if u >= 1:
                    pe.wait_ge(A["pt"], i * (2 * NU) + u)
                for j in range(nt):
                    mm = pe.transpose(ps[:, 4 + j // 4, (j % 4) * P:(j % 4 + 1) * P], SX[:, u % 2, j * P:(j + 1) * P],
                                      ident[:, :])
                mm.then_inc(A["turned"], 1)

            def att_pv(pe, i, u):
                qb, s, nt, kb0 = unit_of(u % NU)
                if u % NU == 0:
                    pe.wait_ge(J["v"], i * 4 + (2 * (u // NU) + 2 + 4))
                pe.wait_ge(A["pt"], i * (2 * NU) + (u + 1))
                pe.wait_ge(A["ao"], i * (2 * NU) + (u + 1))
                for j in range(nt):
                    mm = pe.matmul(ps[:, 6 + u % 2, 0:P], VB[:, u // NU, kb0 + j, s, :], PT[:, u % 2, j * P:(j + 1) * P],
                                   start=(j == 0), stop=(j == nt - 1))
                mm.then_inc(A["pv"], 1)

            def dn_pe_rows(pe, t):
                ge(pe, S["kb"], at(t))
                ge(pe, S["kd"], at(t, 4))
                ge(pe, S["t_first"], at(t))
                pe.wait_ge(S["diag"], at(t, 2, 2))
                pe.matmul(ps[:, 4, :], ones[:, :], flat(DG[:, :, :]), start=True, stop=True)
                pe.matmul(ps[:, 5, :], ones[:, :], flat(DB[:, :, :]), start=True, stop=True).then_inc(S["rows"], 1)

            def dn_pe_gram(pe, t):
                pe.wait_ge(S["ks"], at(t, 1, 1))
                pe.wait_ge(S["sub"], at(t, 1, 1))
                pe.wait_ge(S["br"], at(t, 1, 1))
                for h in range(NHD):
                    for bank, first in ((4, DK0), (5, DQ0)):
                        mm = pe.matmul(ps[:, bank, h * P:(h + 1) * P], KS[:, h, :], PROJ[:, first + h, tokens(t)],
                                       start=True, stop=True)
                mm.then_inc(S["gram"], 1)

            def dn_pe_turn(pe, t):
                pe.wait_ge(S["nl"], at(t, 1, 1))
                for h in range(NHD):
                    mm = pe.transpose(ps[:, 4, h * P:(h + 1) * P], KS[:, h, :], ident[:, :])
                mm.then_inc(S["turned"], 1)

            def dn_pe_t(pe, t):
                pe.wait_ge(S["u_first"], at(t, 1, 1))
                pe.wait_ge(S["in"], at(t, 1, 1))
                for h in range(NHD):
                    mm = pe.transpose(ps[:, 5, h * P:(h + 1) * P], UT[:, t[1] % 2, h, :], ident[:, :])
                mm.then_inc(S["u_turned"], 1)

            def dn_pe_new(pe, t):
                p = t[1] % 2
                pe.wait_ge(S["wt"], at(t, 2, 2))
                pe.wait_ge(S["vb"], at(t, 1, 1))
                pe.wait_ge(S["st"], at(t, 4, 4))
                ge(pe, S["oln"], at(t, 1, FREE0))
                for h in range(NHD):
                    o = ps[:, 6, h * P:(h + 1) * P]
                    pe.matmul(o, UT[:, p, h, :], VBD[:, p, h, :], start=True, stop=False)
                    mm = pe.matmul(o, WT[:, h, :], STATE[:, h, :], start=False, stop=True)
                mm.then_inc(S["new_mm"], 1)

            def dn_pe_out(pe, t):
                p = t[1] % 2
                pe.wait_ge(S["new"], at(t, 1, 1))
                pe.wait_ge(S["qd"], at(t, 1, 1))
                ge(pe, S["of"], at(t, 1, FREE0))
                for h in range(NHD):
                    o = ps[:, 7, h * P:(h + 1) * P]
                    pe.matmul(o, STATE[:, h, :], QD[:, p, h, :], start=True, stop=False)
                    mm = pe.matmul(o, VNEW[:, h, :], IN[:, p, h, :], start=False, stop=True)
                mm.then_inc(S["out_mm"], 1)

            def dn_pe_kv(pe, t):
                pe.wait_ge(S["kd"], at(t, 4, 4))
                for h in range(NHD):
                    mm = pe.matmul(ps[:, 6, h * P:(h + 1) * P], KD[:, t[1] % 2, h, :], VNEW[:, h, :],
                                   start=True, stop=True)
                mm.then_inc(S["kv_mm"], 1)

            def dn_pe_osum(pe, t):
                pe.wait_ge(S["osq"], at(t, 1, 1))
                pe.wait_ge(S["st"], at(t, 4, 8))
                pe.matmul(ps[:, 6, :], ones[:, :], flat(OSQ[:, :, :]), start=True, stop=True).then_inc(S["osum"], 1)

            def dn_pe(pe, t, before, after):
                p = t[1] % 2
                prev, nxt = (t[0], t[1] - 1), (t[0], t[1] + 1)
                for lv in range(1, LEVELS):
                    for c in range(2):
                        if lv == 1:
                            pe.wait_ge(S["t_first"], at(t, 1, 1))
                            ge(pe, C[c]["u"], at(t, DOUBLINGS))
                        else:
                            pe.wait_ge(C[c]["t"], at(t, DOUBLINGS - 1, lv - 1))
                            pe.wait_ge(C[c]["u"], at(t, DOUBLINGS, lv - 1))
                        for h in range(2):
                            mm = pe.matmul(ps[:, 2 * c, h * P:(h + 1) * P], NL[:, p, 2 * c + h, :],
                                           TT[:, p, 2 * c + h, :], start=True, stop=True)
                        mm.then_inc(C[c]["p_mm"], 1)
                    if lv == 1 and after:
                        dn_pe_rows(pe, nxt)
                    if lv == 2 and before:
                        dn_pe_out(pe, prev)
                    if lv == 3 and after:
                        dn_pe_gram(pe, nxt)
                    if lv == 4 and after:
                        dn_pe_turn(pe, nxt)
                    if lv == 6 and after:
                        dn_pe_t(pe, nxt)
                    for c in range(2):
                        pe.wait_ge(C[c]["p"], at(t, DOUBLINGS, lv))
                        if lv == 1:
                            ge(pe, S["wt"], at(t, 2))
                        if lv < LEVELS - 1:
                            for h in range(2):
                                mm = pe.matmul(ps[:, 2 * c + 1, h * P:(h + 1) * P], UT[:, p, 2 * c + h, :],
                                               PP[:, 2 * c + h, :], start=True, stop=True)
                            mm.then_inc(C[c]["t_mm"], 1)
                        for h in range(2):
                            mm = pe.matmul(ps[:, 2 * c, h * P:(h + 1) * P], PP[:, 2 * c + h, :],
                                           UT[:, p, 2 * c + h, :], start=True, stop=True)
                        mm.then_inc(C[c]["u_mm"], 1)
                    if lv == 1 and before:
                        dn_pe_new(pe, prev)
                    if lv == 2 and before:
                        dn_pe_kv(pe, prev)
                    if lv == 3 and before:
                        dn_pe_osum(pe, prev)
                pe.wait_ge(S["kb"], at(t, 1, 1))
                for c in range(2):
                    pe.wait_ge(C[c]["u"], at(t, DOUBLINGS, DOUBLINGS))
                    for h in range(2):
                        mm = pe.matmul(ps[:, 2 * c + 1, h * P:(h + 1) * P], KB[:, p, 2 * c + h, :],
                                       UT[:, p, 2 * c + h, :], start=True, stop=True)
                    mm.then_inc(S["wt_mm"], 1)

            def ffn_pe(pe, f, par, slot):
                first = isinstance(f, int) and f == 0
                if not first:
                    pe.wait_ge(F["silu"], f)
                pe.wait_ge(split_done, gate_unit(f) + 1)
                columns_unit(pe, slot, 0).then_inc(unit_used, 1)
                if not first:
                    pe.wait_ge(F["h"], f)
                pe.wait_ge(split_done, up_unit(f) + 1)
                columns_unit(pe, 1 - slot, 2).then_inc(unit_used, 1)
                if not first:
                    down_pe(pe, f - 1, 1 - par, slot)

            def down_pe(pe, f, par, slot):
                pe.wait_ge(F["hi"], f + 1)
                pe.wait_ge(F["lo"], f + 1)
                pe.wait_ge(split_done, down_unit(f) + 1)
                rows_unit(pe, slot, lambda part, t: HS[:, par, part, t * P:(t + 1) * P], f * NT + KT * NT, 2, 4)

            @block.tensor
            def _(pe):
                pe.wait_ge(consts, 1)
                norm_pe(pe, "inp", XN)
                pe.wait_ge(nrm["inp"]["lo"], NT)
                pe.wait_ge(split_done, U_GATES + 1)
                columns_unit(pe, 0, 4).then_inc(unit_used, 1)
                project(pe, (None, 0))
                pe.wait_ge(banks_free, U_GATES + 1 + BANKS0)
                for m in range(NT):
                    mm = pe.transpose(ps[:, 2, m * 8:(m + 1) * 8], GT[0:8, m * P:(m + 1) * P], ident[0:8, 0:8])
                mm.then_inc(A["gt_turned"], 1)
                with pe.Fori(0, 4) as i:
                    for off in (1, 2):
                        project(pe, (i, off))
                        side_sum(pe, (i, off - 1), (i, off - 1), ones_pair)
                pe.wait_ge(consts, 2)
                pe.wait_ge(G["dve"], 5)
                pe.matmul(ps[:, 3, 0:NT * NHD], tri[:, :], gstep[:, :, :].rearrange("p m h -> p (m h)"),
                          start=True, stop=True).then_inc(G["cum"], 1)
                for j in range(V0 + 1, V0 + 5):
                    project(pe, (None, j))
                    side_turn(pe, j - 1, banks_free, U_TILE + j + BANKS0)
                with pe.Fori(DQ0 // 2, DQ0 // 2 + 4) as i:
                    for off in (1, 2):
                        project(pe, (i, off))
                        side_sum(pe, (i, off - 1), (i, off - 5), ones)
                for j in range(DV0 + 1, DV0 + 5):
                    project(pe, (None, j))
                    side_turn(pe, j - 1, proj_final, j - DQ0)
                for j in range(Z0 + 1, NPROJ):
                    project(pe, (None, j))
                pe.wait_ge(J["free"], Z0 + FREE0)
                pe.wait_ge(G["dve"], 6)
                pe.wait_ge(J["normed"], 8 + FREE0)
                pe.wait_ge(banks_free, U_OUT + BANKS0)
                with pe.Fori(0, NPAIR // 2) as i:
                    att_scores(pe, i, 0)
                    for u in range(2 * NU):
                        if u + 1 < 2 * NU:
                            att_scores(pe, i, u + 1)
                        att_turn(pe, i, u)
                        if u >= 1:
                            att_pv(pe, i, u - 1)
                    att_pv(pe, i, 2 * NU - 1)
                    pe.wait_ge(A["biased"], i * (2 * NU) + 2 * NU)
                pe.wait_ge(A["pt"], NPAIR * NU)
                pe.wait_ge(A["ao"], NPAIR * NU + AO0)
                dn_pe_rows(pe, (None, 0))
                for j in range(4):
                    pe.wait_ge(A["sq"], j + 1)
                    for th in range(2):
                        mm = pe.matmul(ps[:, th, :], ones[:, :], ASQ[:, j % 2, th * HALF:(th + 1) * HALF],
                                       start=(j == 0), stop=(j == 3))
                    mm.then_inc(A["sums"], 1)
                dn_pe_gram(pe, (None, 0))
                dn_pe_turn(pe, (None, 0))
                dn_pe_t(pe, (None, 0))
                pe.wait_ge(A["ln"], 1)
                dn_pe(pe, (None, 0), False, True)
                with pe.Fori(0, NT // 2 - 1) as i:
                    for off in (1, 2):
                        dn_pe(pe, (i, off), True, True)
                dn_pe(pe, (None, NT - 1), True, False)
                for step in (dn_pe_new, dn_pe_out, dn_pe_kv, dn_pe_osum):
                    step(pe, (None, NT - 1))
                pe.wait_ge(S["mixed"], NT + FREE0)
                with pe.Fori(0, KT // 2) as i:
                    for slot in range(2):
                        pe.wait_ge(mix_hi, i * 2 + (slot + 1))
                        pe.wait_ge(mix_lo, i * 2 + (slot + 1))
                        pe.wait_ge(split_done, i * 2 + (U_OUT + slot + 1))
                        rows_unit(pe, (U_OUT + slot) % 2, lambda part, t, slot=slot: MS[:, slot, part, t * P:(t + 1) * P],
                                  i * (2 * NT) + slot * NT, 4, 0)
                norm_pe(pe, "ffn", FXN)
                pe.wait_ge(nrm["ffn"]["lo"], NT)
                ffn_pe(pe, 0, 0, U_FFN % 2)
                with pe.Fori(0, (NF - 2) // 2) as i:
                    ffn_pe(pe, i * 2 + 1, 1, 1)
                    ffn_pe(pe, i * 2 + 2, 0, 0)
                ffn_pe(pe, NF - 1, 1, 1)
                down_pe(pe, NF - 1, 1, 0)


def _units(w_in, w_out, w_gate, w_up, w_down):
    def columns(w, j):
        c = w[:, j * P:(j + 1) * P]
        if c.shape[1] < P:
            c = np.concatenate([c, np.zeros((D, P - c.shape[1]), w.dtype)], axis=1)
        return c.reshape(KT, P, P).transpose(1, 0, 2).reshape(P, D)

    def rows(w, j):
        return w[j * P:(j + 1) * P, :]

    order = [columns(w_in, j) for j in [NPROJ, *range(NPROJ)]] + [rows(w_out, j) for j in range(KT)]
    for f in range(NF):
        order += [columns(w_gate, f), columns(w_up, f)]
        if f:
            order.append(rows(w_down, f - 1))
    order.append(rows(w_down, NF - 1))
    return np.ascontiguousarray(np.stack(order))


def kernel(x, norm_mix_g, w_in, attn_q_norm_g, attn_k_norm_g, rel_bias, attn_out_norm_g, conv_w, a_log, dt_bias,
           dn_out_norm_g, w_out, norm_ffn_g, w_gate, w_up, w_down):
    import concourse.bacc as bacc
    from concourse.bass_utils import run_bass_kernel_spmd

    arrays = {
        "x": np.ascontiguousarray(x[0]),
        "units": _units(np.asarray(w_in[0]), np.asarray(w_out[0]), np.asarray(w_gate[0]), np.asarray(w_up[0]),
                        np.asarray(w_down[0])),
        "gain_mix": np.ascontiguousarray(norm_mix_g[0]),
        "gain_q": np.ascontiguousarray(attn_q_norm_g[0].reshape(DHA, 1)),
        "gain_k": np.ascontiguousarray(attn_k_norm_g[0].reshape(DHA, 1)),
        "bias_rev": np.ascontiguousarray(rel_bias[0][::-1].T),
        "gain_att": np.ascontiguousarray(attn_out_norm_g[0].reshape(4, P).T),
        "conv_w": np.ascontiguousarray(np.asarray(conv_w[0]).reshape(CONV, 12, P).transpose(2, 1, 0)),
        "a_log": np.ascontiguousarray(a_log[0]),
        "dt_bias": np.ascontiguousarray(dt_bias[0]),
        "gain_dn": np.ascontiguousarray(dn_out_norm_g[0].reshape(P, 1)),
        "gain_ffn": np.ascontiguousarray(norm_ffn_g[0]),
    }
    nc = bacc.Bacc("TRN2", target_bir_lowering=False, num_devices=1)
    args = {n: nc.dram_tensor(n, a.shape, F32, kind="ExternalInput").ap() for n, a in arrays.items()}
    bias_ext = nc.dram_tensor("bias_ext", (NHA, 6 * P), F32, kind="Internal").ap()
    bias_rows = nc.dram_tensor("bias_rows", (NPAIR, 2, P, KEYS), F32, kind="Internal").ap()
    out = nc.dram_tensor("out", (T, D), F32, kind="ExternalOutput").ap()
    hymba_block(nc, bias_ext=bias_ext, bias_rows=bias_rows, out=out, **args)
    r = run_bass_kernel_spmd(nc, [arrays], core_ids=[0])
    return r.results[0]["out"].reshape(1, T, D)
```

```python
from contextlib import ExitStack

import numpy as np
import concourse.bass as bass
from concourse import mybir

F32 = mybir.dt.float32
F32R = mybir.dt.float32r
ACT = mybir.ActivationFunctionType
ALU = mybir.AluOpType
ds = bass.ds

P = 128
T = 1024
D = 1024
NT = T // P
KT = D // P
HALF = 512
CHUNK = 64
DHA = 64
NHA = 8
NPAIR = NHA // 2
BAND = 5
KEYS = BAND * P
CLIP = 128
TILE_ORDER = (0, 7, 1, 6, 2, 5, 3, 4)
NHD = 4
CONV = 4
FFN = 2816
NF = FFN // P
EPS = 1e-6
NEG = -1e30
LEVELS = 7
DOUBLINGS = LEVELS - 1

Q0, K0, V0, DQ0, DK0, DV0, Z0, NPROJ = 0, 4, 8, 12, 16, 20, 24, 28
U_GATES, U_TILE = 0, 1
U_OUT = U_TILE + NPROJ
U_FFN = U_OUT + KT
N_UNITS = U_FFN + 3 * NF
BANKS0 = 2
AO0 = 2
FREE0 = 1
USED0 = 2


def down_unit(f):
    return U_FFN + 3 * f + 4 if not isinstance(f, int) or f < NF - 1 else N_UNITS - 1


def gate_unit(f):
    return U_FFN + 3 * f - 1 if not isinstance(f, int) or f > 0 else U_FFN


def up_unit(f):
    return U_FFN + 3 * f if not isinstance(f, int) or f > 0 else U_FFN + 1


def ge(eng, sem, value):
    if isinstance(value, int) and value <= 0:
        return
    eng.wait_ge(sem, value)


def at(t, per=1, plus=0):
    i, off = t
    return off * per + plus if i is None else i * (2 * per) + (off * per + plus)


def wait_apart(eng, sem, value, passed):
    if isinstance(value, int):
        ge(eng, sem, value)
    else:
        eng.wait_ge(sem, value)
        eng.sem_inc(passed, 1)


def hymba_block(nc, x, units, gain_mix, gain_q, gain_k, bias_rev, gain_att, conv_w, a_log, dt_bias,
                gain_dn, gain_ffn, bias_ext, bias_rows, out):
    with ExitStack() as ctx:
        def sb(name, shape, dt=F32, stack=ctx):
            return stack.enter_context(nc.sbuf_tensor(name, shape, dt))

        def sem(name):
            return ctx.enter_context(nc.semaphore(name))

        ident = sb("ident", [P, P])
        ones_r = sb("ones_r", [P, P], F32R)
        ones_pair_r = sb("ones_pair_r", [P, P], F32R)
        tri = sb("tri", [P, P])
        causal = sb("causal", [P, P])
        level_mask = sb("level_mask", [P, LEVELS, P])
        eps_col = sb("eps_col", [P, 1])
        ssq = sb("ssq", [P, NT])
        rstd = sb("rstd", [P, NT])
        gq_col = sb("gq_col", [P, 1])
        gk_col = sb("gk_col", [P, 1])
        gdn_col = sb("gdn_col", [P, 1])
        taps = sb("taps", [P, 12, CONV])
        alog_row = sb("alog_row", [P, NHD])
        dtb_row = sb("dtb_row", [P, NHD])
        neg_max = sb("neg_max", [P, 4])
        row_sum = sb("row_sum", [P, 4])
        row_inv = sb("row_inv", [P, 4])
        gain_att_col = sb("gain_att_col", [P, 4])
        gates = sb("gates", [P, NT, 8])
        beta = sb("beta", [P, NT, NHD])
        gstep = sb("gstep", [P, NT, NHD])
        gcum = sb("gcum", [P, NT, NHD])
        nbeg = sb("nbeg", [P, NT, NHD])
        gparts = sb("gparts", [P, 2, NT, NHD], F32R)
        bparts = sb("bparts", [P, 2, NT, NHD], F32R)
        EXL = sb("EXL", [P, 2, NHD])
        RAW = sb("RAW", [P, 2, D])
        SPLIT = sb("SPLIT", [P, 2, 2, D], F32R)

        def overlapped(*layouts):
            got = []
            for layout in layouts:
                with ExitStack() as stack:
                    got.append([sb(n, s, d, stack) for n, s, d in layout])
            return got

        att_layout = [("pad_att", [P, 5, NHD, P], F32),
                      ("QB", [P, 2, T], F32), ("KA", [P, 2, T], F32), ("VB", [P, 2, T], F32),
                      ("BIAS", [P, 4, KEYS], F32),
                      ("SX", [P, 4, KEYS], F32), ("PT", [P, 2, KEYS], F32)]
        dn_two = ["NL", "KB", "VBD", "IN", "QD", "KD", "UT", "TT"]
        dn_one = ["KS", "EX", "DD", "BR", "PP", "WT", "VNEW", "OSQ", "ORS", "STATE"]
        dn_layout = ([(n, [P, 2, NHD, P], F32R) for n in ("DG", "DB")] + [(n, [P, NHD, P], F32) for n in dn_one]
                     + [(n, [P, 2, NHD, P], F32) for n in dn_two])
        with ExitStack() as stack:
            HT = sb("HT", [P, 2, KT, T], F32R, stack)
        (att, dna, outs, ffn1) = overlapped(
            att_layout, dn_layout,
            [("WO", [P, KT - 2, 2, D], F32R)],
            [("HS", [P, 2, 2, T], F32R), ("GG", [P, 2, T], F32)])
        ctx.enter_context(nc.sbuf_tensor("region1", [P, 2 * KT * T], F32))
        _, QB, KA, VB, BIAS, SX, PT = att
        DG, DB, KS, EX, DD, BR, PP, WT, VNEW, OSQ, ORS, STATE, NL, KB, VBD, IN, QD, KD, UT, TT = dna
        WO = outs[0]
        HS, GG = ffn1
        (proj_l, late_l, mix_l, sq_l) = overlapped(
            [("PROJ", [P, NPROJ, T], F32)],
            [("LO", [P, KT, T], F32R), ("X2", [P, NT, T], F32), ("HI", [P, KT, T], F32R), ("gain_ffn_bc", [P, T], F32),
             ("FXN", [P, 2, T], F32), ("FJUNK", [P, T], F32)],
            [("MIX", [P, KT, T], F32)],
            [("pad_sq", [P, DV0 + 2, T], F32), ("SQS", [P, 2, T], F32R)])
        PROJ = proj_l[0]
        LO, X2, HI, gain_ffn_bc, FXN, FJUNK = late_l
        MIX = mix_l[0]
        SQS = sq_l[1]
        ctx.enter_context(nc.sbuf_tensor("region2", [P, NPROJ * T], F32))

        XIN = PROJ[:, 20:28, :]
        gain_mix_bc = PROJ[:, 19, :]
        XN = PROJ[:, 17:19, :]
        JUNK = PROJ[:, 16, :]
        EXT = PROJ[:, 15, :]
        ones, ones_pair = PROJ[:, 14, 0:P], PROJ[:, 14, P:2 * P]
        gtmp = PROJ[:, 14, 2 * P:2 * P + NT * NHD].rearrange("p (m h) -> p m h", h=NHD)
        SQ, RS, GT, VT = (PROJ[:, j, :] for j in (26, 27, 24, 25))
        ASQ, ARS = PROJ[:, V0:V0 + 2, :], PROJ[:, V0 + 2, :]

        ps = ctx.enter_context(nc.psum_tensor("ps", [P, 8, HALF], F32))

        small_in, gain_mix_in = sem("small_in"), sem("gain_mix_in")
        x_in = [sem(f"x_in{m}") for m in range(NT)]
        x_again = sem("x_again")
        ext_in, ext_filled, ext_out = sem("ext_in"), sem("ext_filled"), sem("ext_out")
        gain_ffn_in = sem("gain_ffn_in")
        bias_in = [sem("bias_in0"), sem("bias_in1")]
        out_stored = sem("out_stored")
        passed_pool, passed_act, passed_dve = sem("passed_pool"), sem("passed_act"), sem("passed_dve")
        consts, const_step = sem("consts"), sem("const_step")
        raw_in = [sem("raw_in0"), sem("raw_in1")]
        hi_done, split_done, unit_used = sem("hi_done"), sem("split_done"), sem("unit_used")
        nrm = {w: {n: sem(f"norm_{w}_{n}") for n in
                   ("ssq", "root", "rstd", "xn", "turned", "hi", "lo")} for w in ("inp", "ffn")}
        conv_first, conv_tap = sem("conv_first"), sem("conv_tap")
        banks_free = sem("banks_free")
        proj_final = sem("proj_final")
        rows_done, rows_added = sem("rows_done"), sem("rows_added")

        def bank_pair(slot, base=0):
            b = base + 2 * slot
            return ps[:, b:b + 2, :]

        def unit_dma(sp, j, slot):
            sp.dma_start(RAW[:, slot, :], units[j, :, :] if isinstance(j, int)
                         else units[ds(j, 1), :, :].rearrange("u p n -> (u p) n")).then_inc(raw_in[slot], 16)

        def unit_split(pool, slot, turn, used, j, dst=None):
            dst = SPLIT[:, slot, :, :] if dst is None else dst
            pool.wait_ge(raw_in[slot], 16 * turn)
            wait_apart(pool, unit_used, used, passed_pool)
            pool.tensor_copy(dst[:, 0, :], RAW[:, slot, :]).then_inc(hi_done, 1)
            pool.wait_ge(hi_done, j)
            pool.tensor_tensor(dst[:, 1, :], RAW[:, slot, :], dst[:, 0, :].bitcast(F32),
                               ALU.subtract).then_inc(split_done, 1)

        def norm_stats(act, w, src, junk, m):
            act.activation(junk, src, ACT.Square, accum_out=ssq[:, m:m + 1]).then_inc(nrm[w]["ssq"], 1)
            act.wait_ge(nrm[w]["ssq"], m + 1)
            act.activation(ssq[:, m:m + 1], ssq[:, m:m + 1], ACT.Sqrt, bias=eps_col[:, :],
                           scale=1.0 / D).then_inc(nrm[w]["root"], 1)

        def norm_hi(act, w, m, parts, base):
            act.wait_ge(nrm[w]["turned"], m + 1)
            act.activation(parts[0][:, :, m * P:(m + 1) * P],
                           bank_pair(m % 2, base).rearrange("p b (k c) -> p (b k) c", c=P),
                           ACT.Copy).then_inc(nrm[w]["hi"], 1)

        def norm_scale(dve, w, src, gain_bc, xn, m):
            dve.wait_ge(nrm[w]["root"], m + 1)
            dve.reciprocal(rstd[:, m:m + 1], ssq[:, m:m + 1]).then_inc(nrm[w]["rstd"], 1)
            dve.wait_ge(nrm[w]["rstd"], m + 1)
            ge(dve, nrm[w]["turned"], m - 1)
            dve.scalar_tensor_tensor(out=xn[:, m % 2, :], in0=src, scalar=rstd[:, m:m + 1],
                                     in1=gain_bc, op0=ALU.mult, op1=ALU.mult).then_inc(nrm[w]["xn"], 1)

        def norm_lo(dve, w, m, parts, base):
            dve.wait_ge(nrm[w]["hi"], m + 1)
            cols = slice(m * P, (m + 1) * P)
            dve.tensor_tensor(parts[1][:, :, cols], bank_pair(m % 2, base).rearrange("p b (k c) -> p (b k) c", c=P),
                              parts[0][:, :, cols].bitcast(F32), ALU.subtract).then_inc(nrm[w]["lo"], 1)

        def norm_turn(pe, w, xn, m, base):
            pe.wait_ge(nrm[w]["xn"], m + 1)
            ge(pe, nrm[w]["lo"], m - 1)
            for k in range(KT):
                mm = pe.transpose(ps[:, base + 2 * (m % 2) + k // 4, (k % 4) * P:(k % 4 + 1) * P],
                                  xn[:, m % 2, k * P:(k + 1) * P], ident[:, :])
            mm.then_inc(nrm[w]["turned"], 1)

        def columns_unit(pe, slot, bank, right, first=0, end=T):
            width = min(HALF, end - first)
            for k in range(KT):
                for part in range(2):
                    w = SPLIT[:, slot, part, k * P:(k + 1) * P]
                    for a in range(first, end, width):
                        for other in range(2 - part):
                            mm = pe.matmul(ps[:, bank + a // HALF, a % HALF:a % HALF + width], w,
                                           right[other][:, k, a:a + width],
                                           start=(k == 0 and part == 0 and other == 0),
                                           stop=(k == KT - 1 and part == 1))
            return mm

        def row_products(pe, bank, left, unit, first=True, last=True):
            for part in range(2):
                for dh in range(2):
                    for other in range(2 - part):
                        mm = pe.matmul(ps[:, bank + dh, :], left(part), unit[:, other, dh * HALF:(dh + 1) * HALF],
                                       start=(first and part == 0 and other == 0), stop=(last and part == 1))
            return mm

        def add_rows(dve, t, bank):
            row = X2[:, t, :].rearrange("p (b c) -> p b c", c=HALF)
            dve.tensor_tensor(row, ps[:, bank:bank + 2, :], row, ALU.add).then_inc(rows_added, 1)


        J = {n: sem("side_" + n) for n in ("sq", "split", "mm", "free", "rs", "normed", "q", "v", "q_gain", "ones")}
        A = {n: sem("att_" + n) for n in
             ("gt", "gt_turned", "masked", "scores", "biased", "prob", "turned", "pt", "pv", "inv", "scaled", "ao",
              "sq", "sums", "ln", "rs", "mix")}
        G = {n: sem("gate_" + n) for n in ("in", "act", "dve", "cum")}
        S = {n: sem("dn_" + n) for n in
             ("diag", "ks", "rows", "ex", "br", "exl", "sub", "pre", "dec", "qd", "gram", "in", "db", "nl", "turned",
              "kb", "kd", "vb", "u_masked", "u_first", "u_turned", "t_first", "wt_mm", "wt",
              "new_mm", "new", "out_mm", "kv_mm", "st", "osq", "osum", "oln", "ors", "of", "mixed")}
        C = [{n: sem(f"dn_half{c}_{n}") for n in ("p_mm", "p", "t_mm", "t", "u_mm", "u")} for c in range(2)]
        mix_hi, mix_lo = sem("mix_hi"), sem("mix_lo")
        F = {n: sem("ffn_" + n) for n in ("silu", "h", "hi", "lo")}

        NU = 2 * NT

        def unit_of(w):
            qb, s = TILE_ORDER[w // 2], w % 2
            nt = min(qb + 1, BAND)
            return qb, s, nt, qb + 1 - nt

        def heads(bank):
            return ps[:, bank, :].rearrange("p (h c) -> p h c", c=P)

        def half_heads(bank):
            return ps[:, bank, 0:2 * P].rearrange("p (h c) -> p h c", c=P)

        def over_heads(tile, n=NHD):
            return tile.unsqueeze(1).to_broadcast([P, n, P])

        def over_cols(col):
            return col.unsqueeze(2).to_broadcast([P, NHD, P])

        def tile_cols(t, m):
            return t[:, ds(m, 1), :].rearrange("p a h -> p (a h)")

        def flat(t):
            return t.rearrange("p h c -> p (h c)")

        def proj_tile(j):
            return PROJ[:, ds(j, 1), :].rearrange("p a c -> p (a c)")

        def proj_banks(j):
            return PROJ[:, ds(j, 1), :].rearrange("p a (b c) -> p (a b) c", c=HALF)

        def out_bank(t):
            return 2 * t if t < 4 else 2 * (t % 2)

        def down_bank(t):
            return (4, 6, 0)[t % 3]

        HTP = (HT[:, 0, :, :], HT[:, 1, :, :])

        FFN_NORM_ACT = [("stats", 0), ("stats", 1), ("stats", 2), ("stats", 3), ("hi", 0), ("hi", 1), ("stats", 4),
                        ("hi", 2), ("hi", 3), ("stats", 5), ("hi", 4), ("hi", 5), ("stats", 6), ("stats", 7),
                        ("hi", 6), ("hi", 7)]
        FFN_NORM_DVE = [("add", 0), ("add", 1), ("add", 2), ("add", 3), ("scale", 0), ("scale", 1), ("add", 4),
                        ("lo", 0), ("scale", 2), ("lo", 1), ("scale", 3), ("add", 5), ("lo", 2), ("scale", 4),
                        ("lo", 3), ("scale", 5), ("add", 6), ("lo", 4), ("scale", 6), ("lo", 5), ("add", 7), ("scale", 7),
                        ("lo", 6), ("lo", 7)]
        FFN_NORM_PE = {4: (0, 1), 5: (2, 3), 6: (4, 5), 7: (6,)}

        def slot_of(t):
            return (t[1] + U_TILE) % 2

        def tokens(t):
            return ds(at(t) * P, P)

        with nc.Block() as block:

            @block.sync
            def _(sp):
                for m in range(NT):
                    sp.dma_start(XIN[:, m, :], x[m * P:(m + 1) * P, :]).then_inc(x_in[m], 16)
                    if m == 1:
                        unit_dma(sp, 0, 0)
                    if m == 3:
                        unit_dma(sp, 1, 1)
                for half in range(2):
                    sp.dma_start(gq_col[half * 64:(half + 1) * 64, :], gain_q).then_inc(small_in, 16)
                    sp.dma_start(gk_col[half * 64:(half + 1) * 64, :], gain_k).then_inc(small_in, 16)
                sp.dma_start(gdn_col[:, :], gain_dn).then_inc(small_in, 16)
                sp.dma_start(gain_att_col[:, :], gain_att).then_inc(small_in, 16)
                sp.dma_start(taps[:, :, :], conv_w).then_inc(small_in, 16)
                sp.dma_start(alog_row[:, :], a_log.partition_broadcast(P)).then_inc(small_in, 16)
                sp.dma_start(dtb_row[:, :], dt_bias.partition_broadcast(P)).then_inc(small_in, 16)
                with sp.Fori(1, (U_OUT + 3) // 2) as i:
                    for slot in range(2):
                        sp.wait_ge(split_done, i * 2 + (slot - 1))
                        unit_dma(sp, i * 2 + slot, slot)
                sp.wait_ge(A["mix"], 4)
                for m in range(4):
                    sp.dma_start(X2[:, m, :], x[m * P:(m + 1) * P, :]).then_inc(x_in[m], 16)
                sp.wait_ge(S["qd"], NT)
                sp.wait_ge(S["gram"], NT)
                for m in range(4, NT):
                    sp.dma_start(X2[:, m, :], x[m * P:(m + 1) * P, :]).then_inc(x_in[m], 16)
                with sp.Fori((U_OUT + 3) // 2, N_UNITS // 2) as i:
                    for slot in range(2):
                        sp.wait_ge(split_done, i * 2 + (slot - 1))
                        unit_dma(sp, i * 2 + slot, slot)
                sp.wait_ge(split_done, N_UNITS - 2)
                unit_dma(sp, N_UNITS - 1, 0)
                for t in range(NT):
                    sp.wait_ge(rows_added, NT * NF + t + 1)
                    sp.dma_start(out[t * P:(t + 1) * P, :], X2[:, t, :]).then_inc(out_stored, 16)
                sp.wait_ge(out_stored, 16 * NT)

            def dn_pool(pool, t):
                p, m = t[1] % 2, at(t)
                ge(pool, S["rows"], m + FREE0)
                for diag, parts in ((DG, gparts), (DB, bparts)):
                    for part in range(2):
                        pool.tensor_tensor(diag[:, part, :, :], over_heads(ident[:, :]),
                                           over_cols(tile_cols(parts[:, part, :, :].bitcast(F32), m)),
                                           ALU.mult).then_inc(S["diag"], 1)
                wait_apart(pool, S["turned"], m + FREE0, passed_pool)
                pool.tensor_copy(KS[:, :, :], PROJ[:, DK0:DK0 + NHD, tokens(t)]).then_inc(S["ks"], 1)
                pool.wait_ge(A["ao"], NPAIR * NT + AO0)
                pool.wait_ge(S["sub"], at(t, 1, 1))
                pool.tensor_tensor(DD[:, :, :], DD[:, :, :], over_heads(causal[:, :]), ALU.add).then_inc(S["pre"], 1)
                pool.wait_ge(S["br"], at(t, 1, 1))
                pool.wait_ge(S["dec"], at(t, 1, 1))
                pool.tensor_tensor(BR[:, :, :], DD[:, :, :], BR[:, :, :], ALU.mult).then_inc(S["db"], 1)
                wait_apart(pool, S["new_mm"], at(t, 1, 1), passed_pool)
                pool.tensor_tensor(VBD[:, p, :, :], PROJ[:, DV0:DV0 + NHD, tokens(t)],
                                   over_cols(tile_cols(beta, m)), ALU.mult).then_inc(S["vb"], 1)
                pool.wait_ge(S["nl"], at(t, 1, 1))
                pool.tensor_tensor(UT[:, p, :, :], NL[:, p, :, :], over_heads(level_mask[:, 0, :]),
                                   ALU.mult).then_inc(S["u_masked"], 1)
                pool.wait_ge(S["u_masked"], at(t, 1, 1))
                pool.tensor_tensor(UT[:, p, :, :], UT[:, p, :, :], over_heads(ident[:, :]),
                                   ALU.add).then_inc(S["u_first"], 1)
                wait_apart(pool, S["out_mm"], at(t, 1, 1), passed_pool)
                wait_apart(pool, S["ex"], at(t, 1, 1), passed_pool)
                pool.tensor_tensor(QD[:, p, :, :], PROJ[:, DQ0:DQ0 + NHD, tokens(t)], EX[:, :, :],
                                   ALU.mult).then_inc(S["qd"], 1)

            @block.gpsimd
            def _(pool):
                pool.memset(ident[:, :], 0.0).then_inc(const_step, 1)
                pool.memset(ones[:, :], 1.0).then_inc(const_step, 1)
                pool.memset(ones_pair[:, :], 1.0).then_inc(const_step, 1)
                pool.memset(tri[:, :], 1.0).then_inc(const_step, 1)
                pool.memset(causal[:, :], 0.0).then_inc(const_step, 1)
                pool.memset(level_mask[:, :, :], 1.0).then_inc(const_step, 1)
                pool.memset(eps_col[:, :], EPS).then_inc(const_step, 1)
                pool.wait_ge(const_step, 7)
                pool.affine_select(out=ident[:, :], in_=ident[:, :], compare_op=ALU.not_equal, fill=1.0, base=0,
                                   pattern=[[-1, P]], channel_multiplier=1).then_inc(consts, 1)
                pair = ones_pair[:, :].rearrange("p (b c) -> p b c", c=DHA)
                pool.affine_select(out=pair, in_=pair, compare_op=ALU.is_ge, fill=0.0, base=0,
                                   pattern=[[-DHA, 2], [0, DHA]], channel_multiplier=1).then_inc(const_step, 1)
                pool.wait_ge(const_step, 8)
                pool.affine_select(out=pair, in_=pair, compare_op=ALU.is_ge, fill=0.0, base=DHA - 1,
                                   pattern=[[DHA, 2], [0, DHA]], channel_multiplier=-1).then_inc(const_step, 1)
                pool.affine_select(out=tri[:, :], in_=tri[:, :], compare_op=ALU.is_ge, fill=0.0, base=0,
                                   pattern=[[1, P]], channel_multiplier=-1).then_inc(const_step, 1)
                pool.affine_select(out=causal[:, :], in_=causal[:, :], compare_op=ALU.is_ge, fill=NEG, base=0,
                                   pattern=[[1, P]], channel_multiplier=-1).then_inc(const_step, 1)
                unit_split(pool, 0, 1, 0, 1)
                unit_split(pool, 1, 1, 0, 2)
                n = 11
                for lv in range(LEVELS):
                    s = 1 << lv
                    first = 0 if lv == 0 else s
                    blocks = level_mask[:, lv, :].rearrange("p (b h r) -> p b h r", h=2, r=s)
                    pool.wait_ge(const_step, n)
                    pool.affine_select(out=blocks, in_=blocks, compare_op=ALU.is_ge, fill=0.0, base=-first,
                                       pattern=[[-2 * s, P // (2 * s)], [0, 2], [0, s]],
                                       channel_multiplier=1).then_inc(const_step, 1)
                    pool.wait_ge(const_step, n + 1)
                    pool.affine_select(out=blocks, in_=blocks, compare_op=ALU.is_ge, fill=0.0, base=first + s - 1,
                                       pattern=[[2 * s, P // (2 * s)], [0, 2], [0, s]],
                                       channel_multiplier=-1).then_inc(const_step, 1)
                    pool.wait_ge(const_step, n + 2)
                    pool.memset(blocks[:, :, 0 if lv == 0 else 1, :], 0.0).then_inc(const_step if lv < LEVELS - 1 else consts, 1)
                    n += 3
                first_late = U_OUT + 1
                with pool.Fori(1, first_late // 2) as i:
                    for slot in range(2):
                        unit_split(pool, slot, i + 1, i * 2 + (slot - 1), i * 2 + (slot + 1))
                pool.wait_ge(unit_used, U_OUT)
                pool.wait_ge(J["free"], DQ0 + FREE0)
                for pair in range(NPAIR):
                    ge(pool, A["pv"], (pair - 1) * NU)
                    pool.tensor_copy(VB[:, pair % 2, :], PROJ[:, V0 + pair, :]).then_inc(J["v"], 1)
                unit_split(pool, 0, first_late // 2 + 1, U_OUT, first_late + 1)
                pool.wait_ge(J["normed"], 16 + FREE0)
                pool.wait_ge(J["free"], Z0 + FREE0)
                with pool.Fori(0, NT // 2) as i:
                    for off in range(2):
                        dn_pool(pool, (i, off))
                for k in range(2, KT):
                    if k == 2:
                        pool.wait_ge(S["rows"], NT + FREE0)
                    if k == 3:
                        pool.wait_ge(S["kd"], NHD * NT)
                        pool.wait_ge(S["exl"], NT)
                        pool.wait_ge(S["nl"], NT)
                    if k == 4:
                        pool.wait_ge(S["mixed"], NT + FREE0)
                    j = U_OUT + k
                    unit_split(pool, j % 2, j // 2 + 1, 0, j + 1, WO[:, k - 2, :, :])
                for j in range(U_FFN, U_FFN + 3):
                    unit_split(pool, j % 2, j // 2 + 1, j - KT + 1 if j < U_FFN + 2 else j - 1, j + 1)
                with pool.Fori((U_FFN + 3) // 2, N_UNITS // 2) as i:
                    for slot in range(2):
                        unit_split(pool, slot, i + 1, i * 2 + (slot - 1), i * 2 + (slot + 1))
                unit_split(pool, 0, N_UNITS // 2 + 1, N_UNITS - 2, N_UNITS)

            def side_scale(act, t, n, width):
                act.wait_ge(J["mm"], at(t, 1, 1))
                ge(act, J["normed"], at(n, 1, FREE0))
                act.activation(RS.rearrange("p (b c) -> p b c", c=HALF), bank_pair(0), ACT.Ln,
                               bias=eps_col[:, :], scale=1.0 / width).then_inc(J["free"], 1)
                act.wait_ge(J["free"], at(t, 1, 1 + FREE0))
                act.activation(RS, RS, ACT.Exp, scale=-0.5).then_inc(J["rs"], 1)

            def side_square(act, t, n, done, count):
                wait_apart(act, done, count, passed_act)
                wait_apart(act, J["split"], at(n, 2, FREE0), passed_act)
                act.activation(SQ, proj_tile(at(t)), ACT.Square).then_inc(J["sq"], 1)

            def plain_tile(act, t):
                wait_apart(act, unit_used, at(t, 1, U_TILE + 1), passed_act)
                act.activation(proj_banks(at(t)), bank_pair(slot_of(t), 4), ACT.Copy).then_inc(banks_free, 1)

            def conv_tile(act, t, dst, before=None):
                wait_apart(act, unit_used, at(t, 1, U_TILE + 1), passed_act)
                act.activation(proj_banks(at(t)), bank_pair(slot_of(t), 4), ACT.Copy,
                               scale=taps[:, ds(at(t, 1, -DQ0), 1), CONV - 1]).then_inc(conv_first, 1)
                if before is not None:
                    before()
                wait_apart(act, banks_free, at(t, 1, U_TILE + 1 + BANKS0), passed_act)
                act.activation(dst, proj_tile(at(t)), ACT.Silu).then_inc(proj_final, 1)

            def conv_square(act, t):
                side_square(act, t, back(t, 4), proj_final, at(t, 1, 1 - DQ0))

            def back(t, by):
                return (t[0], t[1] - by)

            def att_pt(dve, i, u):
                nt = unit_of(u % NU)[2]
                c = i * (2 * NU)
                dve.wait_ge(A["turned"], c + (u + 1))
                if u >= 2:
                    dve.wait_ge(A["pv"], c + (u - 1))
                dve.tensor_copy(PT[:, u % 2, 0:nt * P], ps[:, 4:6, :].rearrange("p b c -> p (b c)")[:, 0:nt * P]
                                ).then_inc(A["pt"], 1)

            def dn_act_rows(act, t):
                act.wait_ge(S["rows"], at(t, 1, 1 + FREE0))
                ge(act, S["qd"], at(t))
                ge(act, S["exl"], at(t))
                act.activation(EX[:, :, :], heads(4), ACT.Exp).then_inc(S["ex"], 1)
                ge(act, S["nl"], at(t))
                act.activation(BR[:, :, :], heads(5), ACT.Copy).then_inc(S["br"], 1)
                act.wait_ge(S["pre"], at(t, 1, 1))
                act.activation(DD[:, :, :], DD[:, :, :], ACT.Exp).then_inc(S["dec"], 1)

            def dn_act_kd(act, t):
                act.wait_ge(S["ex"], at(t, 1, 1))
                ge(act, S["st"], at(t, 4))
                act.activation(EXL[:, t[1] % 2, :], EX[:, :, P - 1:P].rearrange("p h a -> p (h a)"),
                               ACT.Copy).then_inc(S["exl"], 1)
                act.wait_ge(S["turned"], at(t, 1, 1 + FREE0))
                ge(act, S["kb"], at(t, 1, 1))
                act.wait_ge(S["kv_mm"], at(t, 1, 1))
                for h in range(NHD):
                    act.activation(KD[:, t[1] % 2, h, :], ps[:, 4, h * P:(h + 1) * P], ACT.Copy,
                                   scale=DD[:, h, P - 1:P]).then_inc(S["kd"], 1)

            def dn_act_t(act, t):
                act.wait_ge(S["u_turned"], at(t, 1, 1))
                act.activation(TT[:, t[1] % 2, :, :], heads(5), ACT.Copy).then_inc(S["t_first"], 1)

            def dn_act_wt(act, t):
                ge(act, S["new_mm"], at(t, 1, USED0))
                for c in range(2):
                    act.wait_ge(S["wt_mm"], at(t, 2, c + 1))
                    act.activation(WT[:, 2 * c:2 * c + 2, :], half_heads(2 * c + 1), ACT.Copy).then_inc(S["wt"], 1)

            def dn_act_new(act, t):
                act.wait_ge(S["new_mm"], at(t, 1, 1 + USED0))
                ge(act, S["kv_mm"], at(t, 1, USED0))
                act.activation(VNEW[:, :, :], heads(6), ACT.Copy).then_inc(S["new"], 1)

            def dn_act_out(act, t):
                act.wait_ge(S["out_mm"], at(t, 1, 1 + USED0))
                ge(act, S["osum"], at(t, 1, FREE0))
                act.activation(OSQ[:, :, :], heads(7), ACT.Square).then_inc(S["osq"], 1)
                act.wait_ge(S["osum"], at(t, 1, 1 + FREE0))
                ge(act, S["mixed"], at(t, 1, FREE0))
                act.activation(ORS[:, :, :], heads(6), ACT.Ln, bias=eps_col[:, :],
                               scale=1.0 / P).then_inc(S["oln"], 1)
                act.wait_ge(S["oln"], at(t, 1, 1 + FREE0))
                act.activation(ORS[:, :, :], ORS[:, :, :], ACT.Exp, scale=-0.5).then_inc(S["ors"], 1)

            def dn_act(act, t, before, after):
                if after:
                    dn_act_rows(act, (t[0], t[1] + 1))
                if before:
                    dn_act_new(act, back(t, 1))
                    dn_act_out(act, back(t, 1))
                if after:
                    dn_act_kd(act, (t[0], t[1] + 1))
                    dn_act_t(act, (t[0], t[1] + 1))
                dn_act_wt(act, t)

            def ffn_act(act, f, par):
                act.wait_ge(unit_used, gate_unit(f) + 1)
                act.activation(GG[:, par, :].rearrange("p (b c) -> p b c", c=HALF), bank_pair(0),
                               ACT.Silu).then_inc(F["silu"], 1)
                act.wait_ge(F["h"], f + 1)
                if not isinstance(f, int) or f >= 2:
                    act.wait_ge(unit_used, down_unit(f - 2) + 1)
                act.activation(HS[:, par, 0, :], GG[:, par, :], ACT.Copy).then_inc(F["hi"], 1)

            @block.scalar
            def _(act):
                act.dma_start(gain_mix_bc, gain_mix.partition_broadcast(P)).then_inc(gain_mix_in, 16)
                act.dma_start(EXT[0:NHA, 4 * P - 1:4 * P + 2 * CLIP], bias_rev).then_inc(ext_in, 16)
                act.wait_ge(consts, 1)
                for m in range(NT):
                    act.wait_ge(x_in[m], 16)
                    norm_stats(act, "inp", XIN[:, m, :], JUNK, m)
                    if m:
                        norm_hi(act, "inp", m - 1, (HT[:, 0, :, :], HT[:, 1, :, :]), 0)
                norm_hi(act, "inp", NT - 1, (HT[:, 0, :, :], HT[:, 1, :, :]), 0)
                act.wait_ge(ext_filled, 1)
                act.dma_start(bias_ext, EXT[0:NHA, 0:6 * P]).then_inc(ext_out, 16)
                act.wait_ge(ext_out, 16)
                act.dma_start(bias_rows.rearrange("a s p c -> (a s) p c"),
                              bass.AP(bias_ext.tensor, P - 1, [[6 * P, NHA], [-1, P], [1, KEYS]])).then_inc(ext_out, 16)
                act.wait_ge(small_in, 9 * 16)
                act.wait_ge(unit_used, U_GATES + 1)
                act.activation(GT[0:8].rearrange("p (b c) -> p b c", c=HALF), bank_pair(0, 4)[0:8],
                               ACT.Copy).then_inc(banks_free, 1)
                plain_tile(act, (None, 0))
                side_square(act, (None, 0), (None, 0), banks_free, U_TILE + 1 + BANKS0)
                act.wait_ge(G["dve"], 1)
                act.activation(gtmp[:, :, :], gstep[:, :, :], ACT.Abs).then_inc(G["act"], 1)
                act.activation(beta[:, :, :], gates[:, :, 0:NHD], ACT.Exp, scale=-1.0).then_inc(G["act"], 1)
                act.activation(alog_row[:, :], alog_row[:, :], ACT.Exp).then_inc(G["act"], 1)
                act.wait_ge(G["act"], 3)
                act.activation(gtmp[:, :, :], gtmp[:, :, :], ACT.Exp, scale=-1.0).then_inc(G["act"], 1)
                act.wait_ge(G["act"], 4)
                act.activation(gtmp[:, :, :], gtmp[:, :, :], ACT.Ln, bias=1.0).then_inc(G["act"], 1)
                def qk_tile(t):
                    plain_tile(act, t)
                    side_scale(act, back(t, 1), back(t, 1), DHA)
                    side_square(act, t, t, banks_free, at(t, 1, U_TILE + 1 + BANKS0))
                with act.Fori(0, 3) as i:
                    for off in (1, 2):
                        qk_tile((i, off))
                qk_tile((None, V0 - 1))
                for j in range(V0, V0 + 4):
                    act.wait_ge(unit_used, U_TILE + j + 1)
                    act.wait_ge(J["mm"], j)
                    act.activation(VT.rearrange("p (b c) -> p b c", c=HALF), bank_pair(slot_of((None, j)), 4),
                                   ACT.Copy).then_inc(banks_free, 1)
                    if j == V0:
                        side_scale(act, (None, V0 - 1), (None, V0 - 1), DHA)
                act.wait_ge(G["dve"], 6)
                act.activation(nbeg[:, :, :], gcum[:, :, :], ACT.Exp).then_inc(G["act"], 1)
                def dn_qk_tile(t):
                    conv_tile(act, t, proj_tile(at(t)), lambda: side_scale(act, back(t, 1), back(t, 5), 1))
                    conv_square(act, t)
                conv_tile(act, (None, DQ0), proj_tile(DQ0))
                conv_square(act, (None, DQ0))
                with act.Fori(DQ0 // 2, DQ0 // 2 + 3) as i:
                    for off in (1, 2):
                        dn_qk_tile((i, off))
                dn_qk_tile((None, DV0 - 1))
                for j in range(DV0, DV0 + 4):
                    act.wait_ge(unit_used, U_TILE + j + 1)
                    act.activation(proj_banks(j), bank_pair(slot_of((None, j)), 4), ACT.Copy,
                                   scale=taps[:, j - DQ0, CONV - 1:CONV]).then_inc(conv_first, 1)
                    if j == DV0:
                        side_scale(act, (None, DV0 - 1), (None, DV0 - 5), 1)
                    act.wait_ge(banks_free, U_TILE + j + 1 + BANKS0)
                    act.wait_ge(J["mm"], j)
                    act.activation(VT, PROJ[:, j, :], ACT.Silu).then_inc(proj_final, 1)
                with act.Fori(Z0 // 2, NPROJ // 2) as i:
                    for off in range(2):
                        wait_apart(act, unit_used, at((i, off), 1, U_TILE + 1), passed_act)
                        act.activation(proj_banks(at((i, off))), bank_pair(slot_of((i, off)), 4),
                                       ACT.Silu).then_inc(banks_free, 1)
                act.wait_ge(unit_used, U_OUT)
                act.wait_ge(J["normed"], V0 + FREE0)
                act.wait_ge(ext_out, 32)
                with act.Fori(0, NPAIR // 2) as i:
                    for slot in range(2):
                        act.dma_start(BIAS[:, 2 * slot:2 * slot + 2, :], bias_rows[ds(i * 2 + slot, 1), :, :, :]
                                      .rearrange("a s p c -> p (a s) c")).then_inc(bias_in[slot], 16)
                    for u in range(2 * NU + 1):
                        if 1 <= u <= 2 * NU:
                            w = u - 1
                            act.wait_ge(A["inv"], i * (2 * NU) + (w + 1))
                            sx = SX[:, w % 4, 0:unit_of(w % NU)[2] * P]
                            act.activation(sx, sx, ACT.Copy, scale=row_inv[:, w % 4:w % 4 + 1]).then_inc(A["scaled"], 1)
                        if u < 2 * NU:
                            nt = unit_of(u % NU)[2]
                            sx = SX[:, u % 4, 0:nt * P]
                            act.wait_ge(A["biased"], i * (2 * NU) + (u + 1))
                            act.activation(sx, sx, ACT.Exp, scale=-1.0, bias=neg_max[:, u % 4:u % 4 + 1],
                                           accum_out=row_sum[:, u % 4:u % 4 + 1]).then_inc(A["prob"], 1)
                        if u == 3:
                            act.activation(QB[:, 1, :], proj_tile(i * 2 + (Q0 + 1)), ACT.Copy).then_inc(J["q"], 1)
                        if u == 5:
                            act.activation(KA[:, 1, :], proj_tile(i * 2 + (K0 + 1)), ACT.Copy).then_inc(J["q"], 1)
                act.wait_ge(A["ao"], NPAIR * NT + AO0)
                def att_square(j):
                    ge(act, A["sums"], j - 1)
                    act.activation(ASQ[:, j % 2, :], PROJ[:, j, :], ACT.Square).then_inc(A["sq"], 1)
                dn_act_rows(act, (None, 0))
                att_square(0)
                att_square(1)
                dn_act_kd(act, (None, 0))
                dn_act_t(act, (None, 0))
                dn_act_rows(act, (None, 1))
                att_square(2)
                att_square(3)
                dn_act_kd(act, (None, 1))
                dn_act_t(act, (None, 1))
                dn_act_wt(act, (None, 0))
                act.wait_ge(A["sums"], 4)
                act.activation(ARS.rearrange("p (b c) -> p b c", c=HALF), bank_pair(0, 6), ACT.Ln, bias=eps_col[:, :],
                               scale=1.0 / HALF).then_inc(A["ln"], 1)
                act.wait_ge(A["ln"], 1)
                act.activation(ARS, ARS, ACT.Exp, scale=-0.5).then_inc(A["rs"], 1)
                with act.Fori(0, NT // 2 - 1) as i:
                    for off in (1, 2):
                        dn_act(act, (i, off), True, True)
                act.wait_ge(A["mix"], 4)
                act.wait_ge(S["ks"], NT)
                act.wait_ge(S["gram"], NT)
                for k in range(4):
                    act.activation(HI[:, k, :], MIX[:, k, :], ACT.Copy).then_inc(mix_hi, 1)
                dn_act(act, (None, NT - 1), True, False)
                dn_act_new(act, (None, NT - 1))
                dn_act_out(act, (None, NT - 1))
                act.wait_ge(S["mixed"], NT + FREE0)
                act.dma_start(gain_ffn_bc[:, :], gain_ffn.partition_broadcast(P)).then_inc(gain_ffn_in, 16)
                act.wait_ge(S["vb"], NT)
                for k in range(4, KT):
                    act.activation(HI[:, k, :], MIX[:, k, :], ACT.Copy).then_inc(mix_hi, 1)
                for step, m in FFN_NORM_ACT:
                    if step == "stats":
                        act.wait_ge(rows_added, m + 1)
                        norm_stats(act, "ffn", X2[:, m, :], FJUNK[:, :], m)
                    else:
                        norm_hi(act, "ffn", m, (HI, LO), 4)
                ffn_act(act, 0, 0)
                with act.Fori(0, (NF - 2) // 2) as i:
                    ffn_act(act, i * 2 + 1, 1)
                    ffn_act(act, i * 2 + 2, 0)
                ffn_act(act, NF - 1, 1)

            def side_split(dve, t, n):
                dve.wait_ge(J["sq"], at(n, 1, 1))
                ge(dve, J["mm"], at(t))
                dve.tensor_copy(SQS[:, 0, :], SQ).then_inc(J["split"], 1)
                dve.wait_ge(J["split"], at(n, 2, 1 + FREE0))
                dve.tensor_tensor(SQS[:, 1, :], SQ, SQS[:, 0, :].bitcast(F32), ALU.subtract).then_inc(J["split"], 1)

            def side_norm(dve, t, n, scalar):
                dve.wait_ge(J["rs"], at(n, 1, 1))
                dve.scalar_tensor_tensor(out=proj_tile(at(t)), in0=proj_tile(at(t)), scalar=scalar, in1=RS,
                                         op0=ALU.mult, op1=ALU.mult).then_inc(J["normed"], 1)

            def side_back(dve, j):
                dve.wait_ge(J["mm"], j + 1)
                dve.tensor_copy(PROJ[:, j, :].rearrange("p (b c) -> p b c", c=HALF), bank_pair(0)
                                ).then_inc(J["free"], 1)

            def conv_taps(dve, t):
                dve.wait_ge(conv_first, at(t, 1, 1 - DQ0))
                for d in range(1, CONV):
                    y = PROJ[:, ds(at(t), 1), d:T].rearrange("p a c -> p (a c)")
                    if d > 1:
                        dve.wait_ge(conv_tap, at(t, 2, d - 1 - 2 * DQ0))
                    dve.scalar_tensor_tensor(
                        out=y, in0=bank_pair(slot_of(t), 4).rearrange("p b c -> p (b c)")[:, 0:T - d],
                        scalar=taps[:, ds(at(t, 1, -DQ0), 1), CONV - 1 - d], in1=y,
                        op0=ALU.mult, op1=ALU.add).then_inc(conv_tap if d < CONV - 1 else banks_free, 1)

            def dn_dve_sub(dve, t):
                dve.wait_ge(S["ex"], at(t, 1, 1))
                ge(dve, S["kd"], at(t, 4))
                ge(dve, S["in"], at(t))
                dve.tensor_tensor(DD[:, :, :], heads(4), over_cols(tile_cols(gcum, at(t))),
                                  ALU.subtract).then_inc(S["sub"], 1)

            def dn_dve_gram(dve, t):
                p = t[1] % 2
                dve.wait_ge(S["gram"], at(t, 1, 1))
                dve.wait_ge(S["dec"], at(t, 1, 1))
                dve.wait_ge(S["out_mm"], at(t, 1, 1))
                dve.tensor_tensor(IN[:, p, :, :], heads(5), DD[:, :, :], ALU.mult).then_inc(S["in"], 1)
                dve.wait_ge(S["db"], at(t, 1, 1))
                dve.scalar_tensor_tensor(out=NL[:, p, :, :], in0=heads(4), scalar=-1.0, in1=BR[:, :, :],
                                         op0=ALU.mult, op1=ALU.mult).then_inc(S["nl"], 1)

            def dn_dve_kb(dve, t):
                dve.wait_ge(S["turned"], at(t, 1, 1 + FREE0))
                dve.tensor_tensor(KB[:, t[1] % 2, :, :], heads(4), over_cols(tile_cols(nbeg, at(t))),
                                  ALU.mult).then_inc(S["kb"], 1)

            def dn_dve_st(dve, t):
                dve.wait_ge(S["kv_mm"], at(t, 1, 1 + USED0))
                dve.wait_ge(S["exl"], at(t, 1, 1))
                dve.wait_ge(S["st"], at(t, 4, 4))
                for h in range(NHD):
                    dve.scalar_tensor_tensor(out=STATE[:, h, :], in0=STATE[:, h, :],
                                             scalar=EXL[:, t[1] % 2, h:h + 1], in1=ps[:, 6, h * P:(h + 1) * P],
                                             op0=ALU.mult, op1=ALU.add).then_inc(S["st"], 1)

            def dn_dve_out(dve, t):
                dve.wait_ge(S["ors"], at(t, 1, 1))
                dve.scalar_tensor_tensor(out=ORS[:, :, :], in0=heads(7), scalar=gdn_col[:, 0:1],
                                         in1=ORS[:, :, :], op0=ALU.mult, op1=ALU.mult).then_inc(S["of"], 1)
                dve.wait_ge(S["of"], at(t, 1, 1 + FREE0))
                dve.tensor_tensor(MIX[:, 4:8, tokens(t)], ORS[:, :, :], PROJ[:, Z0:Z0 + 4, tokens(t)],
                                  ALU.mult).then_inc(S["mixed"], 1)

            def mix_lo_of(dve, k):
                dve.wait_ge(mix_hi, k + 1)
                dve.tensor_tensor(LO[:, k, :], MIX[:, k, :], HI[:, k, :].bitcast(F32), ALU.subtract).then_inc(mix_lo, 1)

            def att_norm(dve, j):
                dve.wait_ge(A["rs"], 1)
                dve.scalar_tensor_tensor(out=MIX[:, j, :], in0=PROJ[:, j, :], scalar=gain_att_col[:, j:j + 1],
                                         in1=ARS, op0=ALU.mult, op1=ALU.mult).then_inc(A["mix"], 1)

            def dn_dve(dve, t, before, after, norm=False):
                p = t[1] % 2
                nxt = (t[0], t[1] + 1)
                def masked(lv, c):
                    dve.wait_ge(C[c]["p_mm"], at(t, DOUBLINGS, lv))
                    dve.tensor_tensor(PP[:, 2 * c:2 * c + 2, :], half_heads(2 * c),
                                      over_heads(level_mask[:, lv, :], 2), ALU.mult).then_inc(C[c]["p"], 1)

                masked(1, 0)
                masked(1, 1)
                for lv in range(1, LEVELS):
                    if lv == 2 and after:
                        dn_dve_sub(dve, nxt)
                    if lv == 3 and after:
                        dn_dve_gram(dve, nxt)
                    if lv == 4 and before:
                        dn_dve_st(dve, back(t, 1))
                    if lv == 5 and after:
                        dn_dve_kb(dve, nxt)
                    for c in range(2):
                        if lv < LEVELS - 1:
                            tt = TT[:, p, 2 * c:2 * c + 2, :]
                            dve.wait_ge(C[c]["t_mm"], at(t, DOUBLINGS - 1, lv))
                            if lv > 1:
                                dve.wait_ge(C[c]["t"], at(t, DOUBLINGS - 1, lv - 1))
                            dve.tensor_tensor(tt, half_heads(2 * c + 1), tt, ALU.add).then_inc(C[c]["t"], 1)
                    for c in range(2):
                        ut = UT[:, p, 2 * c:2 * c + 2, :]
                        dve.wait_ge(C[c]["u_mm"], at(t, DOUBLINGS, lv))
                        if lv < LEVELS - 1:
                            dve.tensor_copy(ut, half_heads(2 * c + 1)).then_inc(C[c]["u"], 1)
                            masked(lv + 1, c)
                        else:
                            dve.wait_ge(C[c]["u"], at(t, DOUBLINGS, lv - 1))
                            dve.tensor_tensor(ut, half_heads(2 * c), ut, ALU.add).then_inc(C[c]["u"], 1)
                    if lv in (1, 2, 3, 5) and not after:
                        mix_lo_of(dve, (1, 2, 3, 5).index(lv))
                    if lv in (2, 3, 5, 6) and norm:
                        att_norm(dve, (2, 3, 5, 6).index(lv))
                    if lv == 6 and before:
                        dn_dve_out(dve, back(t, 1))

            def ffn_dve(dve, f, par, adds):
                dve.wait_ge(F["silu"], f + 1)
                dve.wait_ge(unit_used, up_unit(f) + 1)
                half = GG[:, par, :].rearrange("p (b c) -> p b c", c=HALF)
                dve.tensor_tensor(half, bank_pair(1), half, ALU.mult).then_inc(F["h"], 1)
                if adds:
                    for t in range(2):
                        ffn_add(dve, f - 1, t)
                dve.wait_ge(F["hi"], f + 1)
                if not isinstance(f, int) or f >= 2:
                    dve.wait_ge(unit_used, down_unit(f - 2) + 1)
                dve.tensor_tensor(HS[:, par, 1, :], GG[:, par, :], HS[:, par, 0, :].bitcast(F32),
                                  ALU.subtract).then_inc(F["lo"], 1)
                if adds:
                    for t in range(2, NT):
                        ffn_add(dve, f - 1, t)

            def ffn_add(dve, f, t):
                if t < NT - 1:
                    dve.wait_ge(rows_done, (f + 1) * (NT - 1) + (t + 1))
                else:
                    dve.wait_ge(unit_used, down_unit(f) + 1)
                add_rows(dve, t, down_bank(t))

            def out_add(dve, t):
                dve.wait_ge(x_in[t], 32)
                if t < NT - 1:
                    dve.wait_ge(rows_done, t + 1)
                else:
                    dve.wait_ge(unit_used, U_FFN)
                add_rows(dve, t, out_bank(t))

            @block.vector
            def _(dve):
                dve.sem_inc(banks_free, BANKS0)
                dve.sem_inc(A["ao"], AO0)
                for used in ("new_mm", "out_mm", "kv_mm"):
                    dve.sem_inc(S[used], USED0)
                for one in (J["free"], J["normed"], J["split"], *(S[n] for n in ("rows", "turned", "osum", "oln", "of", "mixed"))):
                    dve.sem_inc(one, FREE0)
                dve.wait_ge(ext_in, 16)
                dve.tensor_copy(EXT[0:NHA, 0:4 * P - 1],
                                EXT[0:NHA, 4 * P - 1:4 * P].to_broadcast([NHA, 4 * P - 1])).then_inc(ext_filled, 1)
                dve.wait_ge(gain_mix_in, 16)
                for m in range(NT + 1):
                    if m < NT:
                        norm_scale(dve, "inp", XIN[:, m, :], gain_mix_bc, XN, m)
                    if m:
                        norm_lo(dve, "inp", m - 1, (HT[:, 0, :, :], HT[:, 1, :, :]), 0)
                dve.wait_ge(small_in, 9 * 16)
                dve.wait_ge(consts, 2)
                dve.tensor_copy(ones_r[:, :], ones[:, :]).then_inc(J["ones"], 1)
                dve.tensor_copy(ones_pair_r[:, :], ones_pair[:, :]).then_inc(J["ones"], 1)
                dve.wait_ge(A["gt_turned"], 1)
                dve.tensor_copy(gates[:, :, :], ps[:, 2, 0:NT * 8].rearrange("p (m c) -> p m c", c=8)).then_inc(G["in"], 1)
                dve.wait_ge(G["in"], 1)
                dve.tensor_tensor(gstep[:, :, :], gates[:, :, NHD:2 * NHD],
                                  dtb_row[:, :].unsqueeze(1).to_broadcast([P, NT, NHD]), ALU.add).then_inc(G["dve"], 1)
                dve.wait_ge(G["act"], 3)
                dve.tensor_scalar(beta[:, :, :], beta[:, :, :], 1.0, None, ALU.add).then_inc(G["dve"], 1)
                dve.wait_ge(G["dve"], 2)
                dve.reciprocal(beta[:, :, :], beta[:, :, :]).then_inc(G["dve"], 1)
                dve.wait_ge(G["act"], 5)
                dve.scalar_tensor_tensor(out=gstep[:, :, :], in0=gstep[:, :, :], scalar=0.0, in1=gtmp[:, :, :],
                                         op0=ALU.max, op1=ALU.add).then_inc(G["dve"], 1)
                dve.wait_ge(G["dve"], 4)
                dve.scalar_tensor_tensor(out=gstep[:, :, :], in0=gstep[:, :, :], scalar=-1.0,
                                         in1=alog_row[:, :].unsqueeze(1).to_broadcast([P, NT, NHD]),
                                         op0=ALU.mult, op1=ALU.mult).then_inc(G["dve"], 1)
                dve.tensor_scalar(gq_col[:, :], gq_col[:, :], float(DHA) ** -0.5, None, ALU.mult).then_inc(J["q_gain"], 1)
                dve.wait_ge(J["q_gain"], 1)
                def attention_qk(t, gain):
                    side_split(dve, t, t)
                    side_norm(dve, back(t, 1), back(t, 1), gain[:, 0:1])
                side_split(dve, (None, 0), (None, 0))
                with dve.Fori(0, 2) as i:
                    for off in (1, 2):
                        attention_qk((i, off), gq_col)
                for j in range(K0 + 1, V0):
                    attention_qk((None, j), gk_col)
                side_norm(dve, (None, V0 - 1), (None, V0 - 1), gk_col[:, 0:1])
                for j in range(V0, V0 + 4):
                    side_back(dve, j)
                    if j == V0:
                        dve.wait_ge(G["cum"], 1)
                        dve.tensor_copy(gcum[:, :, :], ps[:, 3, 0:NT * NHD].rearrange("p (m c) -> p m c", c=NHD)
                                        ).then_inc(G["dve"], 1)
                conv_taps(dve, (None, DQ0))
                for n, (parts, whole) in enumerate(((gparts, gcum), (bparts, beta))):
                    dve.wait_ge(G["dve"], 6 + 2 * n)
                    dve.tensor_copy(parts[:, 0, :, :], whole[:, :, :]).then_inc(G["dve"], 1)
                    dve.wait_ge(G["dve"], 7 + 2 * n)
                    dve.tensor_tensor(parts[:, 1, :, :], whole[:, :, :], parts[:, 0, :, :].bitcast(F32),
                                      ALU.subtract).then_inc(G["dve"], 1)
                dve.wait_ge(G["act"], 6)
                dve.scalar_tensor_tensor(out=nbeg[:, :, :], in0=nbeg[:, :, :], scalar=-1.0, in1=beta[:, :, :],
                                         op0=ALU.mult, op1=ALU.mult).then_inc(G["dve"], 1)
                side_split(dve, (None, DQ0), (None, DQ0 - 4))
                def dn_qk(t, scale, split=True):
                    conv_taps(dve, t)
                    side_norm(dve, back(t, 1), back(t, 5), scale)
                    if split:
                        side_split(dve, t, back(t, 4))
                with dve.Fori(DQ0 // 2, DQ0 // 2 + 2) as i:
                    for off in (1, 2):
                        dn_qk((i, off), float(P) ** -0.5)
                for j in range(DK0 + 1, DV0):
                    dn_qk((None, j), 1.0)
                dn_qk((None, DV0), 1.0, False)
                for j in range(DV0, DV0 + 4):
                    if j > DV0:
                        conv_taps(dve, (None, j))
                        side_back(dve, j - 1)
                side_back(dve, DV0 + 3)
                dve.wait_ge(G["dve"], 11)
                dve.wait_ge(J["normed"], V0 + FREE0)
                dve.wait_ge(unit_used, U_OUT)
                with dve.Fori(0, NPAIR // 2) as i:
                    dve.tensor_copy(KA[:, 0, :], proj_tile(i * 2 + K0)).then_inc(J["q"], 1)
                    dve.tensor_copy(QB[:, 0, :], proj_tile(i * 2 + Q0)).then_inc(J["q"], 1)
                    for u in range(2 * NU + 3):
                        c = i * (2 * NU)
                        if 1 <= u <= 2 * NU:
                            w = u - 1
                            dve.wait_ge(A["prob"], c + (w + 1))
                            if w >= 4:
                                dve.wait_ge(A["scaled"], c + (w - 3))
                            dve.reciprocal(row_inv[:, w % 4:w % 4 + 1], row_sum[:, w % 4:w % 4 + 1]).then_inc(A["inv"], 1)
                        if u < 2 * NU:
                            slot = u // NU
                            qb, s, nt, kb0 = unit_of(u % NU)
                            if u % NU == 0:
                                dve.wait_ge(bias_in[slot], i * 16 + 16)
                                two = slice(2 * slot, 2 * slot + 2)
                                dve.memset(BIAS[CHUNK:P, two, 0:CHUNK], NEG).then_inc(A["masked"], 1)
                                dve.memset(BIAS[0:CHUNK, two, KEYS - CHUNK:KEYS], NEG).then_inc(A["masked"], 1)
                                dve.wait_ge(A["masked"], i * 4 + (2 * slot + 2))
                            wait_apart(dve, A["scores"], c + (u + 1), passed_dve)
                            if u >= 4:
                                wait_apart(dve, A["turned"], c + (u - 3), passed_dve)
                            dve.tensor_tensor_reduce(
                                SX[:, u % 4, 0:nt * P],
                                ps[:, 2 * (u % 2):2 * (u % 2) + 2, :].rearrange("p b c -> p (b c)")[:, 0:nt * P],
                                BIAS[:, 2 * slot + s, (BAND - nt) * P:KEYS], -1.0, 3.0e38, ALU.add, ALU.min,
                                neg_max[:, u % 4:u % 4 + 1]).then_inc(A["biased"], 1)
                        if 2 <= u < 2 * NU + 2:
                            att_pt(dve, i, u - 2)
                        if u >= 4 and u % 2 == 0:
                            w = u - 3
                            qb = unit_of(w % NU)[0]
                            wait_apart(dve, A["pv"], c + (w + 1), passed_dve)
                            dve.tensor_copy(PROJ[:, ds(i * 2 + w // NU, 1), qb * P:(qb + 1) * P]
                                            .rearrange("p a c -> p (a c)"), ps[:, 6 + w // 2 % 2, 0:P]).then_inc(A["ao"], 1)
                dve.wait_ge(A["ao"], NPAIR * NT + AO0)
                dve.memset(STATE[:, :, :], 0.0).then_inc(S["st"], 4)
                dn_dve_sub(dve, (None, 0))
                dn_dve_gram(dve, (None, 0))
                dn_dve_kb(dve, (None, 0))
                dve.wait_ge(S["t_first"], 1)
                dn_dve(dve, (None, 0), False, True)
                dn_dve(dve, (None, 1), True, True, True)
                with dve.Fori(1, NT // 2 - 1) as i:
                    for off in (0, 1):
                        dn_dve(dve, (i, off), True, True)
                dn_dve(dve, (None, NT - 2), True, True)
                dn_dve(dve, (None, NT - 1), True, False)
                dn_dve_st(dve, (None, NT - 1))
                dn_dve_out(dve, (None, NT - 1))
                for k in range(4, KT):
                    mix_lo_of(dve, k)
                for step, t in FFN_NORM_DVE:
                    if step == "add":
                        out_add(dve, t)
                    elif step == "scale":
                        if t == 0:
                            dve.wait_ge(gain_ffn_in, 16)
                        norm_scale(dve, "ffn", X2[:, t, :], gain_ffn_bc[:, :], FXN, t)
                    else:
                        norm_lo(dve, "ffn", t, (HI, LO), 4)
                ffn_dve(dve, 0, 0, False)
                with dve.Fori(0, (NF - 2) // 2) as i:
                    ffn_dve(dve, i * 2 + 1, 1, True)
                    ffn_dve(dve, i * 2 + 2, 0, True)
                ffn_dve(dve, NF - 1, 1, True)
                for t in range(NT):
                    ffn_add(dve, NF - 1, t)

            def project(pe, t):
                pe.wait_ge(split_done, at(t, 1, U_TILE + 1))
                pe.wait_ge(banks_free, at(t, 1, U_TILE + 1))
                columns_unit(pe, slot_of(t), 4 + 2 * slot_of(t), HTP).then_inc(unit_used, 1)

            def side_sum(pe, t, n, which):
                pe.wait_ge(J["split"], at(n, 2, 2 + FREE0))
                ge(pe, J["free"], at(t, 1, FREE0))
                for th in range(2):
                    for part in range(2):
                        mm = pe.matmul(ps[:, th, :], which[:, :], SQS[:, part, th * HALF:(th + 1) * HALF],
                                       start=(part == 0), stop=(part == 1))
                mm.then_inc(J["mm"], 1)

            def side_turn(pe, j, ready, count):
                pe.wait_ge(ready, count)
                pe.wait_ge(J["free"], j + FREE0)
                for m in range(NT):
                    mm = pe.transpose(ps[:, m // 4, (m % 4) * P:(m % 4 + 1) * P], VT[:, m * P:(m + 1) * P], ident[:, :])
                mm.then_inc(J["mm"], 1)

            def att_scores(pe, i, u):
                qb, s, nt, kb0 = unit_of(u % NU)
                if u % NU == 0:
                    pe.wait_ge(J["q"], i * 4 + (2 * (u // NU) + 2))
                if u >= 2:
                    pe.wait_ge(A["biased"], i * (2 * NU) + (u - 1))
                q = QB[s * DHA:(s + 1) * DHA, u // NU, qb * P:(qb + 1) * P]
                for j0 in range(0, nt, 4):
                    j1 = min(nt, j0 + 4)
                    mm = pe.matmul(ps[:, 2 * (u % 2) + j0 // 4, 0:(j1 - j0) * P], q,
                                   KA[s * DHA:(s + 1) * DHA, u // NU, (kb0 + j0) * P:(kb0 + j1) * P],
                                   start=True, stop=True)
                mm.then_inc(A["scores"], 1)

            def att_turn(pe, i, u):
                nt = unit_of(u % NU)[2]
                pe.wait_ge(A["scaled"], i * (2 * NU) + (u + 1))
                if u >= 1:
                    pe.wait_ge(A["pt"], i * (2 * NU) + u)
                for j in range(nt):
                    mm = pe.transpose(ps[:, 4 + j // 4, (j % 4) * P:(j % 4 + 1) * P], SX[:, u % 4, j * P:(j + 1) * P],
                                      ident[:, :])
                mm.then_inc(A["turned"], 1)

            def att_pv(pe, i, u):
                qb, s, nt, kb0 = unit_of(u % NU)
                half = slice(s * DHA, (s + 1) * DHA)
                if u % NU == 0:
                    pe.wait_ge(J["v"], i * 2 + (u // NU + 1))
                if s == 0:
                    pe.wait_ge(A["ao"], i * NU + (u // 2 + 1))
                pe.wait_ge(A["pt"], i * (2 * NU) + (u + 1))
                for j in range(nt):
                    v = VB[:, u // NU, (kb0 + j) * P + s * DHA:(kb0 + j) * P + (s + 1) * DHA]
                    mm = pe.matmul(ps[half, 6 + u // 2 % 2, 0:P], v, PT[:, u % 2, j * P:(j + 1) * P],
                                   start=(j == 0), stop=(j == nt - 1))
                mm.then_inc(A["pv"], 1)

            def dn_pe_rows(pe, t):
                ge(pe, S["kb"], at(t))
                ge(pe, S["kd"], at(t, 4))
                ge(pe, S["t_first"], at(t))
                pe.wait_ge(S["diag"], at(t, 4, 4))
                for bank, diag in ((4, DG), (5, DB)):
                    for part in range(2):
                        mm = pe.matmul(ps[:, bank, :], ones_r[:, :], flat(diag[:, part, :, :]),
                                       start=(part == 0), stop=(part == 1))
                mm.then_inc(S["rows"], 1)

            def dn_pe_gram(pe, t):
                pe.wait_ge(S["ks"], at(t, 1, 1))
                pe.wait_ge(S["sub"], at(t, 1, 1))
                pe.wait_ge(S["br"], at(t, 1, 1))
                for h in range(NHD):
                    for bank, first in ((4, DK0), (5, DQ0)):
                        mm = pe.matmul(ps[:, bank, h * P:(h + 1) * P], KS[:, h, :], PROJ[:, first + h, tokens(t)],
                                       start=True, stop=True)
                mm.then_inc(S["gram"], 1)

            def dn_pe_turn(pe, t):
                pe.wait_ge(S["nl"], at(t, 1, 1))
                for h in range(NHD):
                    mm = pe.transpose(ps[:, 4, h * P:(h + 1) * P], KS[:, h, :], ident[:, :])
                mm.then_inc(S["turned"], 1)

            def dn_pe_t(pe, t):
                pe.wait_ge(S["u_first"], at(t, 1, 1))
                pe.wait_ge(S["in"], at(t, 1, 1))
                for h in range(NHD):
                    mm = pe.transpose(ps[:, 5, h * P:(h + 1) * P], UT[:, t[1] % 2, h, :], ident[:, :])
                mm.then_inc(S["u_turned"], 1)

            def dn_pe_new(pe, t):
                p = t[1] % 2
                pe.wait_ge(S["wt"], at(t, 2, 2))
                pe.wait_ge(S["vb"], at(t, 1, 1))
                pe.wait_ge(S["st"], at(t, 4, 4))
                ge(pe, S["oln"], at(t, 1, FREE0))
                pe.wait_ge(A["ln"], 1)
                for h in range(NHD):
                    o = ps[:, 6, h * P:(h + 1) * P]
                    pe.matmul(o, UT[:, p, h, :], VBD[:, p, h, :], start=True, stop=False)
                    mm = pe.matmul(o, WT[:, h, :], STATE[:, h, :], start=False, stop=True)
                mm.then_inc(S["new_mm"], 1)

            def dn_pe_out(pe, t):
                p = t[1] % 2
                pe.wait_ge(S["new"], at(t, 1, 1))
                pe.wait_ge(S["qd"], at(t, 1, 1))
                ge(pe, S["of"], at(t, 1, FREE0))
                for h in range(NHD):
                    o = ps[:, 7, h * P:(h + 1) * P]
                    pe.matmul(o, STATE[:, h, :], QD[:, p, h, :], start=True, stop=False)
                    mm = pe.matmul(o, VNEW[:, h, :], IN[:, p, h, :], start=False, stop=True)
                mm.then_inc(S["out_mm"], 1)

            def dn_pe_kv(pe, t):
                pe.wait_ge(S["kd"], at(t, 4, 4))
                for h in range(NHD):
                    mm = pe.matmul(ps[:, 6, h * P:(h + 1) * P], KD[:, t[1] % 2, h, :], VNEW[:, h, :],
                                   start=True, stop=True)
                mm.then_inc(S["kv_mm"], 1)

            def dn_pe_osum(pe, t):
                pe.wait_ge(S["osq"], at(t, 1, 1))
                pe.wait_ge(S["st"], at(t, 4, 8))
                pe.matmul(ps[:, 6, :], ones_r[:, :].bitcast(F32), flat(OSQ[:, :, :]), start=True, stop=True).then_inc(S["osum"], 1)

            def att_sum(pe, j):
                pe.wait_ge(A["sq"], j + 1)
                for th in range(2):
                    mm = pe.matmul(ps[:, 6 + th, :], ones_r[:, :].bitcast(F32), ASQ[:, j % 2, th * HALF:(th + 1) * HALF],
                                   start=(j == 0), stop=(j == 3))
                mm.then_inc(A["sums"], 1)

            def dn_pe(pe, t, before, after):
                p = t[1] % 2
                prev, nxt = (t[0], t[1] - 1), (t[0], t[1] + 1)
                def l_t(lv, c):
                    if lv == 1:
                        pe.wait_ge(S["t_first"], at(t, 1, 1))
                        ge(pe, C[c]["u"], at(t, DOUBLINGS))
                    else:
                        pe.wait_ge(C[c]["t"], at(t, DOUBLINGS - 1, lv - 1))
                    for h in range(2):
                        mm = pe.matmul(ps[:, 2 * c, h * P:(h + 1) * P], NL[:, p, 2 * c + h, :],
                                       TT[:, p, 2 * c + h, :], start=True, stop=True)
                    mm.then_inc(C[c]["p_mm"], 1)

                l_t(1, 0)
                l_t(1, 1)
                for lv in range(1, LEVELS):
                    if lv == 2 and before:
                        dn_pe_new(pe, prev)
                    if lv == 5 and after:
                        dn_pe_turn(pe, nxt)
                    if lv == 1 and after:
                        dn_pe_rows(pe, nxt)
                    if lv == 2 and after:
                        dn_pe_gram(pe, nxt)
                    if lv == 3 and before:
                        dn_pe_out(pe, prev)
                    if lv == 4 and before:
                        dn_pe_kv(pe, prev)
                    if lv == 5 and before:
                        dn_pe_osum(pe, prev)
                    if lv == 6 and after:
                        dn_pe_t(pe, nxt)
                    if 3 <= lv and not before:
                        att_sum(pe, lv - 3)
                    for c in range(2):
                        pe.wait_ge(C[c]["p"], at(t, DOUBLINGS, lv))
                        if lv == 1:
                            ge(pe, S["wt"], at(t, 2))
                        else:
                            pe.wait_ge(C[c]["u"], at(t, DOUBLINGS, lv - 1))
                        for h in range(2):
                            if lv < LEVELS - 1:
                                bank, left, right = 2 * c + 1, UT[:, p, 2 * c + h, :], PP[:, 2 * c + h, :]
                            else:
                                bank, left, right = 2 * c, PP[:, 2 * c + h, :], UT[:, p, 2 * c + h, :]
                            mm = pe.matmul(ps[:, bank, h * P:(h + 1) * P], left, right, start=True, stop=True)
                        mm.then_inc(C[c]["t_mm" if lv < LEVELS - 1 else "u_mm"], 1)
                    if lv < LEVELS - 1:
                        for c in range(2):
                            pe.wait_ge(C[c]["t"], at(t, DOUBLINGS - 1, lv))
                            for h in range(2):
                                mm = pe.transpose(ps[:, 2 * c + 1, h * P:(h + 1) * P], TT[:, p, 2 * c + h, :],
                                                  ident[:, :])
                            mm.then_inc(C[c]["u_mm"], 1)
                            l_t(lv + 1, c)
                pe.wait_ge(S["kb"], at(t, 1, 1))
                for c in range(2):
                    pe.wait_ge(C[c]["u"], at(t, DOUBLINGS, DOUBLINGS))
                    for h in range(2):
                        mm = pe.matmul(ps[:, 2 * c + 1, h * P:(h + 1) * P], KB[:, p, 2 * c + h, :],
                                       UT[:, p, 2 * c + h, :], start=True, stop=True)
                    mm.then_inc(S["wt_mm"], 1)

            def ffn_pe(pe, f, par, slot):
                pe.wait_ge(F["silu"], f)
                pe.wait_ge(rows_added, f * NT - 2)
                pe.wait_ge(split_done, gate_unit(f) + 1)
                columns_unit(pe, slot, 0, (HI, LO)).then_inc(unit_used, 1)
                pe.wait_ge(F["h"], f)
                pe.wait_ge(split_done, up_unit(f) + 1)
                columns_unit(pe, 1 - slot, 2, (HI, LO)).then_inc(unit_used, 1)
                down_pe(pe, f - 1, 1 - par, slot)

            def down_pe(pe, f, par, slot):
                pe.wait_ge(F["hi"], f + 1)
                pe.wait_ge(F["lo"], f + 1)
                pe.wait_ge(split_done, down_unit(f) + 1)
                for t in range(NT):
                    if t < 2:
                        pe.wait_ge(rows_added, f * NT + (NT - 1 + t))
                    elif t == 2:
                        pe.wait_ge(F["silu"], f + 1 if isinstance(f, int) and f == NF - 1 else f + 2)
                    else:
                        pe.wait_ge(rows_added, f * NT + (NT + t - 2))
                    row_products(pe, down_bank(t), lambda part: HS[:, par, part, t * P:(t + 1) * P],
                                 SPLIT[:, slot, :, :]).then_inc(rows_done if t < NT - 1 else unit_used, 1)

            def out_pe(pe, k, t):
                pe.wait_ge(mix_lo, k + 1)
                pe.wait_ge(split_done, U_OUT + k + 1)
                unit = SPLIT[:, (U_OUT + k) % 2, :, :] if k < 2 else WO[:, k - 2, :, :]
                mm = row_products(pe, out_bank(t), lambda part: (HI, LO)[part][:, k, t * P:(t + 1) * P], unit,
                                  first=(k == 0), last=(k == KT - 1))
                if t == NT - 1:
                    mm.then_inc(unit_used, 1)
                elif k == KT - 1:
                    mm.then_inc(rows_done, 1)

            @block.tensor
            def _(pe):
                pe.wait_ge(consts, 1)
                for m in range(3):
                    norm_turn(pe, "inp", XN, m, 0)
                for quarter in range(4):
                    span = (quarter * 2 * P, (quarter + 1) * 2 * P)
                    for slot in range(2):
                        pe.wait_ge(nrm["inp"]["lo"], 2 * quarter + 2)
                        pe.wait_ge(split_done, slot + 1)
                        mm = columns_unit(pe, slot, 4 + 2 * slot, HTP, *span)
                        if quarter == 3:
                            mm.then_inc(unit_used, 1)
                        m = 3 + 2 * quarter + slot
                        if m < NT:
                            norm_turn(pe, "inp", XN, m, 0)
                pe.wait_ge(banks_free, U_GATES + 1 + BANKS0)
                for m in range(NT):
                    mm = pe.transpose(ps[:, 2, m * 8:(m + 1) * 8], GT[0:8, m * P:(m + 1) * P], ident[0:8, 0:8])
                mm.then_inc(A["gt_turned"], 1)
                pe.wait_ge(consts, 2)
                pe.wait_ge(J["ones"], 2)
                with pe.Fori(0, 4) as i:
                    for off in (1, 2):
                        project(pe, (i, off))
                        side_sum(pe, (i, off - 1), (i, off - 1), ones_pair_r)
                pe.wait_ge(G["dve"], 5)
                pe.matmul(ps[:, 3, 0:NT * NHD], tri[:, :], gstep[:, :, :].rearrange("p m h -> p (m h)"),
                          start=True, stop=True).then_inc(G["cum"], 1)
                for j in range(V0 + 1, V0 + 5):
                    project(pe, (None, j))
                    side_turn(pe, j - 1, banks_free, U_TILE + j + BANKS0)
                with pe.Fori(DQ0 // 2, DQ0 // 2 + 4) as i:
                    for off in (1, 2):
                        project(pe, (i, off))
                        side_sum(pe, (i, off - 1), (i, off - 5), ones_r)
                for j in range(DV0 + 1, DV0 + 5):
                    project(pe, (None, j))
                    side_turn(pe, j - 1, proj_final, j - DQ0)
                for j in range(Z0 + 1, NPROJ):
                    project(pe, (None, j))
                pe.wait_ge(J["free"], Z0 + FREE0)
                pe.wait_ge(G["dve"], 6)
                pe.wait_ge(J["normed"], 8 + FREE0)
                pe.wait_ge(banks_free, U_OUT + BANKS0)
                with pe.Fori(0, NPAIR // 2) as i:
                    att_scores(pe, i, 0)
                    att_scores(pe, i, 1)
                    for u in range(2 * NU):
                        if u + 2 < 2 * NU:
                            att_scores(pe, i, u + 2)
                        att_turn(pe, i, u)
                        if u >= 1:
                            att_pv(pe, i, u - 1)
                    att_pv(pe, i, 2 * NU - 1)
                    pe.wait_ge(A["biased"], i * (2 * NU) + 2 * NU)
                pe.wait_ge(A["pt"], NPAIR * NU)
                dn_pe_rows(pe, (None, 0))
                pe.wait_ge(A["ao"], NPAIR * NT + AO0)
                dn_pe_gram(pe, (None, 0))
                dn_pe_turn(pe, (None, 0))
                dn_pe_t(pe, (None, 0))
                dn_pe(pe, (None, 0), False, True)
                with pe.Fori(0, NT // 2 - 1) as i:
                    for off in (1, 2):
                        dn_pe(pe, (i, off), True, True)
                dn_pe(pe, (None, NT - 1), True, False)
                last = (None, NT - 1)
                dn_pe_new(pe, last)
                pe.wait_ge(S["wt"], 2 * NT)
                pe.wait_ge(S["kd"], NHD * NT)
                pe.wait_ge(S["t_first"], NT)
                for k in range(4):
                    for t in range(3):
                        out_pe(pe, k, t)
                    if k == 0:
                        dn_pe_out(pe, last)
                        dn_pe_kv(pe, last)
                    if k == 1:
                        dn_pe_osum(pe, last)
                pe.wait_ge(S["oln"], NT + FREE0)
                pe.wait_ge(S["of"], NT + FREE0)
                for k in range(4):
                    out_pe(pe, k, 3)
                for k in range(4, KT):
                    for t in range(4):
                        out_pe(pe, k, t)
                for t in range(4, NT):
                    pe.wait_ge(rows_added, t - 3 if t < 6 else t - 1)
                    for k in range(KT):
                        out_pe(pe, k, t)
                    for m in FFN_NORM_PE[t]:
                        if m == 0:
                            pe.wait_ge(rows_added, 4)
                        norm_turn(pe, "ffn", FXN, m, 4)
                pe.wait_ge(rows_added, NT)
                pe.wait_ge(nrm["ffn"]["lo"], 4)
                pe.wait_ge(split_done, U_FFN + 1)
                columns_unit(pe, U_FFN % 2, 0, (HI, LO), 0, HALF)
                norm_turn(pe, "ffn", FXN, NT - 1, 4)
                pe.wait_ge(split_done, U_FFN + 2)
                columns_unit(pe, 1 - U_FFN % 2, 2, (HI, LO), 0, HALF)
                pe.wait_ge(nrm["ffn"]["lo"], NT)
                columns_unit(pe, U_FFN % 2, 0, (HI, LO), HALF, T).then_inc(unit_used, 1)
                columns_unit(pe, 1 - U_FFN % 2, 2, (HI, LO), HALF, T).then_inc(unit_used, 1)
                with pe.Fori(0, (NF - 2) // 2) as i:
                    ffn_pe(pe, i * 2 + 1, 1, 1)
                    ffn_pe(pe, i * 2 + 2, 0, 0)
                ffn_pe(pe, NF - 1, 1, 1)
                down_pe(pe, NF - 1, 1, 0)


def _units(w_in, w_out, w_gate, w_up, w_down):
    def columns(w, j):
        c = w[:, j * P:(j + 1) * P]
        if c.shape[1] < P:
            c = np.concatenate([c, np.zeros((D, P - c.shape[1]), w.dtype)], axis=1)
        return c.reshape(KT, P, P).transpose(1, 0, 2).reshape(P, D)

    def rows(w, j):
        return w[j * P:(j + 1) * P, :]

    order = [columns(w_in, j) for j in [NPROJ, *range(NPROJ)]] + [rows(w_out, j) for j in range(KT)]
    for f in range(NF):
        order += [columns(w_gate, f), columns(w_up, f)]
        if f:
            order.append(rows(w_down, f - 1))
    order.append(rows(w_down, NF - 1))
    return np.ascontiguousarray(np.stack(order))


def kernel(x, norm_mix_g, w_in, attn_q_norm_g, attn_k_norm_g, rel_bias, attn_out_norm_g, conv_w, a_log, dt_bias,
           dn_out_norm_g, w_out, norm_ffn_g, w_gate, w_up, w_down):
    import concourse.bacc as bacc
    from concourse.bass_utils import run_bass_kernel_spmd

    arrays = {
        "x": np.ascontiguousarray(x[0]),
        "units": _units(np.asarray(w_in[0]), np.asarray(w_out[0]), np.asarray(w_gate[0]), np.asarray(w_up[0]),
                        np.asarray(w_down[0])),
        "gain_mix": np.ascontiguousarray(norm_mix_g[0]),
        "gain_q": np.ascontiguousarray(attn_q_norm_g[0].reshape(DHA, 1)),
        "gain_k": np.ascontiguousarray(attn_k_norm_g[0].reshape(DHA, 1)),
        "bias_rev": np.ascontiguousarray(rel_bias[0][::-1].T),
        "gain_att": np.ascontiguousarray(attn_out_norm_g[0].reshape(4, P).T),
        "conv_w": np.ascontiguousarray(np.asarray(conv_w[0]).reshape(CONV, 12, P).transpose(2, 1, 0)),
        "a_log": np.ascontiguousarray(a_log[0]),
        "dt_bias": np.ascontiguousarray(dt_bias[0]),
        "gain_dn": np.ascontiguousarray(dn_out_norm_g[0].reshape(P, 1)),
        "gain_ffn": np.ascontiguousarray(norm_ffn_g[0]),
    }
    nc = bacc.Bacc("TRN2", target_bir_lowering=False, num_devices=1)
    args = {n: nc.dram_tensor(n, a.shape, F32, kind="ExternalInput").ap() for n, a in arrays.items()}
    bias_ext = nc.dram_tensor("bias_ext", (NHA, 6 * P), F32, kind="Internal").ap()
    bias_rows = nc.dram_tensor("bias_rows", (NPAIR, 2, P, KEYS), F32, kind="Internal").ap()
    out = nc.dram_tensor("out", (T, D), F32, kind="ExternalOutput").ap()
    hymba_block(nc, bias_ext=bias_ext, bias_rows=bias_rows, out=out, **args)
    r = run_bass_kernel_spmd(nc, [arrays], core_ids=[0])
    return r.results[0]["out"].reshape(1, T, D)
```
